# Optimizing a Trainium2 kernel written in Bass

```python
import math
import jax, jax.numpy as jnp
from jax import lax
import numpy as np

D_MODEL = 4096
BATCH = 1
SEQ = 256
DEPTH = 1

EPS = 1e-6
BIG = 1e30
SSM_HEADS = 32
SSM_HEAD_DIM = 64
SSM_INNER = SSM_HEADS * SSM_HEAD_DIM
SSM_GROUPS = 8
SSM_STATE = 128
SSM_CONV = 4
SSM_CHUNK = 128
SSM_XBC = SSM_INNER + 2 * SSM_GROUPS * SSM_STATE
NSA_HEADS = 16
NSA_KV_GROUPS = 2
NSA_HEAD_DIM = 128
NSA_INNER = NSA_HEADS * NSA_HEAD_DIM
KV_W = NSA_KV_GROUPS * NSA_HEAD_DIM
CMP_STRIDE = 16
CMP_LEN = 2 * CMP_STRIDE
CMP_HIDDEN = 256
SEL_LEN = 64
SEL_TOP = 16
WINDOW = 512
Q_BLOCK = 128
ROPE_THETA = 500000.0
ROPE_DIM = NSA_HEAD_DIM // 4
IN_SPLITS = (SSM_INNER,
             SSM_XBC,
             SSM_HEADS,
             NSA_INNER,
             KV_W, KV_W,
             KV_W, KV_W,
             KV_W, KV_W,
             NSA_HEADS * 3,
             NSA_INNER,
             D_MODEL, D_MODEL)
D_IN = int(sum(IN_SPLITS))
IN_OFFSETS = tuple(int(v) for v in np.cumsum(IN_SPLITS)[:-1])

kernel_name = "hybrid_ssd_nsa_gated_block"

def rmsnorm(x, w):
    xf = x.astype(jnp.float32)
    y = xf * lax.rsqrt(jnp.mean(xf * xf, axis=-1, keepdims=True) + EPS)
    return (y * w.astype(jnp.float32)).astype(x.dtype)

def masked_softmax(s, mask):
    s = jnp.where(mask, s.astype(jnp.float32), -BIG)
    m = jnp.max(s, axis=-1, keepdims=True)
    e = jnp.where(mask, jnp.exp(s - m), 0.0)
    return e / jnp.maximum(jnp.sum(e, axis=-1, keepdims=True), 1e-30)

def partial_rope(t, cos, sin):
    half = ROPE_DIM // 2
    cos = cos[None, :, None, :].astype(t.dtype)
    sin = sin[None, :, None, :].astype(t.dtype)
    x1, x2 = t[..., :half], t[..., half:ROPE_DIM]
    return jnp.concatenate([x1 * cos - x2 * sin, x2 * cos + x1 * sin, t[..., ROPE_DIM:]], axis=-1)

def causal_depthwise_conv(x, w, b):
    y = lax.conv_general_dilated(x, w[:, None, :].astype(x.dtype), window_strides=(1,),
                                 padding=[(SSM_CONV - 1, 0)],
                                 dimension_numbers=("NWC", "WIO", "NWC"),
                                 feature_group_count=x.shape[-1])
    return y + b

def ssd_chunked(xs, dt, a, bm, cm):
    B_, S_, H, P = xs.shape
    G, N = bm.shape[2], bm.shape[3]
    R = H // G
    L = SSM_CHUNK
    nc = S_ // L
    xdt = (xs * dt[..., None]).reshape(B_, nc, L, G, R, P)
    adt = (dt * a).reshape(B_, nc, L, G, R).transpose(0, 3, 4, 1, 2)
    bc = bm.reshape(B_, nc, L, G, N)
    cc = cm.reshape(B_, nc, L, G, N)
    a_cs = jnp.cumsum(adt, axis=-1)
    causal = jnp.tril(jnp.ones((L, L), dtype=bool))
    seg = a_cs[..., :, None] - a_cs[..., None, :]
    decay_in = jnp.exp(jnp.where(causal, seg, -jnp.inf))
    cb = jnp.einsum("bclgn,bcsgn->bcgls", cc, bc)
    y_diag = jnp.einsum("bcgls,bgrcls,bcsgrp->bclgrp", cb, decay_in, xdt)
    decay_to_end = jnp.exp(a_cs[..., -1:] - a_cs)
    states = jnp.einsum("bcsgn,bgrcs,bcsgrp->bcgrpn", bc, decay_to_end, xdt)
    chunk_decay = jnp.exp(a_cs[..., -1])

    def step(h, inp):
        st, dc = inp
        return h * dc[..., None, None] + st, h

    _, prev = lax.scan(step, jnp.zeros_like(states[:, 0]),
                       (jnp.moveaxis(states, 1, 0), jnp.moveaxis(chunk_decay, 3, 0)))
    prev = jnp.moveaxis(prev, 0, 1)
    y_off = jnp.einsum("bclgn,bcgrpn,bgrcl->bclgrp", cc, prev, jnp.exp(a_cs))
    return (y_diag + y_off).reshape(B_, S_, H, P)

def compress_blocks(kv, pe, w1, w2):
    B_, S_, G, D = kv.shape
    halves = kv.reshape(B_, S_ // CMP_STRIDE, CMP_STRIDE, G, D)
    blocks = jnp.concatenate([halves[:, :-1], halves[:, 1:]], axis=2)
    blocks = blocks + pe[None, None, :, None, :]
    flat = blocks.transpose(0, 1, 3, 2, 4).reshape(B_, -1, G, CMP_LEN * D)
    return jax.nn.gelu(flat @ w1) @ w2

def nsa_attention(q_raw, q_rot, k_c, v_c, k_s, v_s, k_w, v_w, gates):
    B_, S_ = q_raw.shape[:2]
    G, R, D = NSA_KV_GROUPS, NSA_HEADS // NSA_KV_GROUPS, NSA_HEAD_DIM
    nc = k_c.shape[1]
    ns = S_ // SEL_LEN
    k_top = min(SEL_TOP, ns)
    scale = D ** -0.5
    cmp_end = jnp.arange(nc) * CMP_STRIDE + CMP_LEN - 1
    ic = jnp.arange(nc)[:, None]
    jc = jnp.arange(ns)[None, :]
    overlap = ((ic * CMP_STRIDE < (jc + 1) * SEL_LEN) &
               (ic * CMP_STRIDE + CMP_LEN > jc * SEL_LEN)).astype(jnp.float32)
    ks_blocks = k_s.reshape(B_, ns, SEL_LEN, G, D).transpose(0, 3, 1, 2, 4)
    vs_blocks = v_s.reshape(B_, ns, SEL_LEN, G, D).transpose(0, 3, 1, 2, 4)
    pad = ((0, 0), (WINDOW, 0), (0, 0), (0, 0))
    k_w_pad = jnp.pad(k_w, pad)
    v_w_pad = jnp.pad(v_w, pad)
    bi = jnp.arange(B_)[:, None, None, None]
    gi = jnp.arange(G)[None, :, None, None]
    sel_offsets = jnp.arange(SEL_LEN)
    win_offsets = jnp.arange(Q_BLOCK + WINDOW)
    jb = jnp.arange(ns)

    def block(qb):
        t0 = qb * Q_BLOCK
        pos_q = t0 + jnp.arange(Q_BLOCK)
        qc = lax.dynamic_slice_in_dim(q_raw, t0, Q_BLOCK, 1).reshape(B_, Q_BLOCK, G, R, D)
        qr = lax.dynamic_slice_in_dim(q_rot, t0, Q_BLOCK, 1).reshape(B_, Q_BLOCK, G, R, D)
        gt = lax.dynamic_slice_in_dim(gates, t0, Q_BLOCK, 1).reshape(B_, Q_BLOCK, G, R, 3)
        s = jnp.einsum("bqgrd,bkgd->bgrqk", qc, k_c).astype(jnp.float32) * scale
        p_c = masked_softmax(s, cmp_end[None, :] <= pos_q[:, None])
        o_c = jnp.einsum("bgrqk,bkgd->bqgrd", p_c.astype(v_c.dtype), v_c)
        imp = jnp.einsum("bgrqk,kj->bgqj", p_c, overlap)
        cur = pos_q // SEL_LEN
        eligible = jb[None, :] * SEL_LEN <= pos_q[:, None]
        forced = (jb[None, :] == 0) | (jb[None, :] == cur[:, None]) | (jb[None, :] == cur[:, None] - 1)
        score = jnp.where(forced, BIG, jnp.where(eligible, imp, -BIG))
        _, idx = lax.top_k(score, k_top)
        kg = ks_blocks[bi, gi, idx].reshape(B_, G, Q_BLOCK, k_top * SEL_LEN, D)
        vg = vs_blocks[bi, gi, idx].reshape(B_, G, Q_BLOCK, k_top * SEL_LEN, D)
        kpos = (idx[..., None] * SEL_LEN + sel_offsets).reshape(B_, G, Q_BLOCK, k_top * SEL_LEN)
        s = jnp.einsum("bqgrd,bgqjd->bgrqj", qr, kg).astype(jnp.float32) * scale
        p_s = masked_softmax(s, (kpos <= pos_q[None, None, :, None])[:, :, None])
        o_s = jnp.einsum("bgrqj,bgqjd->bqgrd", p_s.astype(vg.dtype), vg)
        kw = lax.dynamic_slice_in_dim(k_w_pad, t0, Q_BLOCK + WINDOW, 1)
        vw = lax.dynamic_slice_in_dim(v_w_pad, t0, Q_BLOCK + WINDOW, 1)
        kpos_w = t0 - WINDOW + win_offsets
        dlt = pos_q[:, None] - kpos_w[None, :]
        mask_w = (dlt >= 0) & (dlt < WINDOW) & (kpos_w[None, :] >= 0)
        s = jnp.einsum("bqgrd,bkgd->bgrqk", qr, kw).astype(jnp.float32) * scale
        p_w = masked_softmax(s, mask_w)
        o_w = jnp.einsum("bgrqk,bkgd->bqgrd", p_w.astype(vw.dtype), vw)
        return gt[..., 0:1] * o_c + gt[..., 1:2] * o_s + gt[..., 2:3] * o_w

    o = lax.map(block, jnp.arange(S_ // Q_BLOCK))
    return jnp.moveaxis(o, 0, 1).reshape(B_, S_, NSA_HEADS * D)

def hybrid_layer(x, c, cos, sin, w_ada, b_ada, norm_w, w_in, conv_w, conv_b, dt_bias, a_log,
                 d_skip, ssm_norm_w, cmp_pe_k, cmp_pe_v, cmp_k_w1, cmp_k_w2, cmp_v_w1, cmp_v_w2,
                 w_proj_a, w_proj_b, w_out):
    B_, S_, _ = x.shape
    mod = jax.nn.silu(c) @ w_ada + b_ada
    shift, scl, gate = jnp.split(mod, 3, axis=-1)
    h = rmsnorm(x, norm_w) * (1.0 + scl[:, None, :]) + shift[:, None, :]
    proj = h @ w_in
    (z_a, xbc, dt_raw, q, kc, vc, ks, vs, kw, vw, nsa_g, z_b, g_a, g_b) = jnp.split(proj, IN_OFFSETS, axis=-1)

    xbc = jax.nn.silu(causal_depthwise_conv(xbc, conv_w, conv_b))
    xs, bm, cm = jnp.split(xbc, [SSM_INNER, SSM_INNER + SSM_GROUPS * SSM_STATE], axis=-1)
    xs = xs.reshape(B_, S_, SSM_HEADS, SSM_HEAD_DIM)
    bm = bm.reshape(B_, S_, SSM_GROUPS, SSM_STATE)
    cm = cm.reshape(B_, S_, SSM_GROUPS, SSM_STATE)
    dt = jax.nn.softplus(dt_raw.astype(jnp.float32) + dt_bias.astype(jnp.float32))
    a = -jnp.exp(a_log.astype(jnp.float32))
    y = ssd_chunked(xs, dt, a, bm, cm) + d_skip[:, None] * xs
    y_a = rmsnorm(y.reshape(B_, S_, SSM_INNER) * jax.nn.silu(z_a), ssm_norm_w)
    u_a = y_a @ w_proj_a

    hd = NSA_HEAD_DIM
    q = q.reshape(B_, S_, NSA_HEADS, hd)
    q_rot = partial_rope(q, cos, sin)
    kv_shape = (B_, S_, NSA_KV_GROUPS, hd)
    k_c = compress_blocks(kc.reshape(kv_shape), cmp_pe_k, cmp_k_w1, cmp_k_w2)
    v_c = compress_blocks(vc.reshape(kv_shape), cmp_pe_v, cmp_v_w1, cmp_v_w2)
    k_s = partial_rope(ks.reshape(kv_shape), cos, sin)
    k_w = partial_rope(kw.reshape(kv_shape), cos, sin)
    gates = jax.nn.sigmoid(nsa_g).reshape(B_, S_, NSA_HEADS, 3)
    o = nsa_attention(q, q_rot, k_c, v_c, k_s, vs.reshape(kv_shape), k_w, vw.reshape(kv_shape), gates)
    u_b = (o * jax.nn.silu(z_b)) @ w_proj_b

    merged = jax.nn.sigmoid(g_a) * u_a + jax.nn.sigmoid(g_b) * u_b
    out = merged @ w_out
    return x + gate[:, None, :] * out

def setup_inputs(seed: int = 0) -> dict:
    key = jax.random.key(seed)
    k = jax.random.split(key, 24)
    f32 = jnp.float32

    def nrm(kk, shape, s):
        return jax.random.normal(kk, shape, f32) * s

    dt0 = jnp.exp(jax.random.uniform(k[8], (DEPTH, SSM_HEADS), f32, math.log(1e-3), math.log(1e-1)))
    flat_cmp = CMP_LEN * NSA_HEAD_DIM
    return {
        "x": nrm(k[0], (BATCH, SEQ, D_MODEL), 1.0),
        "c": nrm(k[1], (BATCH, D_MODEL), 1.0),
        "w_ada": nrm(k[2], (DEPTH, D_MODEL, 3 * D_MODEL), 0.5 * D_MODEL ** -0.5),
        "b_ada": nrm(k[3], (DEPTH, 3 * D_MODEL), 0.01),
        "norm_w": 1.0 + nrm(k[4], (DEPTH, D_MODEL), 0.02),
        "w_in": nrm(k[5], (DEPTH, D_MODEL, D_IN), D_MODEL ** -0.5),
        "conv_w": nrm(k[6], (DEPTH, SSM_CONV, SSM_XBC), SSM_CONV ** -0.5),
        "conv_b": nrm(k[7], (DEPTH, SSM_XBC), 0.01),
        "dt_bias": dt0 + jnp.log(-jnp.expm1(-dt0)),
        "a_log": jnp.log(jax.random.uniform(k[9], (DEPTH, SSM_HEADS), f32, 1.0, 16.0)),
        "d_skip": 1.0 + nrm(k[10], (DEPTH, SSM_HEADS), 0.02),
        "ssm_norm_w": 1.0 + nrm(k[11], (DEPTH, SSM_INNER), 0.02),
        "cmp_pe_k": nrm(k[12], (DEPTH, CMP_LEN, NSA_HEAD_DIM), 0.02),
        "cmp_pe_v": nrm(k[13], (DEPTH, CMP_LEN, NSA_HEAD_DIM), 0.02),
        "cmp_k_w1": nrm(k[14], (DEPTH, flat_cmp, CMP_HIDDEN), flat_cmp ** -0.5),
        "cmp_k_w2": nrm(k[15], (DEPTH, CMP_HIDDEN, NSA_HEAD_DIM), CMP_HIDDEN ** -0.5),
        "cmp_v_w1": nrm(k[16], (DEPTH, flat_cmp, CMP_HIDDEN), flat_cmp ** -0.5),
        "cmp_v_w2": nrm(k[17], (DEPTH, CMP_HIDDEN, NSA_HEAD_DIM), CMP_HIDDEN ** -0.5),
        "w_proj_a": nrm(k[18], (DEPTH, SSM_INNER, D_MODEL), SSM_INNER ** -0.5),
        "w_proj_b": nrm(k[19], (DEPTH, NSA_INNER, D_MODEL), NSA_INNER ** -0.5),
        "w_out": nrm(k[20], (DEPTH, D_MODEL, D_MODEL), D_MODEL ** -0.5),
        "final_norm_w": 1.0 + nrm(k[21], (D_MODEL,), 0.02),
    }

def reference(x, c, w_ada, b_ada, norm_w, w_in, conv_w, conv_b, dt_bias, a_log, d_skip,
              ssm_norm_w, cmp_pe_k, cmp_pe_v, cmp_k_w1, cmp_k_w2, cmp_v_w1, cmp_v_w2,
              w_proj_a, w_proj_b, w_out, final_norm_w):
    S_ = x.shape[1]
    pos = jnp.arange(S_, dtype=jnp.float32)
    inv_freq = ROPE_THETA ** (-jnp.arange(0, ROPE_DIM, 2, dtype=jnp.float32) / ROPE_DIM)
    ang = pos[:, None] * inv_freq[None, :]
    cos, sin = jnp.cos(ang), jnp.sin(ang)
    for layer in range(DEPTH):
        x = hybrid_layer(x, c, cos, sin, w_ada[layer], b_ada[layer], norm_w[layer], w_in[layer],
                         conv_w[layer], conv_b[layer], dt_bias[layer], a_log[layer], d_skip[layer],
                         ssm_norm_w[layer], cmp_pe_k[layer], cmp_pe_v[layer], cmp_k_w1[layer],
                         cmp_k_w2[layer], cmp_v_w1[layer], cmp_v_w2[layer], w_proj_a[layer],
                         w_proj_b[layer], w_out[layer])
    return rmsnorm(x, final_norm_w)


_drawn_inputs = setup_inputs


def setup_inputs(seed=0):
    import zlib

    import numpy as np

    out = dict(_drawn_inputs(seed))
    spreads = {}
    factors = {'b_ada': 8.0,
     'norm_w': 8.0,
     'conv_b': 64.0,
     'd_skip': 64.0,
     'ssm_norm_w': 64.0,
     'cmp_pe_k': 8.0,
     'cmp_pe_v': 56.793,
     'cmp_k_w1': 6.638,
     'cmp_k_w2': 6.682,
     'final_norm_w': 7.698,
     'a_log': 2.672}
    for name, (base, spread) in spreads.items():
        noise = np.random.default_rng([zlib.crc32(name.encode()), seed]).standard_normal(out[name].shape)
        drawn = base * np.exp(spread * noise) if base else spread * noise
        out[name] = __import__('jax').numpy.asarray(drawn.astype(out[name].dtype))
    for name, factor in factors.items():
        out[name] = (out[name] * factor).astype(out[name].dtype)
    return out
```

```python
from contextlib import ExitStack

import concourse.bass as bass
from concourse import mybir

F32 = mybir.dt.float32
F32R = mybir.dt.float32r
ACT = mybir.ActivationFunctionType
ALU = mybir.AluOpType
AX = mybir.AxisListType

P = 128
D = 4096
S = 256
TT = S // P
KT = D // P
EPS = 1e-6
NEG = -1e30
NEG_CLAMP = -1e29

INNER = 2048
G = 8
R = 4
HP = 64
GW = R * HP
H = 32
NH = 16
DH = 128
NC = S // 16 - 1
ROT = DH // 4
SCALE = DH ** -0.5

C_Z = 0
C_X = C_Z + INNER
C_B = C_X + INNER
C_C = C_B + G * P
C_DT = C_C + G * P
C_Q = C_DT + H
C_KV = C_Q + INNER
C_NG = C_KV + 6 * 256
C_ZB = C_NG + NH * 3
C_GA = C_ZB + INNER
C_GB = C_GA + D
D_IN = C_GB + D
ODD = H + NH * 3

BW = 512
UK = 2
UPB = KT // UK
SLOTS = 4
SLOT = UK * BW

ADA_BLOCKS = 3 * D // BW

K_ID, K_TRI, K_AFT, K_NEG = 0, 128, 256, 384
K_CM = 512
K_COS = K_CM + 32
K_SIN = K_COS + 32
K_ONE = K_SIN + 32
K_N = K_ONE + 1


class Chain:

    def __init__(self, eng, sem):
        self.eng, self.sem, self.total, self.base, self.off = eng, sem, 0, 0, 0

    def enter(self, i=0, per=0):
        self.base, self.off = self.total + i * per, 0

    def leave(self, per, times=1):
        assert self.off == per, (self.off, per)
        self.total += per * times
        self.base, self.off = self.total, 0

    def inc(self, ins):
        self.off += 1
        ins.then_inc(self.sem, 1)

    def wait(self):
        self.eng.wait_ge(self.sem, self.base + self.off)

    def step(self, ins):
        self.inc(ins)
        self.wait()


class Region:

    def __init__(self, after, dmas, iters, units=UPB):
        self.unit0 = after.unit0 + after.units * len(after.dmas) * after.iters if after else 0
        self.dma0 = after.dma0 + after.units // SLOTS * sum(after.dmas) * after.iters if after else 0
        self.dmas, self.iters, self.units = dmas, iters, units

    def unit(self, i, b, u):
        return self.unit0 + i * (self.units * len(self.dmas)) + (self.units * b + u)

    def landed(self, i, b, u):
        per = self.units // SLOTS
        before = per * sum(self.dmas[:b]) + self.dmas[b] * (u // SLOTS + 1)
        return (self.dma0 + before) * 16 + i * (16 * per * sum(self.dmas))


R_ADA = Region(None, [1, 1], ADA_BLOCKS // 2)
R_Z = Region(R_ADA, [1, 1], 2)
R_ODD = Region(R_Z, [2], 1, units=4)
R_G0 = Region(R_ODD, [3], 1)
R_G = Region(R_G0, [3, 3], 3)
R_G7 = Region(R_G, [3], 1)
R_KV = Region(R_G7, [1], 3)
R_W1 = Region(R_KV, [1], 1)
R_QG = Region(R_W1, [4, 1, 1, 4, 1, 1], 4)
R_PR = Region(R_QG, [1], 8)
R_OUT = Region(R_PR, [1, 1], 4)
UNIT_W = R_Z.unit0

B_Z, B_ODD, B_G, B_KV = 0, 4, 5, 13
B_QG = 16
B_PR = B_QG + 24
B_OUT = B_PR + 16


def build(nc, a):
    ctx = ExitStack()
    with ctx:
        def sb(name, shape, dt=F32):
            return ctx.enter_context(nc.sbuf_tensor(name, shape, dt))

        def sem(name):
            return ctx.enter_context(nc.semaphore(name))

        a_hi = sb("a_hi", [P, KT, S], F32R)
        a_lo = sb("a_lo", [P, KT, S], F32R)
        full = sb("full", [P, KT, S])
        raw = sb("raw", [P, SLOTS, SLOT])
        w_hi = sb("w_hi", [P, SLOTS, SLOT], F32R)
        w_lo = sb("w_lo", [P, SLOTS, SLOT], F32R)
        cst = sb("cst", [P, K_N])
        prm = sb("prm", [P, 3, P])
        mod = sb("mod", [P, 96])
        hsc = sb("hsc", [P, KT])
        cT = sb("cT", [P, 3, KT])
        dtb = sb("dtb", [P, 3, H])
        odd = sb("odd", [P, TT, ODD])
        dts = sb("dts", [P, TT, H])
        adt = sb("adt", [P, TT, H])
        tmp = sb("tmp", [P, 3, TT, H])
        dec = sb("dec", [P, 2, H])
        wgt = sb("wgt", [P, TT, NH * 3])
        stat = sb("stat", [P, 40])
        ssa = sb("ssa", [P, TT, G])
        bhl = sb("bhl", [P, 2, 32, 60], F32R)
        ar = sb("ar", [P, 10112])

        def carve(at, *shape):
            n = 1
            for s in shape:
                n *= s
            v = ar[:, at:at + n]
            if len(shape) == 2:
                v = v.rearrange("p (a b) -> p a b", b=shape[1])
            if len(shape) == 3:
                v = v.rearrange("p (a b c) -> p a b c", b=shape[1], c=shape[2])
            return v, at + n

        xin, at = carve(0, TT, D)
        acc, at = carve(at, 2, BW)
        stage, at = carve(at, 3, P)
        cst_in, at = carve(at, P)
        za, at = carve(0, TT, INNER)
        xst, at = carve(at, TT, BW)
        cv, at = carve(at, 4, S)
        th, at = carve(at, 4, S)
        ua = th.rearrange("p a b -> p (a b)").rearrange("p (c r s) -> p c r s", c=2, r=R)
        mm, at = carve(at, 2, R, P)
        xdt, at = carve(at, TT, GW)
        y0, at = carve(at, TT, GW)
        cbm, at = carve(at, 2 * P)
        btok, at = carve(at, P)
        xdd, at = carve(at, GW)
        stt, at = carve(at, GW)
        yof = stt
        kT, at = carve(0, 2, 2, S)
        vv, at = carve(at, 2 * TT, 2, DH)
        kcT, at = carve(at, 2, 16)
        vcT, at = carve(at, 2, DH)
        w2, at = carve(at, 4, DH)
        at_kv = at
        kst, at = carve(at, TT, BW)
        ckT, at = carve(at, 4, S)
        blk, at = carve(at, 32, 30)
        gel, at = carve(at, 4, 60)
        rp, at = carve(at, 6, 64)
        at = at_kv
        qs, at = carve(at, TT, 2 * DH)
        qr, at = carve(at, TT, 2 * DH)
        zt, at = carve(at, TT, 2 * DH)
        qT, at = carve(at, 4 * P)
        p0, at = carve(at, 2, P)
        p1, at = carve(at, 2, S)
        pc, at = carve(at, TT, 16)
        mx, at = carve(at, TT, 3)
        sm, at = carve(at, TT, 3)
        pt0, at = carve(at, 2 * P)
        ptc, at = carve(at, 2 * P)
        pt1, at = carve(at, 4 * P)
        og, at = carve(at, TT, DH)
        rq, at = carve(at, 4, 64)
        gst, at = carve(at, 2 * TT, BW)
        gx, at = carve(0, 2 * TT, BW)
        mg, at = carve(at, TT, BW)
        mb, at = carve(at, TT, BW)
        xr, at = carve(0, 2 * TT, BW)
        gateb, at = carve(4096, D)
        xo = full[:, :, :].rearrange("p k s -> p (k s)").rearrange("p (t n) -> p t n", t=TT)
        ssf = sb("ssf", [P, TT, 8])
        gout = sb("gout", [KT, P])

        M = [ctx.enter_context(nc.psum_tensor(f"main{i}", [P, TT, BW], F32)) for i in range(2)]
        X = [ctx.enter_context(nc.psum_tensor(f"side{i}", [P, BW], F32)) for i in range(4)]

        ident = cst[:, K_ID:K_ID + P]
        tri = cst[:, K_TRI:K_TRI + P]
        after = cst[:, K_AFT:K_AFT + P]
        negm = cst[:, K_NEG:K_NEG + P]
        cmpm = cst[:, K_CM:K_CM + 32].rearrange("p (t k) -> p t k", t=TT)
        cosv = cst[:, K_COS:K_COS + 32].rearrange("p (t k) -> p t k", t=TT)
        sinv = cst[:, K_SIN:K_SIN + 32].rearrange("p (t k) -> p t k", t=TT)
        one = cst[:, K_ONE:K_ONE + 1]
        b_ada, normw = prm[:, 0, 0:96], prm[:, 0, 96:128]

        s_in = sem("inputs_landed")
        s_x = [sem(f"x_landed{t}") for t in range(TT)]
        landed = [sem(f"raw_landed{s}") for s in range(SLOTS)]
        raw_used = sem("raw_used")
        hi_ready = sem("w_hi_ready")
        pe_used = sem("unit_multiplied")
        main_free = sem("main_free")
        v_seq, s_seq = sem("vector_self"), sem("scalar_self")
        s_cT = sem("c_transposed")
        s_cc = sem("c_copied")
        s_silu = sem("c_silu")
        s_col = sem("ada_columns")
        s_colc = sem("ada_columns_copied")
        s_prt = sem("params_transposed")
        s_prm = sem("params_copied")
        s_xn = sem("x_normed")
        s_xms = sem("x_mean_square")
        s_xsq = sem("x_root")
        s_xrs = sem("x_rstd")
        s_xT = sem("x_transposed")
        s_xTc = sem("x_transpose_copied")
        s_mod = sem("mod_ready")
        s_h = sem("h_ready")
        s_ahi = sem("a_hi_ready")
        s_alo = sem("a_lo_ready")
        s_ph = sem("pool_self")
        s_blk0 = sem("blocks_float")
        s_kvf = sem("kv_vector_done")
        s_gb = sem("gate_spread")
        s_gt = sem("gate_transposed")
        s_gc = sem("gate_copied")
        s_gd = sem("gate_in_dram")
        s_du = sem("dt_abs")
        s_de = sem("dt_exp")
        s_adt = sem("adt_ready")
        s_dcp = sem("decay_sums")
        s_dec = sem("decays_ready")
        s_ztanh = sem("z_tanh")
        s_T = sem("xbc_transposed")
        s_conv = sem("conv_done")
        s_cth = sem("conv_tanh")
        s_cs = sem("conv_silu")
        s_ua = sem("segment_operand")
        s_seg = sem("segment_sums")
        s_dm = sem("segment_decays")
        s_A = sem("ssd_tok_major")
        s_bt = sem("b_tok_copied")
        s_m = sem("ssd_operands")
        s_Bq = sem("ssd_diag_done")
        s_st = sem("state_copied")
        s_C = sem("ssd_off_done")
        s_y = sem("y_gated")
        s_D = sem("y_transposed")
        s_Dc = sem("y_stored")
        s_krot = sem("k_rotated")
        s_kt = sem("kv_transposed")
        s_ktc = sem("kv_transpose_copied")
        s_blk = sem("blocks_ready")
        s_bhi = sem("blocks_hi")
        s_hid = sem("hidden_done")
        s_gl1 = sem("gelu_arg")
        s_gl2 = sem("gelu_tanh")
        s_gl3 = sem("gelu_done")
        s_cmp = sem("compressed")
        s_cmpc = sem("compressed_copied")
        s_w2 = sem("w2_landed")
        s_zth = sem("zb_tanh")
        s_zs = sem("zb_silu")
        s_qr = sem("q_rotated")
        s_qa = sem("q_transposed")
        s_qT = sem("q_transpose_copied")
        s_sc = sem("scores_done")
        s_mx = sem("score_max")
        s_ex = sem("exps_done")
        s_pw = sem("probs_weighted")
        s_pt = sem("probs_transposed")
        s_ptc = sem("probs_t_scalar")
        s_ptv = sem("probs_t_vector")
        s_o = sem("o_done")
        s_og = sem("o_gated")
        s_oT = sem("o_transposed")
        s_oTc = sem("o_stored")
        s_gth = sem("merge_tanh")
        s_gsp = [sem("merge_spilled0"), sem("merge_spilled1")]
        s_gfree = [sem("spill_buffer_free0"), sem("spill_buffer_free1")]
        s_rms = sem("y_mean_square")
        s_rsq = sem("y_root")
        s_gl = [sem("merge_loaded0"), sem("merge_loaded1")]
        s_mgd = sem("merged_block")
        s_mT = sem("merged_transposed")
        s_mTc = sem("merged_copied")
        s_xr = [sem("x_again0"), sem("x_again1")]
        s_xo = sem("out_block")
        s_osq = sem("out_squares")
        s_fms = sem("out_mean_square")
        s_fsq = sem("out_root")
        s_fn = sem("final_norm_landed")
        s_fin = sem("final_ready")
        s_out = sem("out_written")

        win = a["w_in"][0].rearrange("(k p) n -> p k n", p=P)
        wada = a["w_ada"][0].rearrange("(k p) n -> p k n", p=P)
        wpa = a["w_proj_a"][0].rearrange("(k p) n -> p k n", p=P)
        wpb = a["w_proj_b"][0].rearrange("(k p) n -> p k n", p=P)
        wout = a["w_out"][0].rearrange("(k p) n -> p k n", p=P)
        w1 = [a["cmp_k_w1"][0].rearrange("(k p) n -> p k n", p=P),
              a["cmp_v_w1"][0].rearrange("(k p) n -> p k n", p=P)]
        xd = a["x"][0].rearrange("(t p) n -> p t n", p=P)
        od = a["out"][0].rearrange("(t p) n -> p t n", p=P)
        gsc = a["gscr"].rearrange("b (t p) n -> p b t n", p=P)

        heads = [win[:, :, c:c + INNER].rearrange("p k (b n) -> p k b n", b=2) for c in (C_Q, C_ZB)]

        def slot(t, u, n=BW, k=UK):
            return t[:, u % SLOTS, 0:k * n].rearrange("p (k n) -> p k n", k=k)

        block = ctx.enter_context(nc.Block())

        @block.sync
        def _(sp):
            def load(reg, i, b, u, parts):
                sp.wait_ge(raw_used, reg.unit(i, b, u) + 1)
                for dst, src in parts:
                    sp.dma_start(dst, src).then_inc(landed[u % SLOTS], 16)

            def load_block(reg, i, b, w, col, k0=0, units=UPB):
                for u in range(units):
                    k = k0 + UK * u
                    load(reg, i, b, u, [(slot(raw, u), w[:, k:k + UK, bass.ds(col, BW)])])

            with sp.Fori(0, ADA_BLOCKS // 2) as i:
                for b in range(2):
                    col = sp.snap(i * (2 * BW) + b * BW)
                    load_block(R_ADA, i, b, wada, col)
            with sp.Fori(0, 2) as i:
                for b in range(2):
                    col = sp.snap(i * (2 * BW) + (C_Z + b * BW))
                    load_block(R_Z, i, b, win, col)
            for u in range(4):
                t = slot(raw, u, ODD, 8)
                k = slice(8 * u, 8 * u + 8)
                load(R_ODD, 0, 0, u, [(t[:, :, 0:H], win[:, k, C_DT:C_DT + H]),
                                      (t[:, :, H:ODD], win[:, k, C_NG:C_NG + ODD - H])])

            def load_group(reg, i, b, g):
                cx, cb, cc = g * GW + C_X, g * P + C_B, g * P + C_C
                if not isinstance(g, int):
                    cx, cb, cc = sp.snap(cx), sp.snap(cb), sp.snap(cc)
                for u in range(UPB):
                    k = slice(UK * u, UK * u + UK)
                    t = slot(raw, u)
                    load(reg, i, b, u, [(t[:, :, 0:GW], win[:, k, bass.ds(cx, GW)]),
                                        (t[:, :, GW:GW + P], win[:, k, bass.ds(cb, P)]),
                                        (t[:, :, GW + P:BW], win[:, k, bass.ds(cc, P)])])

            load_group(R_G0, 0, 0, 0)
            with sp.Fori(0, 3) as i:
                for b in range(2):
                    load_group(R_G, i, b, i * 2 + (1 + b))
            load_group(R_G7, 0, 0, 7)
            for i in range(3):
                load_block(R_KV, i, 0, win, C_KV + i * BW)
            for u in range(UPB):
                k = 4 * (u % 8)
                load(R_W1, 0, 0, u, [(slot(raw, u, 256, 4), w1[u // 8][:, k:k + 4, :])])
            with sp.Fori(0, 4) as i:
                for j2 in range(2):
                    cj = sp.snap(i * (2 * P) + j2 * P)
                    for u in range(UPB):
                        t = slot(raw, u)
                        parts = []
                        for n, c in enumerate((cj, cj)):
                            for k in range(UK):
                                parts.append((t[:, k, 2 * n * P:2 * n * P + 2 * P].rearrange("p (b n) -> p b n", b=2),
                                              heads[n][:, UK * u + k, :, bass.ds(c, P)]))
                        load(R_QG, i, 3 * j2, u, parts)
                    for n, c in enumerate((C_GA, C_GB)):
                        col = sp.snap(i * (2 * BW) + (c + j2 * BW))
                        load_block(R_QG, i, 3 * j2 + 1 + n, win, col)
            with sp.Fori(0, 8) as i:
                col = sp.snap(i * BW)
                load_block(R_PR, i, 0, wpa, col, units=UPB // 2)
                for u in range(UPB // 2):
                    load(R_PR, i, 0, UPB // 2 + u,
                         [(slot(raw, u), wpb[:, UK * u:UK * u + UK, bass.ds(col, BW)])])
            with sp.Fori(0, 4) as i:
                for b in range(2):
                    col = sp.snap(i * (2 * BW) + b * BW)
                    load_block(R_OUT, i, b, wout, col)
            sp.wait_ge(raw_used, R_OUT.unit(3, 1, UPB - 1) + (1 + SLOTS))
            sp.dma_start(raw[:, :, :].rearrange("p a b -> p (a b)"), a["final_norm_w"].partition_broadcast(P))\
              .then_inc(s_fn, 16)
            for q in range(4):
                for t in range(TT):
                    sp.wait_ge(s_fin, q * TT + t + 1)
                    c = slice(q * 1024, q * 1024 + 1024)
                    sp.dma_start(od[:, t, c], xo[:, t, c]).then_inc(s_out, 16)
            sp.wait_ge(s_out, 16 * 8)

        @block.tensor
        def _(pe):
            pe.sem_inc(pe_used, SLOTS)
            pe.sem_inc(s_col, 2)
            pe.sem_inc(s_mT, 1)

            def tr(out, in_, k=P):
                return pe.transpose(out, in_, ident[0:k, 0:k])

            def split_ready(reg, i, b, u):
                pe.wait_ge(raw_used, reg.unit(i, b, u) + (1 + SLOTS))

            def unit(reg, i, b, u, out, k0, last, n=BW, per=UK, first=0):
                split_ready(reg, i, b, u)
                hi, lo = slot(w_hi, u, n, per), slot(w_lo, u, n, per)
                for k in range(per):
                    kt = k0 + k
                    for t in range(TT):
                        tok = slice(t * P, t * P + P)
                        o = out[:, t, 0:n]
                        pe.matmul(o, a_hi[:, kt, tok], hi[:, k, :], start=kt == first, stop=False)
                        pe.matmul(o, a_lo[:, kt, tok], hi[:, k, :], start=False, stop=False)
                        mm_ = pe.matmul(o, a_hi[:, kt, tok], lo[:, k, :], start=False, stop=kt == last)
                mm_.then_inc(pe_used, 1)

            def pair_free(blk_):
                pe.wait_ge(main_free, blk_ + 1)

            def main_block(reg, i, b, blk_, par, hooks=None):
                hooks = hooks or {}
                pair_free(blk_)
                for u in range(UPB):
                    unit(reg, i, b, u, M[par], UK * u, KT - 1)
                    if u in hooks:
                        hooks[u]()

            pe.wait_ge(s_in, 16 * 12)
            tr(X[3][:, 0:KT], cst_in[0:KT, :], KT).then_inc(s_cT, 1)
            tr(X[2][:, 0:P], stage[:, 0, :])
            tr(X[2][:, P:2 * P], stage[:, 1, :])
            tr(X[2][:, 2 * P:2 * P + 112], stage[0:112, 2, :], 112).then_inc(s_prt, 1)
            for t in range(TT):
                pe.wait_ge(s_xn, t + 1)
                for q in range(8):
                    n = 8 * t + q
                    if n < 2:
                        pe.wait_ge(s_prm, 1)
                        pe.wait_ge(s_cc, 1)
                    else:
                        pe.wait_ge(s_xTc, n - 1)
                    for k in range(4):
                        ins = tr(X[2 + n % 2][:, k * P:k * P + P], xin[:, t, (4 * q + k) * P:(4 * q + k + 1) * P])
                    ins.then_inc(s_xT, 1)
            with pe.Fori(0, ADA_BLOCKS // 2) as i:
                for b in range(2):
                    split_ready(R_ADA, i, b, UPB - 1)
                    pe.wait_ge(s_colc, i * 2 + (b + 1))
                    for k in range(4):
                        ins = pe.matmul(X[b][:, k:k + 1], acc[:, b, k * P:k * P + P], one, start=True, stop=True)
                    ins.then_inc(s_col, 1)
            pe.wait_ge(s_mod, 1)
            pe.wait_ge(s_colc, 2 + ADA_BLOCKS)
            tr(X[0][0:KT, 0:P], mod[:, 64:96]).then_inc(s_gt, 1)

            pe.wait_ge(s_alo, 8)
            with pe.Fori(0, 2) as i:
                for b in range(2):
                    main_block(R_Z, i, b, i * 2 + (B_Z + b), b)
            pair_free(B_ODD)
            for u in range(4):
                unit(R_ODD, 0, 0, u, M[0], 8 * u, KT - 1, n=ODD, per=8)

            def decay_sums():
                pe.wait_ge(s_adt, 1)
                pe.matmul(X[3][:, 0:H], tri, adt[:, 1, :], start=True, stop=True)
                pe.matmul(X[3][:, H:2 * H], after, adt[:, 0, :], start=True, stop=True).then_inc(s_dcp, 1)

            def ssd(g, blk_):
                def to_channels():
                    pe.wait_ge(main_free, blk_ + 3)
                    for c in range(4):
                        for t in range(TT):
                            ins = tr(X[c // 2][:, (c % 2) * S + t * P:(c % 2) * S + t * P + P],
                                     xst[:, t, c * P:c * P + P])
                    ins.then_inc(s_T, 1)

                def to_tokens():
                    pe.wait_ge(s_cs, g + 1)
                    for t in range(TT):
                        for c in range(2):
                            tr(X[0][:, t * S + c * P:t * S + c * P + P], cv[:, c, t * P:t * P + P])
                    tr(X[1][:, 0:P], cv[:, 2, 0:P])
                    for t in range(TT):
                        ins = pe.matmul(X[1][:, (1 + t) * P:(2 + t) * P], cv[:, 2, t * P:t * P + P],
                                        cv[:, 3, t * P:t * P + P], start=True, stop=True)
                    ins.then_inc(s_A, 1)
                    pe.wait_ge(s_dec, 2)
                    pe.wait_ge(s_ua, g + 1)
                    pe.wait_ge(s_Dc, g + 1)
                    for c in range(2):
                        for r in range(R):
                            ins = pe.matmul(X[2 + c][:, r * P:r * P + P], ua[:, c, r, :], tri, start=True, stop=True)
                    ins.then_inc(s_seg, 1)

                def diag():
                    pe.wait_ge(s_m, g + 1)
                    for c in range(2):
                        for r in range(R):
                            pe.matmul(X[0][:, c * GW + r * HP:c * GW + r * HP + HP], mm[:, c, r, :],
                                      xdt[:, c, r * HP:r * HP + HP], start=True, stop=True)
                    pe.wait_ge(s_bt, g + 1)
                    pe.matmul(X[1][:, 0:GW], btok, xdd, start=True, stop=True).then_inc(s_Bq, 1)

                def off():
                    pe.wait_ge(s_st, g + 1)
                    pe.matmul(X[1][:, GW:2 * GW], cv[:, 3, P:2 * P], stt, start=True, stop=True).then_inc(s_C, 1)

                def y_channels():
                    pe.wait_ge(s_y, g + 1)
                    for c in range(2):
                        for t in range(TT):
                            ins = tr(X[2][:, c * S + t * P:c * S + t * P + P], y0[:, t, c * P:c * P + P])
                    ins.then_inc(s_D, 1)

                return {2: to_channels, 7: to_tokens, 10: diag, 12: off, 15: y_channels}

            main_block(R_G0, 0, 0, B_G, 1, {6: decay_sums})
            with pe.Fori(0, 3) as i:
                for b in range(2):
                    g = i * 2 + b
                    main_block(R_G, i, b, g + (B_G + 1), b, ssd(g, g + B_G))
            main_block(R_G7, 0, 0, B_G + 7, 0, ssd(6, B_G + 6))
            main_block(R_KV, 0, 0, B_KV, 1, ssd(7, B_G + 7))

            def kv_channels(x):
                def f():
                    pe.wait_ge(main_free, B_KV + x + 3)
                    if x:
                        pe.wait_ge(s_krot, x)
                        pe.wait_ge(s_ktc, x)
                    for c in range(4 if x == 0 else 2):
                        for t in range(TT):
                            ins = tr(X[c // 2][:, (c % 2) * S + t * P:(c % 2) * S + t * P + P],
                                     kst[:, t, c * P:c * P + P])
                    ins.then_inc(s_kt, 1)
                return f

            main_block(R_KV, 1, 0, B_KV + 1, 0, {3: kv_channels(0)})
            main_block(R_KV, 2, 0, B_KV + 2, 1, {6: kv_channels(1)})
            for u in range(UPB):
                w = u // 8
                if u == 0:
                    pair_free(B_KV + 3)
                    pe.wait_ge(s_blk, 2)
                split_ready(R_W1, 0, 0, u)
                hi, lo = slot(w_hi, u, 256, 4), slot(w_lo, u, 256, 4)
                for k in range(4):
                    pos = 4 * (u % 8) + k
                    for half in range(2):
                        o = M[0][:, half, w * 64:w * 64 + 60]
                        cols = slice(half * P, half * P + P)
                        pe.matmul(o, hi[:, k, cols], bhl[:, w, pos, :], start=pos == 0 and w == 0, stop=False,
                                  skip_group_check=True)
                        ins = pe.matmul(o[:, 0:30], lo[:, k, cols], bhl[:, w, pos, 0:30], start=False,
                                        stop=pos == 31, skip_group_check=True)
                ins.then_inc(pe_used, 1)
                if u == 4:
                    kv_channels(2)()
            pe.wait_ge(s_gl3, 1)
            pe.wait_ge(s_w2, 32)
            pe.wait_ge(s_Dc, G + 1)
            for half in range(2):
                pe.matmul(X[2][:, 0:30], w2[:, half, :], gel[:, half, 30:60], start=half == 0, stop=half == 1)
            for g in range(2):
                for half in range(2):
                    ins = pe.matmul(X[3][0:NC, g * DH:g * DH + DH], gel[:, 2 + half, 30 + g * NC:30 + g * NC + NC],
                                    w2[:, 2 + half, :], start=half == 0, stop=half == 1)
            ins.then_inc(s_cmp, 1)
            pe.wait_ge(s_cmpc, 2)
            pe.wait_ge(s_ktc, 3)

            def head(n, j, blk_, a_):
                def q_channels():
                    if a_ == 0:
                        pe.wait_ge(main_free, blk_ + 3)
                        pe.wait_ge(s_qr, j + 1)
                    c = slice(a_ * DH, a_ * DH + DH)
                    for t in range(TT):
                        tr(X[0][:, t * P:t * P + P], qs[:, t, c])
                    for t in range(TT):
                        ins = tr(X[0][:, (2 + t) * P:(3 + t) * P], qr[:, t, c])
                    ins.then_inc(s_qa, 1)

                def scores():
                    pe.wait_ge(s_qT, n + 1)
                    pe.wait_ge(s_oTc, n + 1)
                    for br in range(2):
                        o = X[1][:, br * P:br * P + P]
                        pe.matmul(o, qT[:, 2 * P:3 * P], kT[:, br, a_, 0:P], start=True, stop=False)
                        pe.matmul(o, ident, negm, start=False, stop=True)
                    for t in range(TT):
                        o = X[1][:, 256 + 16 * t:256 + 16 * t + NC]
                        pe.matmul(o, qT[:, t * P:t * P + P], kcT[:, a_, 0:NC], start=True, stop=False)
                        pe.matmul(o, ident, cmpm[:, t, 0:NC], start=False, stop=True)
                    for br in range(2):
                        o = X[2][:, br * S:br * S + S]
                        pe.matmul(o, qT[:, 3 * P:4 * P], kT[:, br, a_, :], start=True, stop=False)
                        ins = pe.matmul(o[:, P:S], ident, negm, start=False, stop=True)
                    ins.then_inc(s_sc, 1)

                def probs_t():
                    pe.wait_ge(s_pw, n + 1)
                    for br in range(2):
                        for t in range(TT):
                            tr(X[0][:, (2 * br + t) * P:(2 * br + t + 1) * P], p1[:, br, t * P:t * P + P])
                    for br in range(2):
                        tr(X[3][:, br * P:br * P + P], p0[:, br, :])
                    for t in range(TT):
                        ins = tr(X[3][0:NC, (2 + t) * P:(3 + t) * P], pc[:, t, 0:NC])
                    ins.then_inc(s_pt, 1)

                def values():
                    pe.wait_ge(s_ptc, n + 1)
                    pe.wait_ge(s_ptv, n + 1)
                    o = X[1][:, 0:P]
                    pe.matmul(o, pt0[:, 0:P], vv[:, 0, a_, :], start=True, stop=False)
                    pe.matmul(o, pt0[:, P:2 * P], vv[:, 2, a_, :], start=False, stop=False)
                    pe.matmul(o, ptc[0:NC, 0:P], vcT[0:NC, a_, :], start=False, stop=True)
                    o = X[1][:, P:2 * P]
                    for q in range(4):
                        pe.matmul(o, pt1[:, q * P:q * P + P], vv[:, q, a_, :], start=q == 0, stop=False)
                    pe.matmul(o, ptc[0:NC, P:2 * P], vcT[0:NC, a_, :], start=False, stop=True).then_inc(s_o, 1)

                def o_channels():
                    pe.wait_ge(s_og, n + 1)
                    for t in range(TT):
                        ins = tr(X[2][:, t * P:t * P + P], og[:, t, :])
                    ins.then_inc(s_oT, 1)

                return q_channels, scores, probs_t, values, o_channels

            with pe.Fori(0, 4) as i:
                for j2 in range(2):
                    n0 = i * 4 + 2 * j2
                    j = i * 2 + j2
                    bq = i * 6 + (B_QG + 3 * j2)
                    par = (B_QG + 3 * j2) % 2
                    main_block(R_QG, i, 3 * j2, bq, par)
                    q0, s0, t0, v0, o0 = head(n0, j, bq, 0)
                    q1, s1, t1, v1, o1 = head(n0 + 1, j, bq, 1)
                    main_block(R_QG, i, 3 * j2 + 1, bq + 1, 1 - par, {3: q0, 6: s0, 11: t0, 14: v0})
                    main_block(R_QG, i, 3 * j2 + 2, bq + 2, par,
                               {1: o0, 2: q1, 5: s1, 10: t1, 13: v1, 15: o1})

            with pe.Fori(0, 8) as i:
                for half in range(2):
                    pair_free(i * 2 + (B_PR + half))
                    for u in range(UPB // 2):
                        k0 = half * KT // 2 + UK * u
                        first, last = half * KT // 2, half * KT // 2 + KT // 2 - 1
                        pe.wait_ge(s_alo, 8 + k0 // 4 + 1)
                        unit(R_PR, i, 0, half * 8 + u, M[half], k0, last, first=first)
                pe.wait_ge(s_mgd, i + 1)
                pe.wait_ge(s_mTc, i + 1)
                for c in range(4):
                    for t in range(TT):
                        ins = tr(X[c // 2][:, (c % 2) * S + t * P:(c % 2) * S + t * P + P], mg[:, t, c * P:c * P + P])
                ins.then_inc(s_mT, 1)
            pe.wait_ge(s_alo, 24)
            with pe.Fori(0, 4) as i:
                for b in range(2):
                    main_block(R_OUT, i, b, i * 2 + (B_OUT + b), b)

        def split_number(reg, i, b, u):
            return reg.unit(i, b, u) - UNIT_W

        def block_done(eng, reg, i, b, u=UPB - 1):
            eng.wait_ge(pe_used, reg.unit(i, b, u) + (1 + SLOTS - UNIT_W))

        @block.scalar
        def _(act):
            seq = Chain(act, s_seq)
            act.sem_inc(s_colc, 2)
            act.sem_inc(s_Dc, 1)
            act.sem_inc(s_osq, 1)
            act.sem_inc(s_oTc, 1)
            act.sem_inc(s_mTc, 1)
            for dst, src in (
                    (cst_in[0:KT, :], a["c"].rearrange("a (t p) -> (a t) p", p=P)),
                    (cst[:, :], a["consts"]),
                    (stage[0:96, 0, :], a["b_ada"].rearrange("a (t p) -> (a t) p", p=P)),
                    (stage[96:128, 0, :], a["norm_w"].rearrange("a (t p) -> (a t) p", p=P)),
                    (stage[:, 1, :], a["conv_w"][0].rearrange("a (t p) -> (a t) p", p=P)),
                    (stage[0:32, 2, :], a["conv_b"].rearrange("a (t p) -> (a t) p", p=P)),
                    (stage[32:48, 2, :], a["ssm_norm_w"].rearrange("a (t p) -> (a t) p", p=P)),
                    (stage[48:80, 2, :], a["cmp_pe_k"][0]),
                    (stage[80:112, 2, :], a["cmp_pe_v"][0]),
                    (dtb[:, 0, :], a["dt_bias"][0].partition_broadcast(P)),
                    (dtb[:, 1, :], a["a_log"][0].partition_broadcast(P)),
                    (dtb[:, 2, :], a["d_skip"][0].partition_broadcast(P))):
                act.dma_start(dst, src).then_inc(s_in, 16)
            for t in range(TT):
                act.dma_start(xin[:, t, :], xd[:, t, :]).then_inc(s_x[t], 16)
            act.wait_ge(s_cT, 1)
            act.activation(cT[:, 0, :], X[3][:, 0:KT], ACT.Copy).then_inc(s_cc, 1)
            seq.step(act.activation(cT[:, 1, :], X[3][:, 0:KT], ACT.Tanh, scale=0.5))
            act.wait_ge(s_prt, 1)
            act.activation(prm[:, 0:2, :].rearrange("p a b -> p (a b)"), X[2][:, 0:2 * P], ACT.Copy)
            act.activation(prm[:, 2, 0:112], X[2][:, 2 * P:2 * P + 112], ACT.Copy).then_inc(s_prm, 1)
            for t in range(TT):
                act.wait_ge(s_x[t], 16)
                act.activation(full[:, 16 * t:16 * t + 16, :].rearrange("p a b -> p (a b)"), xin[:, t, :],
                               ACT.Square, accum_out=stat[:, t:t + 1]).then_inc(s_xms, 1)
            act.wait_ge(s_xrs, 1)
            for t in range(TT):
                act.activation(xin[:, t, :], xin[:, t, :], ACT.Copy, scale=stat[:, 4 + t:5 + t]).then_inc(s_xn, 1)
            for n in range(16):
                t, q = n // 8, n % 8
                act.wait_ge(s_xT, n + 1)
                act.activation(full[:, 4 * q:4 * q + 4, t * P:t * P + P],
                               X[2 + n % 2][:, :].rearrange("p (k s) -> p k s", k=4), ACT.Copy).then_inc(s_xTc, 1)
            with act.Fori(0, ADA_BLOCKS // 2) as i:
                for b in range(2):
                    act.wait_ge(s_col, i * 2 + (b + 3))
                    act.activation(mod[:, bass.ds(i * 8 + 4 * b, 4)], X[b][:, 0:4], ACT.Copy).then_inc(s_colc, 1)
            act.wait_ge(s_gt, 1)
            act.activation(gout[:, :], X[0][0:KT, 0:P], ACT.Copy).then_inc(s_gc, 1)

            for c in range(8):
                act.wait_ge(s_h, c + 1)
                act.activation(a_hi[:, 4 * c:4 * c + 4, :], full[:, 4 * c:4 * c + 4, :], ACT.Copy).then_inc(s_ahi, 1)

            def split(reg, i, b, u, n=SLOT):
                act.wait_ge(landed[u % SLOTS], reg.landed(i, b, u))
                act.wait_ge(pe_used, split_number(reg, i, b, u) + 1)
                act.activation(w_hi[:, u % SLOTS, 0:n], raw[:, u % SLOTS, 0:n], ACT.Copy).then_inc(hi_ready, 1)

            def main_block(reg, i, b, hooks=None):
                hooks = hooks or {}
                for u in range(UPB):
                    split(reg, i, b, u)
                    if u in hooks:
                        hooks[u]()

            with act.Fori(0, 2) as i:
                for b in range(2):
                    main_block(R_Z, i, b)
                    block_done(act, R_Z, i, b)
                    act.activation(za[:, :, bass.ds(i * (2 * BW) + b * BW, BW)], M[b][:, :, :], ACT.Tanh,
                                   scale=0.5).then_inc(s_ztanh, 1)
            for u in range(4):
                split(R_ODD, 0, 0, u, 8 * ODD)

            def dt_exp():
                act.wait_ge(s_du, 1)
                act.activation(tmp[:, 1, :, :], tmp[:, 0, :, :], ACT.Exp)
                act.activation(dtb[:, 1, :], dtb[:, 1, :], ACT.Exp)
                act.activation(wgt[:, :, :], odd[:, :, H:ODD], ACT.Tanh, scale=0.5).then_inc(s_de, 1)

            def decays():
                act.wait_ge(s_dcp, 1)
                act.activation(dec[:, :, :], X[3][:, 0:2 * H].rearrange("p (a h) -> p a h", a=2), ACT.Exp)\
                   .then_inc(s_dec, 2)

            def ssd(g, reg, i, b, par):
                def copy_block():
                    block_done(act, reg, i, b)
                    act.activation(xst[:, :, :], M[par][:, :, :], ACT.Copy).then_inc(main_free, 1)

                def conv_tanh():
                    act.wait_ge(s_conv, g + 1)
                    act.activation(th[:, :, :], cv[:, :, :], ACT.Tanh).then_inc(s_cth, 1)

                def decay_exp():
                    act.wait_ge(s_A, g + 1)
                    act.activation(btok, X[1][:, 0:P], ACT.Copy).then_inc(s_bt, 1)
                    act.wait_ge(s_seg, g + 1)
                    for c in range(2):
                        ins = act.activation(mm[:, c, :, :], X[2 + c][:, :].rearrange("p (r s) -> p r s", r=R), ACT.Exp)
                    ins.then_inc(s_dm, 1)

                def state():
                    act.wait_ge(s_Bq, g + 1)
                    act.activation(stt, X[1][:, 0:GW], ACT.Copy).then_inc(s_st, 1)

                def y_out():
                    act.wait_ge(s_D, g + 1)
                    for t in range(TT):
                        act.activation(th[:, t, :], y0[:, t, :], ACT.Square, accum_out=ssa[:, t, bass.ds(g, 1)])
                    for c in range(2):
                        ins = act.activation(full[:, bass.ds(g * 2 + c, 1), :], X[2][:, c * S:c * S + S].unsqueeze(1),
                                             ACT.Copy, scale=prm[:, 2, bass.ds(g * 2 + (32 + c), 1)])
                    ins.then_inc(s_Dc, 1)

                return {2: copy_block, 5: conv_tanh, 9: decay_exp, 11: state, 15: y_out}

            main_block(R_G0, 0, 0, {3: dt_exp, 8: decays})
            with act.Fori(0, 3) as i:
                for b in range(2):
                    g = i * 2 + b
                    main_block(R_G, i, b, ssd(g, R_G, i, b - 1, 1 - b))
            main_block(R_G7, 0, 0, ssd(6, R_G7, 0, -1, 1))
            main_block(R_KV, 0, 0, ssd(7, R_KV, 0, -1, 0))

            def kv_copy(x, par):
                def f():
                    block_done(act, R_KV, x, 0)
                    if x:
                        act.wait_ge(s_kt, x)
                        act.wait_ge(s_kvf, x)
                    act.activation(kst[:, :, :], M[par][:, :, :], ACT.Copy).then_inc(main_free, 1)
                return f

            def kv_store(x):
                def f():
                    act.wait_ge(s_kt, x + 1)
                    if x == 0:
                        for c in range(2):
                            ins = act.activation(ckT[:, 2 * c:2 * c + 2, :],
                                                 X[c][:, :].rearrange("p (c s) -> p c s", c=2), ACT.Copy)
                    else:
                        ins = act.activation(kT[:, x - 1, :, :], X[0][:, :].rearrange("p (c s) -> p c s", c=2), ACT.Copy)
                    ins.then_inc(s_ktc, 1)
                return f

            def blk_hi(w):
                def f():
                    act.wait_ge(s_blk0, w + 1)
                    act.activation(bhl[:, w, :, 0:30], blk[:, :, :], ACT.Copy).then_inc(s_bhi, 1)
                return f

            main_block(R_KV, 1, 0, {2: kv_copy(0, 1), 5: kv_store(0), 8: blk_hi(0), 11: blk_hi(1)})
            main_block(R_KV, 2, 0, {2: kv_copy(1, 0), 8: kv_store(1)})
            main_block(R_W1, 0, 0, {2: kv_copy(2, 1), 7: kv_store(2)})
            act.wait_ge(s_gl1, 1)
            act.activation(gel[:, :, 0:30], gel[:, :, 0:30], ACT.Tanh, scale=0.7978845608028654).then_inc(s_gl2, 1)
            act.wait_ge(s_cmp, 1)
            act.activation(vcT[0:NC, :, :], X[3][0:NC, 0:2 * DH].rearrange("p (g d) -> p g d", g=2), ACT.Copy)\
               .then_inc(s_cmpc, 1)

            def head(n, a_, i, j2):
                def q_t():
                    act.wait_ge(s_qa, n + 1)
                    act.activation(qT, X[0][:, :], ACT.Copy).then_inc(s_qT, 1)

                def exps():
                    act.wait_ge(s_mx, n + 1)
                    for t in range(TT):
                        act.activation(pc[:, t, 0:NC], X[1][:, 256 + 16 * t:256 + 16 * t + NC], ACT.Exp, scale=SCALE,
                                       bias=mx[:, t, 0:1], accum_out=sm[:, t, 0:1])
                    for br in range(2):
                        act.activation(p0[:, br, :], X[1][:, br * P:br * P + P], ACT.Exp, scale=SCALE,
                                       bias=mx[:, 0, 1 + br:2 + br], accum_out=sm[:, 0, 1 + br:2 + br])
                        ins = act.activation(p1[:, br, :], X[2][:, br * S:br * S + S], ACT.Exp, scale=SCALE,
                                             bias=mx[:, 1, 1 + br:2 + br], accum_out=sm[:, 1, 1 + br:2 + br])
                    ins.then_inc(s_ex, 1)

                def probs_t():
                    act.wait_ge(s_pt, n + 1)
                    act.activation(pt1, X[0][:, :], ACT.Copy).then_inc(s_ptc, 1)

                def o_store():
                    act.wait_ge(s_oT, n + 1)
                    act.activation(full[:, bass.ds(i * 2 + (16 + 8 * a_ + j2), 1), :], X[2][:, 0:S].unsqueeze(1),
                                   ACT.Copy).then_inc(s_oTc, 1)

                return q_t, exps, probs_t, o_store

            with act.Fori(0, 4) as i:
                for j2 in range(2):
                    par = (B_QG + 3 * j2) % 2
                    n0 = i * 4 + 2 * j2

                    def q_copy():
                        block_done(act, R_QG, i, 3 * j2)
                        act.activation(qs[:, :, :], M[par][:, :, 0:2 * DH], ACT.Copy)
                        act.activation(zt[:, :, :], M[par][:, :, 2 * DH:BW], ACT.Tanh, scale=0.5).then_inc(s_zth, 1)

                    def merge_tanh(m, blk_, par_):
                        def f():
                            block_done(act, R_QG, i, blk_)
                            act.wait_ge(s_gfree[m], i * 2 + (1 + j2))
                            act.activation(gst[:, 2 * m:2 * m + 2, :], M[par_][:, :, :], ACT.Tanh, scale=0.5)\
                               .then_inc(main_free, 1)
                        return f

                    main_block(R_QG, i, 3 * j2, {})
                    q0, e0, t0, o0 = head(n0, 0, i, j2)
                    q1, e1, t1, o1 = head(n0 + 1, 1, i, j2)
                    main_block(R_QG, i, 3 * j2 + 1, {1: q_copy, 4: q0, 8: e0, 13: t0})
                    main_block(R_QG, i, 3 * j2 + 2, {1: merge_tanh(0, 3 * j2 + 1, 1 - par), 2: o0, 4: q1,
                                                     7: e1, 12: t1, 15: o1})
                    merge_tanh(1, 3 * j2 + 2, par)()

            def round_again(base):
                for c in range(8):
                    act.activation(a_hi[:, 4 * c:4 * c + 4, :], full[:, 4 * c:4 * c + 4, :], ACT.Copy)\
                       .then_inc(s_ahi, 1)

            act.wait_ge(s_rms, 1)
            act.activation(stat[:, 8:10], stat[:, 8:10], ACT.Sqrt).then_inc(s_rsq, 1)
            act.wait_ge(s_Dc, G + 1)
            act.wait_ge(s_oTc, NH + 1)
            block_done(act, R_QG, 3, 5)
            round_again(8)
            with act.Fori(0, 8) as i:
                main_block(R_PR, i, 0)

                def mg_store():
                    act.wait_ge(s_mT, i + 2)
                    for c in range(2):
                        ins = act.activation(full[:, bass.ds(i * 4 + 2 * c, 2), :],
                                             X[c][:, :].rearrange("p (c s) -> p c s", c=2), ACT.Copy)
                    ins.then_inc(s_mTc, 1)
                mg_store()
            act.wait_ge(s_mTc, 9)
            block_done(act, R_PR, 7, 0)
            round_again(16)
            with act.Fori(0, 4) as i:
                for b in range(2):
                    main_block(R_OUT, i, b)

                    def squares():
                        act.wait_ge(s_xo, i * 2 + (b + 3))
                        act.wait_ge(s_osq, i * 2 + (b + 1))
                        for t in range(TT):
                            ins = act.activation(mb[:, t, :], xo[:, t, bass.ds(i * (2 * BW) + b * BW, BW)], ACT.Square,
                                                 accum_out=ssf[:, t, bass.ds(i * 2 + b, 1)])
                        ins.then_inc(s_osq, 1)
                    squares()
            act.wait_ge(s_fms, 1)
            act.activation(stat[:, 16:18], stat[:, 16:18], ACT.Sqrt).then_inc(s_fsq, 1)

        @block.vector
        def _(v):
            seq = Chain(v, v_seq)
            v.sem_inc(raw_used, SLOTS)
            v.sem_inc(main_free, 2)

            v.wait_ge(s_cc, 1)
            v.wait_ge(s_seq, 1)
            seq.step(v.scalar_tensor_tensor(cT[:, 2, :], cT[:, 1, :], 1.0, cT[:, 0, :], ALU.add, ALU.mult))
            seq.step(v.tensor_scalar(cT[:, 2, :], cT[:, 2, :], 0.5, None, ALU.mult))
            seq.leave(2)
            with v.Fori(0, ADA_BLOCKS // 2) as i:
                seq.enter(i, 2 * UPB)
                for b in range(2):
                    v.wait_ge(s_col, i * 2 + (b + 1))
                    for u in range(UPB):
                        v.wait_ge(landed[u % SLOTS], R_ADA.landed(i, b, u))
                        t = slot(raw, u)
                        for k in range(UK):
                            kt = UK * u + k
                            s = cT[:, 2, kt:kt + 1]
                            if kt == 0:
                                ins = v.tensor_scalar(acc[:, b, :], t[:, k, :], s, None, ALU.mult)
                            else:
                                ins = v.scalar_tensor_tensor(acc[:, b, :], t[:, k, :], s, acc[:, b, :],
                                                             ALU.mult, ALU.add)
                            if k == 0:
                                seq.step(ins)
                        ins.then_inc(raw_used, 1)
                        v.wait_ge(raw_used, R_ADA.unit(i, b, u) + (1 + SLOTS))
                seq.leave(2 * UPB, ADA_BLOCKS // 2)
            v.wait_ge(s_prm, 1)
            v.wait_ge(s_colc, 2 + ADA_BLOCKS)
            v.tensor_tensor(mod[:, :], mod[:, :], b_ada, ALU.add).then_inc(s_mod, 1)
            v.wait_ge(s_mod, 1)
            seq.step(v.scalar_tensor_tensor(hsc[:, :], mod[:, KT:2 * KT], 1.0, normw, ALU.add, ALU.mult))
            v.wait_ge(s_xTc, 16)
            for k in range(KT):
                ins = v.tensor_scalar(full[:, k, :], full[:, k, :], hsc[:, k:k + 1], mod[:, k:k + 1], ALU.mult, ALU.add)
                if k % 4 == 3:
                    ins.then_inc(s_h, 1)

            def low_a(base):
                for c in range(8):
                    v.wait_ge(s_ahi, base + c + 1)
                    v.tensor_tensor(a_lo[:, 4 * c:4 * c + 4, :], full[:, 4 * c:4 * c + 4, :],
                                    a_hi[:, 4 * c:4 * c + 4, :].bitcast(F32), ALU.subtract).then_inc(s_alo, 1)

            low_a(0)

            def split(reg, i, b, u, n=SLOT):
                v.wait_ge(hi_ready, split_number(reg, i, b, u) + 1)
                v.tensor_tensor(w_lo[:, u % SLOTS, 0:n], raw[:, u % SLOTS, 0:n],
                                w_hi[:, u % SLOTS, 0:n].bitcast(F32), ALU.subtract).then_inc(raw_used, 1)

            def main_block(reg, i, b, hooks=None):
                hooks = hooks or {}
                for u in range(UPB):
                    split(reg, i, b, u)
                    if u in hooks:
                        hooks[u]()

            seq.leave(1)
            with v.Fori(0, 2) as i:
                for b in range(2):
                    main_block(R_Z, i, b)
                    v.wait_ge(s_ztanh, i * 2 + (b + 1))
                    cols = bass.ds(i * (2 * BW) + b * BW, BW)
                    for t in range(TT):
                        ins = v.scalar_tensor_tensor(za[:, t, cols], za[:, t, cols], 1.0, M[b][:, t, :],
                                                     ALU.add, ALU.mult)
                    ins.then_inc(main_free, 1)
            for u in range(4):
                split(R_ODD, 0, 0, u, 8 * ODD)

            def dt_abs():
                block_done(v, R_ODD, 0, 0, 3)
                v.tensor_copy(odd[:, :, :], M[0][:, :, 0:ODD]).then_inc(main_free, 1)
                v.wait_ge(main_free, B_ODD + 3)
                seq.step(v.tensor_tensor(odd[:, :, 0:H], odd[:, :, 0:H],
                                         dtb[:, 0, :].unsqueeze(1).to_broadcast([P, TT, H]), ALU.add))
                seq.step(v.tensor_scalar(tmp[:, 0, :, :], odd[:, :, 0:H], -1.0, None, ALU.mult))
                v.tensor_tensor(tmp[:, 0, :, :], tmp[:, 0, :, :], odd[:, :, 0:H], ALU.min).then_inc(s_du, 1)

            def dt_finish():
                v.wait_ge(s_de, 1)
                u_, z, z2 = tmp[:, 1, :, :], tmp[:, 0, :, :], tmp[:, 2, :, :]
                seq.step(v.tensor_scalar(z, u_, 2.0, None, ALU.add))
                seq.step(v.reciprocal(z, z))
                seq.step(v.tensor_tensor(z, z, u_, ALU.mult))
                seq.step(v.tensor_tensor(z2, z, z, ALU.mult))
                seq.step(v.tensor_scalar(dts[:, :, :], z2, 1.0 / 19, None, ALU.mult))
                for n in range(17, 1, -2):
                    seq.step(v.scalar_tensor_tensor(dts[:, :, :], dts[:, :, :], 1.0 / n, z2, ALU.add, ALU.mult))
                seq.step(v.scalar_tensor_tensor(dts[:, :, :], dts[:, :, :], 1.0, z, ALU.add, ALU.mult))
                seq.step(v.tensor_scalar(z2, odd[:, :, 0:H], 0.0, None, ALU.max))
                seq.step(v.scalar_tensor_tensor(dts[:, :, :], dts[:, :, :], 2.0, z2, ALU.mult, ALU.add))
                v.scalar_tensor_tensor(adt[:, :, :], dts[:, :, :], -1.0,
                                       dtb[:, 1, :].unsqueeze(1).to_broadcast([P, TT, H]), ALU.mult, ALU.mult)\
                 .then_inc(s_adt, 1)
                seq.step(v.tensor_scalar(wgt[:, :, :], wgt[:, :, :], 1.0, 0.25, ALU.add, ALU.mult))
                seq.step(v.tensor_scalar(prm[:, 1, :], prm[:, 1, :], 0.5, None, ALU.mult))
                seq.step(v.tensor_scalar(prm[:, 2, 0:32], prm[:, 2, 0:32], 0.5, None, ALU.mult))

            seq.enter()
            main_block(R_G0, 0, 0, {2: dt_abs, 5: dt_finish})
            seq.leave(2 + 5 + 8 + 3 + 3)

            def wide(x, n):
                return x.unsqueeze(2).to_broadcast([P, R, n])

            def ssd(g):
                def conv(cs):
                    def f():
                        v.wait_ge(s_T, g + 1)
                        tiles = {0: g * 2, 1: g * 2 + 1, 2: g + 16, 3: g + 24}
                        for k in range(3, -1, -1):
                            for c in cs:
                                x = X[c // 2][:, (c % 2) * S:(c % 2) * S + S]
                                w = prm[:, 1, bass.ds(tiles[c] + 32 * k, 1)]
                                if k == 3:
                                    ins = v.tensor_scalar(cv[:, c, :], x, w, prm[:, 2, bass.ds(tiles[c], 1)],
                                                          ALU.mult, ALU.add)
                                else:
                                    s = 3 - k
                                    ins = v.scalar_tensor_tensor(cv[:, c, s:S], x[:, 0:S - s], w, cv[:, c, s:S],
                                                                 ALU.mult, ALU.add)
                            if k or cs[0] == 0:
                                seq.step(ins)
                            else:
                                ins.then_inc(s_conv, 1)
                    return f

                def conv_silu():
                    v.wait_ge(s_cth, g + 1)
                    flat = cv[:, :, :].rearrange("p a b -> p (a b)")
                    v.scalar_tensor_tensor(flat, th[:, :, :].rearrange("p a b -> p (a b)"), 1.0, flat,
                                           ALU.add, ALU.mult).then_inc(s_cs, 1)
                    v.wait_ge(s_cs, g + 1)
                    for c in range(2):
                        ins = v.tensor_tensor(ua[:, c, :, :], wide(adt[:, c, bass.ds(g * R, R)], P),
                                              after.unsqueeze(1).to_broadcast([P, R, P]), ALU.mult)
                    ins.then_inc(s_ua, 1)

                def operands():
                    v.wait_ge(s_A, g + 1)
                    for t in range(TT):
                        x = X[0][:, t * S:t * S + S].rearrange("p (r n) -> p r n", r=R)
                        v.tensor_tensor(xdt[:, t, :].rearrange("p (r n) -> p r n", r=R), x,
                                        wide(dts[:, t, bass.ds(g * R, R)], HP), ALU.mult)
                        ins = v.tensor_tensor(y0[:, t, :].rearrange("p (r n) -> p r n", r=R), x,
                                              wide(dtb[:, 2, bass.ds(g * R, R)], HP), ALU.mult)
                    v.wait_ge(s_bt, g + 1)
                    ins = v.tensor_tensor(cbm.rearrange("p (c l) -> p c l", c=2),
                                          X[1][:, P:3 * P].rearrange("p (c l) -> p c l", c=2),
                                          tri.unsqueeze(1).to_broadcast([P, 2, P]), ALU.mult)
                    seq.step(ins)
                    v.tensor_tensor(xdd.rearrange("p (r n) -> p r n", r=R),
                                    xdt[:, 0, :].rearrange("p (r n) -> p r n", r=R),
                                    wide(dec[:, 1, bass.ds(g * R, R)], HP), ALU.mult)
                    v.wait_ge(s_dm, g + 1)
                    for c in range(2):
                        ins = v.tensor_tensor(mm[:, c, :, :], mm[:, c, :, :],
                                              cbm[:, c * P:c * P + P].unsqueeze(1).to_broadcast([P, R, P]), ALU.mult)
                    ins.then_inc(s_m, 1)

                def y_gate():
                    v.wait_ge(s_C, g + 1)
                    yf = y0[:, :, :].rearrange("p a b -> p (a b)")
                    seq.step(v.tensor_tensor(yf, yf, X[0][:, :], ALU.add))
                    seq.step(v.tensor_tensor(yof.rearrange("p (r n) -> p r n", r=R),
                                             X[1][:, GW:2 * GW].rearrange("p (r n) -> p r n", r=R),
                                             wide(dec[:, 0, bass.ds(g * R, R)], HP), ALU.mult))
                    seq.step(v.tensor_tensor(y0[:, 1, :], y0[:, 1, :], yof, ALU.add))
                    v.tensor_tensor(y0[:, :, :], y0[:, :, :], za[:, :, bass.ds(g * GW, GW)], ALU.mult).then_inc(s_y, 1)

                return {3: conv((0, 1)), 4: conv((2, 3)), 6: conv_silu, 9: operands, 14: y_gate}

            PER_SSD = 4 + 3 + 1 + 3
            v.wait_ge(s_dec, 2)
            with v.Fori(0, 3) as i:
                seq.enter(i, 2 * PER_SSD)
                for b in range(2):
                    main_block(R_G, i, b, ssd(i * 2 + b))
                seq.leave(2 * PER_SSD, 3)
            main_block(R_G7, 0, 0, ssd(6))
            main_block(R_KV, 0, 0, ssd(7))
            seq.leave(2 * PER_SSD)

            def rope(x, buf):
                def quad(n):
                    return buf[:, n, :].rearrange("p (t g r) -> p t g r", t=TT, g=2)
                h = ROT // 2
                cb = cosv[:, :, 0:h].unsqueeze(2).to_broadcast([P, TT, 2, h])
                sb_ = sinv[:, :, 0:h].unsqueeze(2).to_broadcast([P, TT, 2, h])
                x1, x2 = x[:, :, :, 0:h], x[:, :, :, h:ROT]
                v.tensor_tensor(quad(0), x1, cb, ALU.mult)
                v.tensor_tensor(quad(1), x2, sb_, ALU.mult)
                v.tensor_tensor(quad(2), x2, cb, ALU.mult)
                seq.step(v.tensor_tensor(quad(3), x1, sb_, ALU.mult))
                v.tensor_tensor(x1, quad(0), quad(1), ALU.subtract)
                return v.tensor_tensor(x2, quad(2), quad(3), ALU.add)

            def kv_rope(x):
                def f():
                    v.wait_ge(main_free, B_KV + x + 3)
                    rope(kst[:, :, 0:2 * DH].rearrange("p t (g d) -> p t g d", g=2), rp).then_inc(s_krot, 1)
                    v.tensor_copy(vv[:, (x - 1) * TT:x * TT, :, :].rearrange("p t g d -> p t (g d)"),
                                  kst[:, :, 2 * DH:BW]).then_inc(s_kvf, 1)
                return f

            def blocks(w):
                def f():
                    v.wait_ge(s_ktc, 1)
                    if w:
                        v.wait_ge(s_blk, w)
                    c = ckT[:, 2 * w:2 * w + 2, :].rearrange("p g (i q) -> p q g i", q=16)
                    for half in range(2):
                        pe_ = prm[:, 2, 48 + 32 * w + 16 * half:64 + 32 * w + 16 * half]
                        for g in range(2):
                            ins = v.tensor_tensor(blk[:, 16 * half:16 * half + 16, g * NC:g * NC + NC],
                                                  c[:, :, g, half:half + NC],
                                                  pe_.unsqueeze(2).to_broadcast([P, 16, NC]), ALU.add)
                    ins.then_inc(s_blk0, 1)
                return f

            def blocks_lo(w):
                def f():
                    v.wait_ge(s_bhi, w + 1)
                    v.tensor_tensor(bhl[:, w, :, 30:60], blk[:, :, :], bhl[:, w, :, 0:30].bitcast(F32),
                                    ALU.subtract).then_inc(s_blk, 1)
                return f

            v.sem_inc(s_kvf, 1)
            main_block(R_KV, 1, 0, {7: blocks(0), 9: blocks_lo(0), 10: blocks(1), 12: blocks_lo(1)})
            main_block(R_KV, 2, 0, {3: kv_rope(1)})
            main_block(R_W1, 0, 0, {3: kv_rope(2)})
            block_done(v, R_W1, 0, 0)
            for w in range(2):
                for half in range(2):
                    ins = v.tensor_copy(gel[:, 2 * w + half, :], M[0][:, half, 64 * w:64 * w + 60])
            seq.step(ins)
            ga, gb_, g30 = gel[:, :, 0:30], gel[:, :, 30:60], rp[:, 0:4, 0:30]
            seq.step(v.tensor_tensor(gb_, ga, gb_, ALU.add))
            seq.step(v.tensor_tensor(g30, gb_, gb_, ALU.mult))
            seq.step(v.tensor_scalar(g30, g30, 0.044715, 1.0, ALU.mult, ALU.add))
            v.tensor_tensor(ga, g30, gb_, ALU.mult).then_inc(s_gl1, 1)
            v.wait_ge(s_gl2, 1)
            seq.step(v.scalar_tensor_tensor(gb_, ga, 1.0, gb_, ALU.add, ALU.mult))
            v.tensor_scalar(gb_, gb_, 0.5, None, ALU.mult).then_inc(s_gl3, 1)
            v.wait_ge(s_cmp, 1)
            v.tensor_copy(kcT[:, :, 0:NC], X[2][:, 0:30].rearrange("p (g k) -> p g k", g=2)).then_inc(s_cmpc, 1)
            seq.leave(7)

            def head(n, i, a_, j2):
                def maxima():
                    v.wait_ge(s_sc, n + 1)
                    v.tensor_reduce(mx[:, 0, 1:3], X[1][:, 0:2 * P].rearrange("p (b k) -> p b k", b=2), AX.X, ALU.max)
                    v.tensor_reduce(mx[:, 1, 1:3], X[2][:, :].rearrange("p (b k) -> p b k", b=2), AX.X, ALU.max)
                    seq.step(v.tensor_reduce(mx[:, :, 0], X[1][:, 256:288].rearrange("p (t k) -> p t k", t=2)[:, :, 0:NC],
                                             AX.X, ALU.max))
                    v.tensor_scalar(mx[:, :, :], mx[:, :, :], NEG_CLAMP, -SCALE, ALU.max, ALU.mult).then_inc(s_mx, 1)

                def weights():
                    v.wait_ge(s_ex, n + 1)
                    seq.step(v.tensor_scalar(sm[:, :, :], sm[:, :, :], 1e-30, None, ALU.max))
                    seq.step(v.reciprocal(sm[:, :, :], sm[:, :, :]))
                    seq.step(v.tensor_tensor(sm[:, :, :], sm[:, :, :],
                                             wgt[:, :, bass.ds(i * 6 + (3 * j2 + 24 * a_), 3)], ALU.mult))
                    v.tensor_tensor(p0[:, :, :], p0[:, :, :], sm[:, 0, 1:3].unsqueeze(2).to_broadcast([P, 2, P]), ALU.mult)
                    v.tensor_tensor(p1[:, :, :], p1[:, :, :], sm[:, 1, 1:3].unsqueeze(2).to_broadcast([P, 2, S]), ALU.mult)
                    v.tensor_tensor(pc[:, :, 0:NC], pc[:, :, 0:NC],
                                    sm[:, :, 0].unsqueeze(2).to_broadcast([P, TT, NC]), ALU.mult).then_inc(s_pw, 1)

                def probs_c():
                    v.wait_ge(s_pt, n + 1)
                    v.tensor_copy(pt0, X[3][:, 0:2 * P])
                    v.tensor_copy(ptc[0:NC, :], X[3][0:NC, 2 * P:4 * P]).then_inc(s_ptv, 1)

                def gate_o():
                    v.wait_ge(s_o, n + 1)
                    v.tensor_tensor(og[:, :, :], X[1][:, 0:2 * P].rearrange("p (t d) -> p t d", t=TT),
                                    zt[:, :, a_ * DH:a_ * DH + DH], ALU.mult).then_inc(s_og, 1)

                return maxima, weights, probs_c, gate_o

            PER_HEAD = 4
            PER_Q = 2
            with v.Fori(0, 4) as i:
                seq.enter(i, 2 * (2 * PER_HEAD + PER_Q))
                for j2 in range(2):
                    par = (B_QG + 3 * j2) % 2
                    j = i * 2 + j2
                    n0 = i * 4 + 2 * j2

                    def q_prepare():
                        v.wait_ge(s_zth, j + 1)
                        for t in range(TT):
                            ins = v.scalar_tensor_tensor(zt[:, t, :], zt[:, t, :], 1.0, M[par][:, t, 2 * DH:BW],
                                                         ALU.add, ALU.mult)
                        ins.then_inc(main_free, 1)
                        seq.step(v.tensor_copy(qr[:, :, :], qs[:, :, :]))
                        rope(qr[:, :, :].rearrange("p t (g d) -> p t g d", g=2), rq).then_inc(s_qr, 1)

                    main_block(R_QG, i, 3 * j2)
                    m0, w0, c0, g0 = head(n0, i, 0, j2)
                    m1, w1_, c1, g1 = head(n0 + 1, i, 1, j2)
                    main_block(R_QG, i, 3 * j2 + 1, {1: q_prepare, 7: m0, 9: w0, 13: c0})
                    main_block(R_QG, i, 3 * j2 + 2, {0: g0, 6: m1, 8: w1_, 12: c1, 15: g1})
                seq.leave(2 * (2 * PER_HEAD + PER_Q), 4)

            v.wait_ge(s_Dc, G + 1)
            seq.step(v.tensor_reduce(stat[:, 8:10], ssa[:, :, :], AX.X, ALU.add))
            v.tensor_scalar(stat[:, 8:10], stat[:, 8:10], 1.0 / (4 * INNER), EPS, ALU.mult, ALU.add).then_inc(s_rms, 1)
            v.wait_ge(s_rsq, 1)
            seq.step(v.reciprocal(stat[:, 10:12], stat[:, 8:10]))
            seq.step(v.tensor_scalar(stat[:, 10:12], stat[:, 10:12], 0.5, None, ALU.mult))
            low_a(8)
            seq.leave(3)
            PER_MG = 1
            with v.Fori(0, 8) as i:
                seq.enter(i, PER_MG)

                def gate_a():
                    v.wait_ge(s_gl[0], i * 16 + 16)
                    v.wait_ge(s_gl[1], i * 16 + 16)
                    for t in range(TT):
                        v.tensor_scalar(gx[:, t, :], gx[:, t, :], 1.0, stat[:, 10 + t:11 + t], ALU.add, ALU.mult)
                    seq.step(v.tensor_scalar(gx[:, TT:2 * TT, :], gx[:, TT:2 * TT, :], 1.0, None, ALU.add))

                def merge_a():
                    block_done(v, R_PR, i, 0, UPB // 2 - 1)
                    v.wait_ge(s_mT, i + 1)
                    v.tensor_tensor(mg[:, :, :], gx[:, 0:TT, :], M[0][:, :, :], ALU.mult).then_inc(main_free, 1)

                main_block(R_PR, i, 0, {2: gate_a, 10: merge_a})
                block_done(v, R_PR, i, 0)
                v.tensor_tensor(mb[:, :, :], gx[:, TT:2 * TT, :], M[1][:, :, :], ALU.mult).then_inc(main_free, 1)
                v.wait_ge(main_free, i * 2 + (B_PR + 4))
                v.tensor_tensor(mg[:, :, :], mb[:, :, :], mg[:, :, :], ALU.add).then_inc(s_mgd, 1)
                seq.leave(PER_MG, 8)
            low_a(16)
            v.sem_inc(s_xo, 2)
            with v.Fori(0, 4) as i:
                for b in range(2):
                    main_block(R_OUT, i, b)
                    block_done(v, R_OUT, i, b)
                    v.wait_ge(s_xr[b], i * 16 + 16)
                    v.wait_ge(s_gb, 32)
                    v.wait_ge(s_xo, i * 2 + (b + 2))
                    cols = bass.ds(i * (2 * BW) + b * BW, BW)
                    v.scalar_tensor_tensor(mg[:, 0, :], M[b][:, 0, :], 0.5, gateb[:, cols], ALU.mult, ALU.mult)
                    v.scalar_tensor_tensor(mg[:, 1, :], M[b][:, 1, :], 0.5, gateb[:, cols], ALU.mult, ALU.mult)\
                     .then_inc(main_free, 1)
                    v.wait_ge(main_free, i * 2 + (B_OUT + b + 3))
                    v.tensor_tensor(xo[:, :, cols], mg[:, :, :], xr[:, TT * b:TT * b + TT, :], ALU.add).then_inc(s_xo, 1)
            v.wait_ge(s_osq, 9)
            seq.enter()
            seq.step(v.tensor_reduce(stat[:, 16:18], ssf[:, :, :], AX.X, ALU.add))
            v.tensor_scalar(stat[:, 16:18], stat[:, 16:18], 1.0 / D, EPS, ALU.mult, ALU.add).then_inc(s_fms, 1)
            v.wait_ge(s_fsq, 1)
            seq.step(v.reciprocal(stat[:, 18:20], stat[:, 16:18]))
            v.wait_ge(s_fn, 16)
            fn = raw[:, :, :].rearrange("p a b -> p (a b)")
            for q in range(4):
                for t in range(TT):
                    c = slice(q * 1024, q * 1024 + 1024)
                    v.scalar_tensor_tensor(xo[:, t, c], xo[:, t, c], stat[:, 18 + t:19 + t], fn[:, c],
                                           ALU.mult, ALU.mult).then_inc(s_fin, 1)

        @block.gpsimd
        def _(pool):
            pool.sem_inc(s_gfree[0], 1)
            pool.sem_inc(s_gfree[1], 1)
            pool.memset(stat[:, 20:22], -0.5).then_inc(s_ph, 1)
            pool.wait_ge(s_xms, 2)
            pool.tensor_scalar(stat[:, 2:4], stat[:, 0:2], 1.0 / D, EPS, ALU.mult, ALU.add).then_inc(s_ph, 1)
            pool.wait_ge(s_ph, 2)
            pool.tensor_tensor(stat[:, 4:6], stat[:, 2:4], stat[:, 20:22], ALU.pow).then_inc(s_xrs, 1)
            pool.wait_ge(s_gc, 1)
            pool.dma_start(a["gated"].rearrange("(t p) -> t p", p=P), gout[:, :]).then_inc(s_gd, 16)
            pool.wait_ge(s_Dc, G + 1)
            for w, name in enumerate(("cmp_k_w2", "cmp_v_w2")):
                pool.dma_start(w2[:, 2 * w:2 * w + 2, :], a[name][0].rearrange("(h p) n -> p h n", p=P))\
                    .then_inc(s_w2, 16)
            with pool.Fori(0, 4) as i:
                for j2 in range(2):
                    col = pool.snap(i * (2 * BW) + j2 * BW)
                    for m in range(2):
                        pool.wait_ge(main_free, i * 6 + (B_QG + 3 * j2 + m + 4))
                        pool.dma_start(gsc[:, m, :, bass.ds(col, BW)], gst[:, 2 * m:2 * m + 2, :]).then_inc(s_gsp[m], 16)
                        pool.wait_ge(s_gsp[m], i * 32 + (16 + 16 * j2))
                        pool.sem_inc(s_gfree[m], 1)
            pool.wait_ge(s_gd, 16)
            pool.wait_ge(s_oTc, NH + 1)
            for h in range(2):
                pool.dma_start(gateb[:, h * D // 2:(h + 1) * D // 2],
                               a["gated"][h * D // 2:(h + 1) * D // 2].partition_broadcast(P)).then_inc(s_gb, 16)
            with pool.Fori(0, 8) as i:
                col = pool.snap(i * BW)
                pool.wait_ge(main_free, i * 2 + (B_PR + 2))
                for m in range(2):
                    pool.dma_start(gx[:, TT * m:TT * m + TT, :], gsc[:, m, :, bass.ds(col, BW)]).then_inc(s_gl[m], 16)
            pool.wait_ge(s_mgd, 8)
            with pool.Fori(0, 4) as i:
                for b in range(2):
                    col = pool.snap(i * (2 * BW) + b * BW)
                    pool.wait_ge(s_xo, i * 2 + (b + 1))
                    pool.dma_start(xr[:, TT * b:TT * b + TT, :], xd[:, :, bass.ds(col, BW)]).then_inc(s_xr[b], 16)


def kernel(x, c, w_ada, b_ada, norm_w, w_in, conv_w, conv_b, dt_bias, a_log, d_skip, ssm_norm_w, cmp_pe_k,
           cmp_pe_v, cmp_k_w1, cmp_k_w2, cmp_v_w1, cmp_v_w2, w_proj_a, w_proj_b, w_out, final_norm_w):
    import numpy as np
    import concourse.bacc as bacc
    from concourse.bass_utils import run_bass_kernel_spmd

    row, col = np.arange(P)[:, None], np.arange(P)[None, :]
    consts = np.zeros((P, K_N), np.float32)
    consts[:, K_ID:K_ID + P] = row == col
    consts[:, K_TRI:K_TRI + P] = row <= col
    consts[:, K_AFT:K_AFT + P] = row > col
    consts[:, K_NEG:K_NEG + P] = np.where(col > row, NEG, 0.0)
    pos = np.arange(S)
    cmp_end = np.arange(16) * 16 + 31
    mask = np.where(cmp_end[None, :] <= pos[:, None], 0.0, NEG)
    inv = np.float32(500000.0) ** (-np.arange(0, ROT, 2, dtype=np.float32) / np.float32(ROT))
    ang = pos.astype(np.float32)[:, None] * inv[None, :]
    for t in range(TT):
        tok = slice(t * P, t * P + P)
        consts[:, K_CM + 16 * t:K_CM + 16 * t + 16] = mask[tok]
        consts[:, K_COS + 16 * t:K_COS + 16 * t + 16] = np.cos(ang[tok])
        consts[:, K_SIN + 16 * t:K_SIN + 16 * t + 16] = np.sin(ang[tok])
    consts[:, K_ONE] = 1.0

    given = dict(x=x, c=c, w_ada=w_ada, b_ada=b_ada, norm_w=norm_w, w_in=w_in, conv_w=conv_w, conv_b=conv_b,
                 dt_bias=dt_bias, a_log=a_log, d_skip=d_skip, ssm_norm_w=ssm_norm_w, cmp_pe_k=cmp_pe_k,
                 cmp_pe_v=cmp_pe_v, cmp_k_w1=cmp_k_w1, cmp_k_w2=cmp_k_w2, cmp_v_w1=cmp_v_w1, cmp_v_w2=cmp_v_w2,
                 w_proj_a=w_proj_a, w_proj_b=w_proj_b, w_out=w_out, final_norm_w=final_norm_w, consts=consts)
    nc = bacc.Bacc("TRN2", target_bir_lowering=False, num_devices=1)
    arrays, aps = {}, {}
    for name, value in given.items():
        value = np.ascontiguousarray(value)
        arrays["in_" + name] = value
        aps[name] = nc.dram_tensor("in_" + name, value.shape, F32, kind="ExternalInput").ap()
    aps["out"] = nc.dram_tensor("out", (1, S, D), F32, kind="ExternalOutput").ap()
    aps["gscr"] = nc.dram_tensor("merge_gates", (2, S, D), F32, kind="Internal").ap()
    aps["gated"] = nc.dram_tensor("gate_row", (D,), F32, kind="Internal").ap()
    build(nc, aps)
    r = run_bass_kernel_spmd(nc, [arrays], core_ids=[0])
    return r.results[0]["out"]
```

```python
from contextlib import ExitStack

import concourse.bass as bass
from concourse import mybir

F32 = mybir.dt.float32
F32R = mybir.dt.float32r
ACT = mybir.ActivationFunctionType
ALU = mybir.AluOpType
AX = mybir.AxisListType

P = 128
D = 4096
S = 256
TT = S // P
KT = D // P
EPS = 1e-6
NEG = -1e30
NEG_CLAMP = -1e29

INNER = 2048
G = 8
R = 4
HP = 64
GW = R * HP
H = 32
NH = 16
DH = 128
NC = S // 16 - 1
ROT = DH // 4
SCALE = DH ** -0.5

C_Z = 0
C_X = C_Z + INNER
C_B = C_X + INNER
C_C = C_B + G * P
C_DT = C_C + G * P
C_Q = C_DT + H
C_KV = C_Q + INNER
C_NG = C_KV + 6 * 256
C_ZB = C_NG + NH * 3
C_GA = C_ZB + INNER
C_GB = C_GA + D
D_IN = C_GB + D
ODD = H + NH * 3

BW = 512
UK = 2
UPB = KT // UK
SLOTS = 4
SLOT = UK * BW

ADA_FRONT = 2 * D // BW

K_ID, K_TRI, K_AFT, K_NEG = 0, 128, 256, 384
K_CM = 512
K_COS = K_CM + 32
K_SIN = K_COS + 32
K_ONE = K_SIN + 32
K_N = K_ONE + 1


class Chain:

    def __init__(self, eng, sem):
        self.eng, self.sem, self.total, self.base, self.off = eng, sem, 0, 0, 0

    def enter(self, i=0, per=0):
        self.base, self.off = self.total + i * per, 0

    def leave(self, per, times=1):
        assert self.off == per, (self.off, per)
        self.total += per * times
        self.base, self.off = self.total, 0

    def inc(self, ins):
        self.off += 1
        ins.then_inc(self.sem, 1)

    def flat(self):
        self.total = self.base + self.off
        self.base, self.off = self.total, 0

    def wait(self):
        self.eng.wait_ge(self.sem, self.base + self.off)

    def step(self, ins):
        self.inc(ins)
        self.wait()


def both(x, y):
    return {u: list(x.get(u, ())) + list(y.get(u, ())) for u in {*x, *y}}




def by_block(steps, n):
    return [{u - UPB * b: fs for u, fs in steps.items() if u // UPB == b} for b in range(n)]


class Region:

    def __init__(self, after, kinds, iters=1, dmas=1):
        n_w, n_m = kinds.count("w"), kinds.count("m")
        dmas = dmas if isinstance(dmas, list) else [dmas] * n_w
        assert len(kinds) % SLOTS == 0 and n_w % SLOTS == 0 and len(dmas) == n_w
        self.w0 = after.w_end if after else 0
        self.m0 = after.m_end if after else 0
        self.slot0 = after.slot_end if after else [0] * SLOTS
        self.kinds, self.n_w, self.n_m = kinds, n_w, n_m
        self.at_w = [r for r, k in enumerate(kinds) if k == "w"]
        self.at_m = [r for r, k in enumerate(kinds) if k == "m"]
        self.count, self.per, w = [], [0] * SLOTS, 0
        for r, k in enumerate(kinds):
            self.per[r % SLOTS] += dmas[w] if k == "w" else 1
            w += k == "w"
            self.count.append(self.per[r % SLOTS])
        self.w_end, self.m_end = self.w0 + n_w * iters, self.m0 + n_m * iters
        self.slot_end = [x + y * iters for x, y in zip(self.slot0, self.per)]

    def w(self, i, k):
        return i * self.n_w + (self.w0 + k)

    def m(self, i, k):
        return i * self.n_m + (self.m0 + k)

    def landed(self, i, r):
        s = r % SLOTS
        return i * (16 * self.per[s]) + 16 * (self.slot0[s] + self.count[r])


MIX = "wwwm"
Q_DMAS = [4] * UPB
R_ADA = Region(None, "m" * 2 * UPB, ADA_FRONT // 2)
R_ODD = Region(R_ADA, "wwww", dmas=2)
R_KV0 = Region(R_ODD, "w" * UPB)
R_Z0 = Region(R_KV0, "w" * UPB)
R_ZW = Region(R_Z0, "w" * 4 * UPB)
R_G01 = Region(R_ZW, "w" * 2 * UPB, dmas=3)
R_G = Region(R_G01, "w" * 2 * UPB, 3, dmas=3)
R_KQ = Region(R_G, MIX * UPB, dmas=[1] * 2 * UPB + Q_DMAS)
R_QG = Region(R_KQ, MIX * 2 * UPB, 3, dmas=([1] * 2 * UPB + Q_DMAS) * 2)
R_Q6 = Region(R_QG, MIX * UPB, dmas=[1] * 2 * UPB + Q_DMAS)
R_Q7 = Region(R_Q6, "w" * 2 * UPB)
R_PR0 = Region(R_Q7, "w" * UPB)
R_PR = Region(R_PR0, "w" * UPB, 6)
R_PR7 = Region(R_PR, "w" * UPB)
R_OUT0 = Region(R_PR7, "w" * UPB)
R_OUT = Region(R_OUT0, "w" * 2 * UPB, 3)
R_OUT7 = Region(R_OUT, "w" * UPB)

B_ODD, B_KV0, B_Z, B_G, B_KV = 0, 1, 2, 6, 14
B_QG = 16
B_PR = B_QG + 24
B_OUT = B_PR + 16


def build(nc, a):
    ctx = ExitStack()
    with ctx:
        def sb(name, shape, dt=F32):
            return ctx.enter_context(nc.sbuf_tensor(name, shape, dt))

        def sem(name):
            return ctx.enter_context(nc.semaphore(name))

        a_hi = sb("a_hi", [P, KT, S], F32R)
        a_lo = sb("a_lo", [P, KT, S], F32R)
        full = sb("full", [P, KT, S])
        raw = sb("raw", [P, SLOTS, SLOT])
        w_hi = sb("w_hi", [P, SLOTS, SLOT], F32R)
        w_lo = sb("w_lo", [P, SLOTS, SLOT], F32R)
        cst = sb("cst", [P, K_N])
        prm = sb("prm", [P, 3, P])
        mod = sb("mod", [P, 96])
        hsc = sb("hsc", [P, KT])
        cT = sb("cT", [P, 3, KT])
        dtb = sb("dtb", [P, 3, H])
        dt_work = sb("dt_work", [P, TT * (ODD + 6 * H + NH * 3)])
        stat = sb("stat", [P, 40])
        kcT = sb("kcT", [P, 2, 16])
        vcT = sb("vcT", [P, 2, DH])
        gacc = sb("gacc", [P, BW])
        ssa = sb("ssa", [P, TT, G])
        bhl = sb("bhl", [P, 2, 32, 60], F32R)
        ar = sb("ar", [P, 9216])

        def carve(at, *shape, of=None):
            n = 1
            for s in shape:
                n *= s
            v = (ar if of is None else of)[:, at:at + n]
            if len(shape) == 2:
                v = v.rearrange("p (a b) -> p a b", b=shape[1])
            if len(shape) == 3:
                v = v.rearrange("p (a b c) -> p a b c", b=shape[1], c=shape[2])
            return v, at + n

        odd, at = carve(0, TT, ODD, of=dt_work)
        dts, at = carve(at, TT, H, of=dt_work)
        adt, at = carve(at, TT, H, of=dt_work)
        tmp, at = carve(at, 3, TT, H, of=dt_work)
        dec, at = carve(at, 2, H, of=dt_work)
        wgt, at = carve(at, TT, NH * 3, of=dt_work)

        xin, at = carve(0, TT, D)
        acc1, at = carve(at, BW)
        stage, at = carve(at, 3, P)
        cst_in, at = carve(at, P)
        za, at = carve(0, TT, INNER)
        xst, at = carve(at, TT, BW)
        cv, at = carve(at, 4, S)
        th, at = carve(at, 4, S)
        ua = th.rearrange("p a b -> p (a b)").rearrange("p (c r s) -> p c r s", c=2, r=R)
        mm = xst.rearrange("p a b -> p (a b)").rearrange("p (c r s) -> p c r s", c=2, r=R)
        xdt, at = carve(at, TT, GW)
        y0, at = carve(at, TT, GW)
        cbm, at = carve(at, 2 * P)
        btok, at = carve(at, P)
        xdd, at = carve(at, GW)
        stt, at = carve(at, GW)
        yof = stt
        acc = [(gacc[:, :], dt_work[:, 0:BW]), (acc1, ar[:, TT * D + BW:TT * D + 2 * BW])]
        cst0, at = carve(TT * INNER, TT, BW)
        ckT, at = carve(at, 4, S)
        blk, at = carve(at, 32, 30)
        gel, at = carve(at, 4, 60)
        gsq, at = carve(at, 4, 30)
        w2, at = carve(at, 4, DH)
        kT, at = carve(0, 2, 2, S)
        vv, at = carve(at, 2 * TT, 2, DH)
        at_kv = at
        kst, at = carve(at, TT, BW)
        rp, at = carve(at, 4, 64)
        at = at_kv
        qs, at = carve(at, TT, 2 * DH)
        qr, at = carve(at, TT, 2 * DH)
        zt, at = carve(at, TT, 2 * DH)
        qT, at = carve(at, 4 * P)
        p0, at = carve(at, 2, P)
        p1, at = carve(at, 2, S)
        pc, at = carve(at, TT, 16)
        mx, at = carve(at, TT, 3)
        sm, at = carve(at, TT, 3)
        pt0, at = carve(at, 2 * P)
        ptc, at = carve(at, 2 * P)
        pt1, at = carve(at, 4 * P)
        og, at = carve(at, TT, DH)
        rq, at = carve(at, 4, 64)
        gst, at = carve(at, 2 * TT, BW)
        gx, at = carve(0, 2 * TT, BW)
        mg, at = carve(at, TT, BW)
        mb, at = carve(at, TT, BW)
        xr, at = carve(0, 2 * TT, BW)
        gateb, at = carve(4096, D)
        xo = full[:, :, :].rearrange("p k s -> p (k s)").rearrange("p (t n) -> p t n", t=TT)
        ssf = sb("ssf", [P, TT, 8])
        gout = sb("gout", [KT, P])

        M = [ctx.enter_context(nc.psum_tensor(f"main{i}", [P, TT, BW], F32)) for i in range(2)]
        X = [ctx.enter_context(nc.psum_tensor(f"side{i}", [P, BW], F32)) for i in range(4)]

        ident = cst[:, K_ID:K_ID + P]
        tri = cst[:, K_TRI:K_TRI + P]
        after = cst[:, K_AFT:K_AFT + P]
        negm = cst[:, K_NEG:K_NEG + P]
        cmpm = cst[:, K_CM:K_CM + 32].rearrange("p (t k) -> p t k", t=TT)
        cosv = cst[:, K_COS:K_COS + 32].rearrange("p (t k) -> p t k", t=TT)
        sinv = cst[:, K_SIN:K_SIN + 32].rearrange("p (t k) -> p t k", t=TT)
        one = cst[:, K_ONE:K_ONE + 1]
        b_ada, normw = prm[:, 0, 0:96], prm[:, 0, 96:128]

        s_in = sem("inputs_landed")
        s_x = [sem(f"x_landed{t}") for t in range(TT)]
        landed = [sem(f"raw_landed{s}") for s in range(SLOTS)]
        lo_ready = sem("w_lo_ready")
        mac_even = sem("ada_first_tile_summed")
        mac_done = sem("ada_last_tile_summed")
        hi_ready = sem("w_hi_ready")
        pe_used = sem("unit_multiplied")
        main_free = sem("main_free")
        v_seq, s_seq = sem("vector_self"), sem("scalar_self")
        s_cT = sem("c_transposed")
        s_cc = sem("c_copied")
        s_silu = sem("c_silu")
        s_col = sem("ada_columns")
        s_colc = sem("ada_columns_copied")
        s_prt = sem("params_transposed")
        s_prm = sem("params_copied")
        s_xn = sem("x_normed")
        s_xms = sem("x_mean_square")
        s_xsq = sem("x_root")
        s_xrs = sem("x_rstd")
        s_xT = sem("x_transposed")
        s_xTc = sem("x_transpose_copied")
        s_mod = sem("mod_ready")
        s_h = sem("h_ready")
        s_ahi = sem("a_hi_ready")
        s_alo = sem("a_lo_ready")
        s_ph = sem("pool_self")
        s_blk0 = sem("blocks_float")
        s_kvf = sem("kv_vector_done")
        s_gb = sem("gate_spread")
        s_gt = sem("gate_transposed")
        s_gc = sem("gate_copied")
        s_gd = sem("gate_in_dram")
        s_du = sem("dt_abs")
        s_de = sem("dt_exp")
        s_adt = sem("adt_ready")
        s_dcp = sem("decay_sums")
        s_dec = sem("decays_ready")
        s_ztanh = sem("z_tanh")
        s_T = sem("xbc_transposed")
        s_conv = sem("conv_done")
        s_cth = sem("conv_tanh")
        s_cs = sem("conv_silu")
        s_ua = sem("segment_operand")
        s_seg = sem("segment_sums")
        s_dm = sem("segment_decays")
        s_A = sem("ssd_tok_major")
        s_bt = sem("b_tok_copied")
        s_m = sem("ssd_operands")
        s_Bq = sem("ssd_diag_done")
        s_st = sem("state_copied")
        s_C = sem("ssd_off_done")
        s_y = sem("y_gated")
        s_D = sem("y_transposed")
        s_Dc = sem("y_stored")
        s_krot = sem("k_rotated")
        s_kt = sem("kv_transposed")
        s_ktc = sem("kv_transpose_copied")
        s_blk = sem("blocks_ready")
        s_bhi = sem("blocks_hi")
        s_gl1 = sem("gelu_arg")
        s_gl2 = sem("gelu_tanh")
        s_gl3 = sem("gelu_done")
        s_cmp = sem("compressed")
        s_cmpc = sem("compressed_copied")
        s_w2 = sem("w2_landed")
        s_zth = sem("zb_tanh")
        s_zs = sem("zb_silu")
        s_qr = sem("q_rotated")
        s_qa = sem("q_transposed")
        s_qT = sem("q_transpose_copied")
        s_sc = sem("scores_done")
        s_mx = sem("score_max")
        s_ex = sem("exps_done")
        s_pw = sem("probs_weighted")
        s_pt = sem("probs_transposed")
        s_ptc = sem("probs_t_scalar")
        s_ptv = sem("probs_t_vector")
        s_o = sem("o_done")
        s_og = sem("o_gated")
        s_oT = sem("o_transposed")
        s_oTc = sem("o_stored")
        s_gth = sem("merge_tanh")
        s_gsp = [sem("merge_spilled0"), sem("merge_spilled1")]
        s_gfree = [sem("spill_buffer_free0"), sem("spill_buffer_free1")]
        s_gmod = sem("gate_mod_ready")
        s_rms = sem("y_mean_square")
        s_rsq = sem("y_root")
        s_gl = [sem("merge_loaded0"), sem("merge_loaded1")]
        s_mgd = sem("merged_block")
        s_mT = sem("merged_transposed")
        s_mTc = sem("merged_copied")
        s_xr = [sem("x_again0"), sem("x_again1")]
        s_xo = sem("out_block")
        s_osq = sem("out_squares")
        s_fms = sem("out_mean_square")
        s_fsq = sem("out_root")
        s_fn = sem("final_norm_landed")
        s_fin = sem("final_ready")
        s_out = sem("out_written")

        win = a["w_in"][0].rearrange("(k p) n -> p k n", p=P)
        wada = a["w_ada"][0].rearrange("(k p) n -> p k n", p=P)
        wpa = a["w_proj_a"][0].rearrange("(k p) n -> p k n", p=P)
        wpb = a["w_proj_b"][0].rearrange("(k p) n -> p k n", p=P)
        wout = a["w_out"][0].rearrange("(k p) n -> p k n", p=P)
        w1 = [a["cmp_k_w1"][0].rearrange("(k p) n -> p k n", p=P),
              a["cmp_v_w1"][0].rearrange("(k p) n -> p k n", p=P)]
        xd = a["x"][0].rearrange("(t p) n -> p t n", p=P)
        od = a["out"][0].rearrange("(t p) n -> p t n", p=P)
        gsc = a["gscr"].rearrange("b (t p) n -> p b t n", p=P)

        heads = [win[:, :, c:c + INNER].rearrange("p k (b n) -> p k b n", b=2) for c in (C_Q, C_ZB)]

        def slot(t, u, n=BW, k=UK):
            return t[:, u % SLOTS, 0:k * n].rearrange("p (k n) -> p k n", k=k)

        block = ctx.enter_context(nc.Block())

        @block.sync
        def _(sp):
            def load_w(reg, i, k, parts):
                r = reg.at_w[k]
                mixed = reg.n_m or (reg is R_Q7 and k < SLOTS - 1)
                if reg is R_Q7 and k == SLOTS - 1:
                    sp.wait_ge(mac_done, R_Q7.m0 + SLOTS)
                sp.wait_ge(lo_ready, reg.w(i, k) + (2 if mixed else 1))
                for dst, src in parts(slot(raw, r)):
                    sp.dma_start(dst, src).then_inc(landed[r % SLOTS], 16)

            def load_m(reg, i, k, col):
                r = reg.at_m[k]
                if reg is R_KQ and k == 0:
                    sp.wait_ge(lo_ready, R_KQ.w0 + SLOTS)
                if reg.n_w:
                    sp.wait_ge(mac_done, reg.m(i, k) + SLOTS)
                else:
                    value = sp.snap(reg.m(i, k) + 1)
                    sp.wait_ge(mac_even, value)
                    sp.wait_ge(mac_done, value)
                kt = UK * (k % UPB)
                sp.dma_start(slot(raw, r), wada[:, kt:kt + UK, bass.ds(col, BW)]).then_inc(landed[r % SLOTS], 16)

            def load_run(reg, i, blocks, cols=()):
                w = m = 0
                for kind in reg.kinds:
                    if kind == "w":
                        load_w(reg, i, w, blocks[w // UPB](w % UPB))
                        w += 1
                    else:
                        load_m(reg, i, m, cols[m // UPB])
                        m += 1

            def plain(w, col):
                return lambda u: lambda t: [(t, w[:, UK * u:UK * u + UK, bass.ds(col, BW)])]

            def group(g):
                cx, cb, cc = g * GW + C_X, g * P + C_B, g * P + C_C
                if not isinstance(g, int):
                    cx, cb, cc = sp.snap(cx), sp.snap(cb), sp.snap(cc)

                def unit(u):
                    k = slice(UK * u, UK * u + UK)
                    return lambda t: [(t[:, :, 0:GW], win[:, k, bass.ds(cx, GW)]),
                                      (t[:, :, GW:GW + P], win[:, k, bass.ds(cb, P)]),
                                      (t[:, :, GW + P:BW], win[:, k, bass.ds(cc, P)])]
                return unit

            def queries(j):
                col = j * P if isinstance(j, int) else sp.snap(j * P)

                def unit(u):
                    return lambda t: [(t[:, k, 2 * n * P:2 * n * P + 2 * P].rearrange("p (b n) -> p b n", b=2),
                                       heads[n][:, UK * u + k, :, bass.ds(col, P)])
                                      for k in range(UK) for n in range(2)]
                return unit

            def merge_gate(base, j):
                return plain(win, j * BW + base if isinstance(j, int) else sp.snap(j * BW + base))

            with sp.Fori(0, ADA_FRONT // 2) as i:
                cols = [sp.snap(i * (2 * BW) + b * BW) for b in range(2)]
                load_run(R_ADA, i, (), cols)
            sp.wait_ge(mac_even, R_ADA.m_end + SLOTS)
            sp.wait_ge(mac_done, R_ADA.m_end + SLOTS)
            for u in range(4):
                t = slot(raw, u, ODD, 8)
                k = slice(8 * u, 8 * u + 8)
                load_w(R_ODD, 0, u, lambda _, t=t, k=k: [(t[:, :, 0:H], win[:, k, C_DT:C_DT + H]),
                                                         (t[:, :, H:ODD], win[:, k, C_NG:C_NG + ODD - H])])
            load_run(R_KV0, 0, [plain(win, C_KV)])
            load_run(R_Z0, 0, [plain(win, C_Z)])
            for n in range(3 * UPB):
                b, u, v = 1 + n // UPB, n % UPB, n // 3
                load_w(R_ZW, 0, n + v, plain(win, C_Z + b * BW)(u))
                if n % 3 == 2:
                    k = 4 * (v % 8)
                    load_w(R_ZW, 0, 4 * v + 3, lambda _, v=v, k=k: [(slot(raw, 3, 256, 4), w1[v // 8][:, k:k + 4, :])])
            load_run(R_G01, 0, [group(0), group(1)])
            with sp.Fori(0, 3) as i:
                load_run(R_G, i, [group(i * 2 + 2), group(i * 2 + 3)])
            load_run(R_KQ, 0, [plain(win, C_KV + BW), plain(win, C_KV + 2 * BW), queries(0)], [2 * D])
            with sp.Fori(0, 3) as i:
                blocks, cols = [], []
                for j2 in range(2):
                    j = i * 2 + j2
                    blocks += [merge_gate(C_GA, j), merge_gate(C_GB, j), queries(i * 2 + (j2 + 1))]
                    cols.append(sp.snap(i * (2 * BW) + (2 * D + BW + j2 * BW)))
                load_run(R_QG, i, blocks, cols)
            load_run(R_Q6, 0, [merge_gate(C_GA, 6), merge_gate(C_GB, 6), queries(7)], [3 * D - BW])
            load_run(R_Q7, 0, [merge_gate(C_GA, 7), merge_gate(C_GB, 7)])

            def project(col):
                return lambda u: plain(wpa, col)(u) if u < UPB // 2 else plain(wpb, col)(u - UPB // 2)

            load_run(R_PR0, 0, [project(0)])
            with sp.Fori(0, 6) as i:
                load_run(R_PR, i, [project(sp.snap(i * BW + BW))])
            load_run(R_PR7, 0, [project(7 * BW)])
            load_run(R_OUT0, 0, [plain(wout, 0)])
            with sp.Fori(0, 3) as i:
                load_run(R_OUT, i, [plain(wout, sp.snap(i * (2 * BW) + BW)), plain(wout, sp.snap(i * (2 * BW) + 2 * BW))])
            load_run(R_OUT7, 0, [plain(wout, 7 * BW)])
            sp.wait_ge(lo_ready, R_OUT7.w_end + SLOTS)
            sp.dma_start(raw[:, :, :].rearrange("p a b -> p (a b)"), a["final_norm_w"].partition_broadcast(P))\
              .then_inc(s_fn, 16)
            for q in range(4):
                for t in range(TT):
                    sp.wait_ge(s_fin, q * TT + t + 1)
                    c = slice(q * 1024, q * 1024 + 1024)
                    sp.dma_start(od[:, t, c], xo[:, t, c]).then_inc(s_out, 16)
            sp.wait_ge(s_out, 16 * 8)

        def multiplied(eng, reg, i, k):
            eng.wait_ge(pe_used, reg.w(i, k) + (1 + SLOTS))

        def emptied(eng, blk_):
            eng.wait_ge(main_free, blk_ + 3)

        @block.tensor
        def _(pe):
            pe.sem_inc(pe_used, SLOTS)
            pe.sem_inc(s_col, 2)
            pe.sem_inc(s_mT, 1)

            def tr(out, in_, k=P):
                return pe.transpose(out, in_, ident[0:k, 0:k])

            def unit(reg, i, k, out, k0, last, n=BW, per=UK, first=0):
                pe.wait_ge(lo_ready, reg.w(i, k) + (1 + SLOTS))
                hi, lo = slot(w_hi, k, n, per), slot(w_lo, k, n, per)
                for kk in range(per):
                    kt = k0 + kk
                    for t in range(TT):
                        tok = slice(t * P, t * P + P)
                        o = out[:, t, 0:n]
                        pe.matmul(o, a_hi[:, kt, tok], hi[:, kk, :], start=kt == first, stop=False)
                        pe.matmul(o, a_lo[:, kt, tok], hi[:, kk, :], start=False, stop=False)
                        ins = pe.matmul(o, a_hi[:, kt, tok], lo[:, kk, :], start=False, stop=kt == last)
                ins.then_inc(pe_used, 1)

            def pair_free(blk_):
                pe.wait_ge(main_free, blk_ + 1)

            def main_block(reg, i, k, blk_, par, hooks=None, alo=None):
                pair_free(blk_)
                for u in range(UPB):
                    if alo is not None:
                        pe.wait_ge(s_alo, alo + u // 2 + 1)
                    unit(reg, i, k + u, M[par], UK * u, KT - 1)
                    for f in (hooks or {}).get(u, ()):
                        f()

            pe.wait_ge(s_in, 16 * 12)
            tr(X[3][:, 0:KT], cst_in[0:KT, :], KT).then_inc(s_cT, 1)
            tr(X[2][:, 0:P], stage[:, 0, :])
            tr(X[2][:, P:2 * P], stage[:, 1, :])
            tr(X[2][:, 2 * P:2 * P + 112], stage[0:112, 2, :], 112).then_inc(s_prt, 1)
            for t in range(TT):
                pe.wait_ge(s_xn, t + 1)
                for q in range(8):
                    n = 8 * t + q
                    if n < 2:
                        pe.wait_ge(s_prm, 1)
                        pe.wait_ge(s_cc, 1)
                    else:
                        pe.wait_ge(s_xTc, n - 1)
                    for k in range(4):
                        ins = tr(X[2 + n % 2][:, k * P:k * P + P], xin[:, t, (4 * q + k) * P:(4 * q + k + 1) * P])
                    ins.then_inc(s_xT, 1)

            def columns(reg, i, k, bank, sums):
                pe.wait_ge(mac_done, reg.m(i, k) + (1 + SLOTS))
                if len(sums) == 2:
                    pe.wait_ge(mac_even, reg.m(i, k) + (1 + SLOTS))
                for c in range(4):
                    for n, s in enumerate(sums):
                        ins = pe.matmul(bank[:, c:c + 1], s[:, c * P:c * P + P], one, start=n == 0,
                                        stop=n == len(sums) - 1)
                ins.then_inc(s_col, 1)

            with pe.Fori(0, ADA_FRONT // 2) as i:
                for b in range(2):
                    pe.wait_ge(s_colc, i * 2 + (b + 1))
                    columns(R_ADA, i, UPB * b + UPB - 1, X[b], acc[b])

            pair_free(B_ODD)
            for u in range(4):
                pe.wait_ge(s_alo, 2 * u + 2)
                unit(R_ODD, 0, u, M[0], 8 * u, KT - 1, n=ODD, per=8)

            def decay_sums():
                pe.wait_ge(s_adt, 1)
                pe.matmul(X[3][:, 0:H], tri, adt[:, 1, :], start=True, stop=True)
                pe.matmul(X[3][:, H:2 * H], after, adt[:, 0, :], start=True, stop=True).then_inc(s_dcp, 1)

            def to_channels(src, n):
                for c in range(n):
                    for t in range(TT):
                        ins = tr(X[c // 2][:, (c % 2) * S + t * P:(c % 2) * S + t * P + P], src[:, t, c * P:c * P + P])
                return ins

            def cmp_channels():
                emptied(pe, B_KV0)
                to_channels(cst0, 4).then_inc(s_kt, 1)

            main_block(R_KV0, 0, 0, B_KV0, 1, {8: [decay_sums]})
            main_block(R_Z0, 0, 0, B_Z, 0, {3: [cmp_channels]})

            def hidden(v):
                w = v // 8
                if v == 0:
                    pe.wait_ge(s_dec, 2)
                if v % 8 == 0:
                    pe.wait_ge(s_blk, w + 1)
                pe.wait_ge(lo_ready, R_ZW.w(0, 4 * v + 3) + (1 + SLOTS))
                hi, lo = slot(w_hi, 3, 256, 4), slot(w_lo, 3, 256, 4)
                for k in range(4):
                    pos = 4 * (v % 8) + k
                    for half in range(2):
                        o = X[2 + half][:, w * 64:w * 64 + 60]
                        cols = slice(half * P, half * P + P)
                        pe.matmul(o, hi[:, k, cols], bhl[:, w, pos, :], start=pos == 0 and w == 0, stop=False,
                                  skip_group_check=True)
                        ins = pe.matmul(o[:, 0:30], lo[:, k, cols], bhl[:, w, pos, 0:30], start=False,
                                        stop=pos == 31, skip_group_check=True)
                ins.then_inc(pe_used, 1)

            for n in range(3 * UPB):
                b, u, v = n // UPB, n % UPB, n // 3
                if u == 0:
                    pair_free(B_Z + 1 + b)
                unit(R_ZW, 0, n + v, M[(1 + b) % 2], UK * u, KT - 1)
                if n % 3 == 2:
                    hidden(v)

            def compress():
                pe.wait_ge(s_gl3, 1)
                pe.wait_ge(s_w2, 32)
                for half in range(2):
                    pe.matmul(X[0][:, 0:30], w2[:, half, :], gel[:, half, 30:60], start=half == 0, stop=half == 1)
                for g in range(2):
                    for half in range(2):
                        ins = pe.matmul(X[1][0:NC, g * DH:g * DH + DH],
                                        gel[:, 2 + half, 30 + g * NC:30 + g * NC + NC],
                                        w2[:, 2 + half, :], start=half == 0, stop=half == 1)
                ins.then_inc(s_cmp, 1)

            def ssd(g):
                def channels():
                    emptied(pe, g + B_G)
                    pe.wait_ge(s_cmpc, 2)
                    to_channels(xst, 4).then_inc(s_T, 1)

                def tokens():
                    pe.wait_ge(s_cs, g + 1)
                    pe.wait_ge(s_Dc, g + 1)
                    for t in range(TT):
                        for c in range(2):
                            tr(X[0][:, t * S + c * P:t * S + c * P + P], cv[:, c, t * P:t * P + P])
                    tr(X[1][:, 0:P], cv[:, 2, 0:P])
                    for t in range(TT):
                        ins = pe.matmul(X[1][:, (1 + t) * P:(2 + t) * P], cv[:, 2, t * P:t * P + P],
                                        cv[:, 3, t * P:t * P + P], start=True, stop=True)
                    ins.then_inc(s_A, 1)
                    pe.wait_ge(s_ua, g + 1)
                    for c in range(2):
                        for r in range(R):
                            ins = pe.matmul(X[2 + c][:, r * P:r * P + P], ua[:, c, r, :], tri, start=True, stop=True)
                    ins.then_inc(s_seg, 1)

                def diag():
                    pe.wait_ge(s_m, g + 1)
                    for c in range(2):
                        for r in range(R):
                            pe.matmul(X[0][:, c * GW + r * HP:c * GW + r * HP + HP], mm[:, c, r, :],
                                      xdt[:, c, r * HP:r * HP + HP], start=True, stop=True)
                    pe.wait_ge(s_bt, g + 1)
                    pe.matmul(X[1][:, 0:GW], btok, xdd, start=True, stop=True).then_inc(s_Bq, 1)

                def off():
                    pe.wait_ge(s_st, g + 1)
                    pe.matmul(X[1][:, GW:2 * GW], cv[:, 3, P:2 * P], stt, start=True, stop=True).then_inc(s_C, 1)

                def y_channels():
                    pe.wait_ge(s_y, g + 1)
                    for c in range(2):
                        for t in range(TT):
                            ins = tr(X[2][:, c * S + t * P:c * S + t * P + P], y0[:, t, c * P:c * P + P])
                    ins.then_inc(s_D, 1)

                return {1: [channels], 7: [tokens], 11: [diag], 13: [off], 15: [y_channels]}

            main_block(R_G01, 0, 0, B_G, 0, {6: [compress]})
            main_block(R_G01, 0, UPB, B_G + 1, 1, ssd(0))
            with pe.Fori(0, 3) as i:
                for b in range(2):
                    main_block(R_G, i, UPB * b, i * 2 + (B_G + 2 + b), b,
                               ssd(i * 2 + (1 + b)))
            main_block(R_KQ, 0, 0, B_KV, 0, ssd(7))

            def keys_channels(x):
                def f():
                    pe.wait_ge(s_krot, x)
                    pe.wait_ge(s_ktc, x)
                    to_channels(kst, 2).then_inc(s_kt, 1)
                return f

            main_block(R_KQ, 0, UPB, B_KV + 1, 1, {8: [keys_channels(1)]})
            main_block(R_KQ, 0, 2 * UPB, B_QG, 0, {5: [keys_channels(2)]})
            pe.wait_ge(s_ktc, 3)

            def head(n, j, a_):
                def q_channels():
                    if a_ == 0:
                        pe.wait_ge(s_qr, j + 1)
                    c = slice(a_ * DH, a_ * DH + DH)
                    for t in range(TT):
                        tr(X[0][:, t * P:t * P + P], qs[:, t, c])
                    for t in range(TT):
                        ins = tr(X[0][:, (2 + t) * P:(3 + t) * P], qr[:, t, c])
                    ins.then_inc(s_qa, 1)

                def scores():
                    pe.wait_ge(s_qT, n + 1)
                    pe.wait_ge(s_oTc, n + 1)
                    for br in range(2):
                        o = X[1][:, br * P:br * P + P]
                        pe.matmul(o, qT[:, 2 * P:3 * P], kT[:, br, a_, 0:P], start=True, stop=False)
                        pe.matmul(o, ident, negm, start=False, stop=True)
                    for t in range(TT):
                        o = X[1][:, 256 + 16 * t:256 + 16 * t + NC]
                        pe.matmul(o, qT[:, t * P:t * P + P], kcT[:, a_, 0:NC], start=True, stop=False)
                        pe.matmul(o, ident, cmpm[:, t, 0:NC], start=False, stop=True)
                    for br in range(2):
                        o = X[2][:, br * S:br * S + S]
                        pe.matmul(o, qT[:, 3 * P:4 * P], kT[:, br, a_, :], start=True, stop=False)
                        ins = pe.matmul(o[:, P:S], ident, negm, start=False, stop=True)
                    ins.then_inc(s_sc, 1)

                def probs_t():
                    pe.wait_ge(s_pw, n + 1)
                    if a_ == 0:
                        pe.wait_ge(s_colc, j + (3 + ADA_FRONT))
                    for br in range(2):
                        for t in range(TT):
                            tr(X[0][:, (2 * br + t) * P:(2 * br + t + 1) * P], p1[:, br, t * P:t * P + P])
                    for br in range(2):
                        tr(X[3][:, br * P:br * P + P], p0[:, br, :])
                    for t in range(TT):
                        ins = tr(X[3][0:NC, (2 + t) * P:(3 + t) * P], pc[:, t, 0:NC])
                    ins.then_inc(s_pt, 1)

                def values():
                    pe.wait_ge(s_ptc, n + 1)
                    pe.wait_ge(s_ptv, n + 1)
                    o = X[1][:, 0:P]
                    pe.matmul(o, pt0[:, 0:P], vv[:, 0, a_, :], start=True, stop=False)
                    pe.matmul(o, pt0[:, P:2 * P], vv[:, 2, a_, :], start=False, stop=False)
                    pe.matmul(o, ptc[0:NC, 0:P], vcT[0:NC, a_, :], start=False, stop=True)
                    o = X[1][:, P:2 * P]
                    for q in range(4):
                        pe.matmul(o, pt1[:, q * P:q * P + P], vv[:, q, a_, :], start=q == 0, stop=False)
                    pe.matmul(o, ptc[0:NC, P:2 * P], vcT[0:NC, a_, :], start=False, stop=True).then_inc(s_o, 1)

                def o_channels():
                    pe.wait_ge(s_og, n + 1)
                    for t in range(TT):
                        ins = tr(X[2][:, t * P:t * P + P], og[:, t, :])
                    ins.then_inc(s_oT, 1)

                return q_channels, scores, probs_t, values, o_channels

            def two_heads(j):
                q0, s0, t0, v0, o0 = head(j * 2, j, 0)
                q1, s1, t1, v1, o1 = head(j * 2 + 1, j, 1)

                def gate_columns():
                    columns(R_KQ, 0, j * UPB + (UPB - 1), X[3], (gacc,))

                return by_block({0: [gate_columns], 3: [q0], 5: [s0], 11: [t0], 13: [v0], 15: [o0],
                                 16: [q1], 18: [s1], 24: [t1], 26: [v1], 28: [o1]}, 2)

            with pe.Fori(0, 3) as i:
                for j2 in range(2):
                    steps = two_heads(i * 2 + j2)
                    for n in range(3):
                        q = 3 * j2 + n
                        main_block(R_QG, i, UPB * q, i * 6 + (B_QG + 1 + q), (1 + q) % 2, steps[n] if n < 2 else {})
            steps = two_heads(6)
            for n in range(3):
                main_block(R_Q6, 0, UPB * n, B_QG + 19 + n, (19 + n) % 2, steps[n] if n < 2 else {})
            steps = two_heads(7)
            for n in range(2):
                main_block(R_Q7, 0, UPB * n, B_QG + 22 + n, (22 + n) % 2, steps[n])

            def project(reg, i, j, hooks, fresh=False):
                for u in range(UPB):
                    half = u // (UPB // 2)
                    if u % (UPB // 2) == 0:
                        pair_free(j * 2 + (B_PR + half))
                    if fresh:
                        pe.wait_ge(s_alo, 8 + u // 2 + 1)
                    unit(reg, i, u, M[half], UK * u, (half + 1) * KT // 2 - 1, first=half * KT // 2)
                    for f in hooks.get(u, ()):
                        f()

            def merged_channels(j):
                def f():
                    pe.wait_ge(s_mgd, j + 1)
                    to_channels(mg, 4).then_inc(s_mT, 1)
                return f

            def gate_row():
                pe.wait_ge(s_gmod, 1)
                tr(X[3][0:KT, 0:P], mod[:, 2 * KT:3 * KT]).then_inc(s_gt, 1)

            project(R_PR0, 0, 0, {4: [gate_row]}, fresh=True)
            with pe.Fori(0, 6) as i:
                project(R_PR, i, i + 1, {5: [merged_channels(i)]})
            project(R_PR7, 0, 7, {5: [merged_channels(6)]})
            main_block(R_OUT0, 0, 0, B_OUT, 0, {5: [merged_channels(7)]}, alo=16)
            with pe.Fori(0, 3) as i:
                for b in range(2):
                    main_block(R_OUT, i, UPB * b, i * 2 + (B_OUT + 1 + b), (1 + b) % 2)
            main_block(R_OUT7, 0, 0, B_OUT + 7, 1)

        @block.scalar
        def _(act):
            seq = Chain(act, s_seq)
            act.sem_inc(s_colc, 2)
            act.sem_inc(s_Dc, 1)
            act.sem_inc(s_oTc, 1)
            act.sem_inc(s_mTc, 1)
            act.sem_inc(s_osq, 1)
            for dst, src in (
                    (cst_in[0:KT, :], a["c"].rearrange("a (t p) -> (a t) p", p=P)),
                    (cst[:, :], a["consts"]),
                    (stage[0:96, 0, :], a["b_ada"].rearrange("a (t p) -> (a t) p", p=P)),
                    (stage[96:128, 0, :], a["norm_w"].rearrange("a (t p) -> (a t) p", p=P)),
                    (stage[:, 1, :], a["conv_w"][0].rearrange("a (t p) -> (a t) p", p=P)),
                    (stage[0:32, 2, :], a["conv_b"].rearrange("a (t p) -> (a t) p", p=P)),
                    (stage[32:48, 2, :], a["ssm_norm_w"].rearrange("a (t p) -> (a t) p", p=P)),
                    (stage[48:80, 2, :], a["cmp_pe_k"][0]),
                    (stage[80:112, 2, :], a["cmp_pe_v"][0]),
                    (dtb[:, 0, :], a["dt_bias"][0].partition_broadcast(P)),
                    (dtb[:, 1, :], a["a_log"][0].partition_broadcast(P)),
                    (dtb[:, 2, :], a["d_skip"][0].partition_broadcast(P))):
                act.dma_start(dst, src).then_inc(s_in, 16)
            for t in range(TT):
                act.dma_start(xin[:, t, :], xd[:, t, :]).then_inc(s_x[t], 16)
            act.wait_ge(s_cT, 1)
            act.activation(cT[:, 0, :], X[3][:, 0:KT], ACT.Copy).then_inc(s_cc, 1)
            seq.step(act.activation(cT[:, 1, :], X[3][:, 0:KT], ACT.Tanh, scale=0.5))
            act.wait_ge(s_prt, 1)
            act.activation(prm[:, 0:2, :].rearrange("p a b -> p (a b)"), X[2][:, 0:2 * P], ACT.Copy)
            act.activation(prm[:, 2, 0:112], X[2][:, 2 * P:2 * P + 112], ACT.Copy).then_inc(s_prm, 1)
            for t in range(TT):
                act.wait_ge(s_x[t], 16)
                act.activation(full[:, 16 * t:16 * t + 16, :].rearrange("p a b -> p (a b)"), xin[:, t, :],
                               ACT.Square, accum_out=stat[:, t:t + 1]).then_inc(s_xms, 1)
            act.wait_ge(s_xrs, 1)
            for t in range(TT):
                act.activation(xin[:, t, :], xin[:, t, :], ACT.Copy, scale=stat[:, 4 + t:5 + t]).then_inc(s_xn, 1)
            for n in range(16):
                t, q = n // 8, n % 8
                act.wait_ge(s_xT, n + 1)
                act.activation(full[:, 4 * q:4 * q + 4, t * P:t * P + P],
                               X[2 + n % 2][:, :].rearrange("p (k s) -> p k s", k=4), ACT.Copy).then_inc(s_xTc, 1)
            with act.Fori(0, ADA_FRONT // 2) as i:
                for b in range(2):
                    act.wait_ge(s_col, i * 2 + (b + 3))
                    act.activation(mod[:, bass.ds(i * 8 + 4 * b, 4)], X[b][:, 0:4], ACT.Copy).then_inc(s_colc, 1)

            def round_a(c):
                act.activation(a_hi[:, 4 * c:4 * c + 4, :], full[:, 4 * c:4 * c + 4, :], ACT.Copy).then_inc(s_ahi, 1)

            def round_behind(reg, k, c):
                def f():
                    multiplied(act, reg, 0, k + 2 * c + 1)
                    round_a(c)
                return f

            def split(reg, i, k, n=SLOT):
                r = reg.at_w[k] % SLOTS
                act.wait_ge(landed[r], reg.landed(i, reg.at_w[k]))
                act.wait_ge(pe_used, reg.w(i, k) + 1)
                act.activation(w_hi[:, k % SLOTS, 0:n], raw[:, r, 0:n], ACT.Copy).then_inc(hi_ready, 1)

            def main_block(reg, i, k, hooks=None):
                for u in range(UPB):
                    split(reg, i, k + u)
                    for f in (hooks or {}).get(u, ()):
                        f()

            for c in range(8):
                act.wait_ge(s_h, c + 1)
                round_a(c)
                if c % 2:
                    split(R_ODD, 0, c // 2, 8 * ODD)

            def dt_exp():
                act.wait_ge(s_du, 1)
                act.activation(tmp[:, 1, :, :], tmp[:, 0, :, :], ACT.Exp)
                act.activation(dtb[:, 1, :], dtb[:, 1, :], ACT.Exp)
                act.activation(wgt[:, :, :], odd[:, :, H:ODD], ACT.Tanh, scale=0.5).then_inc(s_de, 1)

            def decays():
                act.wait_ge(s_dcp, 1)
                act.activation(dec[:, :, :], X[3][:, 0:2 * H].rearrange("p (a h) -> p a h", a=2), ACT.Exp)\
                   .then_inc(s_dec, 2)

            def copy_out(reg, i, k, par, dst):
                def f():
                    multiplied(act, reg, i, k - 1)
                    act.activation(dst, M[par][:, :, :], ACT.Copy).then_inc(main_free, 1)
                return f

            def cmp_store():
                act.wait_ge(s_kt, 1)
                for c in range(2):
                    ins = act.activation(ckT[:, 2 * c:2 * c + 2, :],
                                         X[c][:, :].rearrange("p (c s) -> p c s", c=2), ACT.Copy)
                ins.then_inc(s_ktc, 1)

            def blk_hi(w):
                def f():
                    act.wait_ge(s_blk0, w + 1)
                    act.activation(bhl[:, w, :, 0:30], blk[:, :, :], ACT.Copy).then_inc(s_bhi, 1)
                return f

            def z_tanh(reg, k, b):
                def f():
                    multiplied(act, reg, 0, k - 1)
                    act.activation(za[:, :, b * BW:b * BW + BW], M[b % 2][:, :, :], ACT.Tanh, scale=0.5)\
                       .then_inc(s_ztanh, 1)
                return f

            main_block(R_KV0, 0, 0, {4: [dt_exp], 10: [decays]})
            main_block(R_Z0, 0, 0, {2: [copy_out(R_Z0, 0, 0, 1, cst0[:, :, :])], 5: [cmp_store], 7: [blk_hi(0)],
                                    10: [blk_hi(1)]})
            for n in range(3 * UPB):
                b, u, v = n // UPB, n % UPB, n // 3
                split(R_ZW, 0, n + v)
                if n % 3 == 2:
                    split(R_ZW, 0, 4 * v + 3)
                if u == 2:
                    z_tanh(R_ZW, (n - 3) + (n - 3) // 3 + 1, b)()

            def gelu_tanh():
                act.wait_ge(s_gl1, 1)
                act.activation(gel[:, :, 0:30], gel[:, :, 0:30], ACT.Tanh, scale=0.7978845608028654).then_inc(s_gl2, 1)

            def cmp_values():
                act.wait_ge(s_cmp, 1)
                act.activation(vcT[0:NC, :, :], X[1][0:NC, 0:2 * DH].rearrange("p (g d) -> p g d", g=2), ACT.Copy)\
                   .then_inc(s_cmpc, 1)

            def ssd(g, reg, i, k, par):
                def conv_tanh():
                    act.wait_ge(s_conv, g + 1)
                    act.wait_ge(s_Dc, g + 1)
                    act.activation(th[:, :, :], cv[:, :, :], ACT.Tanh).then_inc(s_cth, 1)

                def decay_exp():
                    act.wait_ge(s_A, g + 1)
                    act.activation(btok, X[1][:, 0:P], ACT.Copy).then_inc(s_bt, 1)
                    act.wait_ge(s_seg, g + 1)
                    for c in range(2):
                        ins = act.activation(mm[:, c, :, :], X[2 + c][:, :].rearrange("p (r s) -> p r s", r=R), ACT.Exp)
                    ins.then_inc(s_dm, 1)

                def state():
                    act.wait_ge(s_Bq, g + 1)
                    act.activation(stt, X[1][:, 0:GW], ACT.Copy).then_inc(s_st, 1)

                return {3: [copy_out(reg, i, k, par, xst[:, :, :])], 8: [conv_tanh], 11: [decay_exp], 15: [state]}

            def ssd_tail(g):
                def y_out():
                    act.wait_ge(s_D, g + 1)
                    for t in range(TT):
                        act.activation(th[:, t, :], y0[:, t, :], ACT.Square, accum_out=ssa[:, t, bass.ds(g, 1)])
                    for c in range(2):
                        ins = act.activation(full[:, bass.ds(g * 2 + c, 1), :], X[2][:, c * S:c * S + S].unsqueeze(1),
                                             ACT.Copy, scale=prm[:, 2, bass.ds(g * 2 + (32 + c), 1)])
                    ins.then_inc(s_Dc, 1)
                return {3: [y_out]}

            main_block(R_G01, 0, 0, {2: [z_tanh(R_G01, 0, 3)], 3: [gelu_tanh], 8: [cmp_values]})
            main_block(R_G01, 0, UPB, ssd(0, R_G01, 0, UPB, 0))
            with act.Fori(0, 3) as i:
                for b in range(2):
                    main_block(R_G, i, UPB * b, both(ssd_tail(i * 2 + b),
                                                     ssd(i * 2 + (1 + b), R_G, i, UPB * b, (1 + b) % 2)))
            main_block(R_KQ, 0, 0, both(ssd_tail(6), ssd(7, R_KQ, 0, 0, 1)))

            def kv_copy(x):
                def f():
                    if x == 2:
                        act.wait_ge(s_kt, 2)
                        act.wait_ge(s_kvf, 1)
                    copy_out(R_KQ, 0, UPB * x, (x - 1) % 2, kst[:, :, :])()
                return f

            def kv_store(x):
                def f():
                    act.wait_ge(s_kt, x + 1)
                    act.activation(kT[:, x - 1, :, :], X[0][:, :].rearrange("p (c s) -> p c s", c=2), ACT.Copy)\
                       .then_inc(s_ktc, 1)
                return f

            main_block(R_KQ, 0, UPB, both(ssd_tail(7), {3: [kv_copy(1)], 12: [kv_store(1)]}))
            main_block(R_KQ, 0, 2 * UPB, {3: [kv_copy(2)], 9: [kv_store(2)]})

            def head(n, a_, j):
                def q_t():
                    act.wait_ge(s_qa, n + 1)
                    act.activation(qT, X[0][:, :], ACT.Copy).then_inc(s_qT, 1)

                def exps():
                    act.wait_ge(s_mx, n + 1)
                    for t in range(TT):
                        act.activation(pc[:, t, 0:NC], X[1][:, 256 + 16 * t:256 + 16 * t + NC], ACT.Exp, scale=SCALE,
                                       bias=mx[:, t, 0:1], accum_out=sm[:, t, 0:1])
                    for br in range(2):
                        act.activation(p0[:, br, :], X[1][:, br * P:br * P + P], ACT.Exp, scale=SCALE,
                                       bias=mx[:, 0, 1 + br:2 + br], accum_out=sm[:, 0, 1 + br:2 + br])
                        ins = act.activation(p1[:, br, :], X[2][:, br * S:br * S + S], ACT.Exp, scale=SCALE,
                                             bias=mx[:, 1, 1 + br:2 + br], accum_out=sm[:, 1, 1 + br:2 + br])
                    ins.then_inc(s_ex, 1)

                def probs_t():
                    act.wait_ge(s_pt, n + 1)
                    act.activation(pt1, X[0][:, :], ACT.Copy).then_inc(s_ptc, 1)

                def o_store():
                    act.wait_ge(s_oT, n + 1)
                    act.activation(full[:, bass.ds(j + (16 + 8 * a_), 1), :], X[2][:, 0:S].unsqueeze(1),
                                   ACT.Copy).then_inc(s_oTc, 1)

                return q_t, exps, probs_t, o_store

            def two_heads(j, regs, i, k, pars):
                q0, e0, t0, o0 = head(j * 2, 0, j)
                q1, e1, t1, o1 = head(j * 2 + 1, 1, j)

                def q_copy():
                    multiplied(act, regs[0], i, k[0] - 1)
                    act.activation(qs[:, :, :], M[pars[0]][:, :, 0:2 * DH], ACT.Copy)
                    act.activation(zt[:, :, :], M[pars[0]][:, :, 2 * DH:BW], ACT.Tanh, scale=0.5).then_inc(s_zth, 1)

                def gate_columns():
                    act.wait_ge(s_col, j + (3 + ADA_FRONT))
                    act.activation(mod[:, bass.ds(j * 4 + 2 * KT, 4)], X[3][:, 0:4], ACT.Copy).then_inc(s_colc, 1)

                def merge_tanh(m):
                    def f():
                        multiplied(act, regs[m + 1], i, k[m + 1] - 1)
                        act.wait_ge(s_gfree[m], j + 1)
                        act.activation(gst[:, 2 * m:2 * m + 2, :], M[pars[m + 1]][:, :, :], ACT.Tanh, scale=0.5)\
                           .then_inc(main_free, 1)
                    return f

                return by_block({3: [q_copy], 4: [gate_columns], 7: [q0], 11: [e0], 15: [t0], 19: [merge_tanh(0), o0],
                                 20: [q1], 24: [e1], 28: [t1], 32: [o1], 35: [merge_tanh(1)]}, 3)

            with act.Fori(0, 3) as i:
                for j2 in range(2):
                    ks = [UPB * (3 * j2 + n) for n in range(3)]
                    steps = two_heads(i * 2 + j2, [R_QG] * 3, i, ks, [(3 * j2 + n) % 2 for n in range(3)])
                    for n in range(3):
                        main_block(R_QG, i, ks[n], steps[n])
            steps = two_heads(6, [R_Q6] * 3, 0, [0, UPB, 2 * UPB], [(18 + n) % 2 for n in range(3)])
            for n in range(3):
                main_block(R_Q6, 0, UPB * n, steps[n])
            steps = two_heads(7, [R_Q7, R_Q7, R_PR0], 0, [0, UPB, 0], [(21 + n) % 2 for n in range(3)])
            main_block(R_Q7, 0, 0, steps[0])
            main_block(R_Q7, 0, UPB, both(steps[1], {2 * c + 5: [round_behind(R_Q7, UPB, c)] for c in range(6)}))

            def y_root():
                act.wait_ge(s_rms, 1)
                act.activation(stat[:, 8:10], stat[:, 8:10], ACT.Sqrt).then_inc(s_rsq, 1)

            def gate_row():
                act.wait_ge(s_gt, 1)
                act.activation(gout[:, :], X[3][0:KT, 0:P], ACT.Copy).then_inc(s_gc, 1)

            def merged_store(j):
                def f():
                    act.wait_ge(s_mT, j + 2)
                    for c in range(2):
                        ins = act.activation(full[:, bass.ds(j * 4 + 2 * c, 2), :],
                                             X[c][:, :].rearrange("p (c s) -> p c s", c=2), ACT.Copy)
                    ins.then_inc(s_mTc, 1)
                return f

            def again(reg, k, sem_, value, c):
                def f():
                    act.wait_ge(sem_, value)
                    multiplied(act, reg, 0, k - 1)
                    round_a(c)
                return f

            main_block(R_PR0, 0, 0, both({1: [round_behind(R_Q7, UPB, 6)]},
                                         both(steps[2], {4: [again(R_PR0, 0, s_oTc, NH + 1, 7)], 5: [y_root],
                                                         8: [gate_row]})))
            with act.Fori(0, 6) as i:
                main_block(R_PR, i, 0, {9: [merged_store(i)]})
            main_block(R_PR7, 0, 0, both({9: [merged_store(6)]},
                                         {2 * c + 5: [round_behind(R_PR7, 0, c)] for c in range(6)}))
            def squares(n):
                def f():
                    act.wait_ge(s_xo, n + 3)
                    act.wait_ge(s_osq, n + 1)
                    for t in range(TT):
                        ins = act.activation(mb[:, t, :], xo[:, t, bass.ds(n * BW, BW)], ACT.Square,
                                             accum_out=ssf[:, t, bass.ds(n, 1)])
                    ins.then_inc(s_osq, 1)
                return f

            main_block(R_OUT0, 0, 0, {1: [round_behind(R_PR7, 0, 6)], 8: [merged_store(7)], 9: [again(R_OUT0, 0, s_mTc, 9, 7)]})
            with act.Fori(0, 3) as i:
                for b in range(2):
                    main_block(R_OUT, i, UPB * b, {5: [squares(i * 2 + b)]})
            main_block(R_OUT7, 0, 0, {5: [squares(6)]})
            squares(7)()
            act.wait_ge(s_fms, 1)
            act.activation(stat[:, 16:18], stat[:, 16:18], ACT.Sqrt).then_inc(s_fsq, 1)

        @block.vector
        def _(v):
            seq = Chain(v, v_seq)
            v.sem_inc(lo_ready, SLOTS)
            v.sem_inc(mac_even, SLOTS)
            v.sem_inc(mac_done, SLOTS)
            v.sem_inc(main_free, 2)
            v.sem_inc(s_xo, 2)

            v.wait_ge(s_cc, 1)
            v.wait_ge(s_seq, 1)
            seq.step(v.scalar_tensor_tensor(cT[:, 2, :], cT[:, 1, :], 1.0, cT[:, 0, :], ALU.add, ALU.mult))
            seq.step(v.tensor_scalar(cT[:, 2, :], cT[:, 2, :], 0.5, None, ALU.mult))
            seq.flat()

            def mac(reg, i, k, sums):
                r = reg.at_m[k]
                v.wait_ge(landed[r % SLOTS], reg.landed(i, r))
                t = slot(raw, r)
                for kk in range(UK):
                    kt = UK * (k % UPB) + kk
                    s, to = cT[:, 2, kt:kt + 1], sums[kk % len(sums)]
                    if len(sums) == 2:
                        v.wait_ge((mac_even, mac_done)[kk], reg.m(i, k) + SLOTS)
                    if kt < len(sums):
                        ins = v.tensor_scalar(to, t[:, kk, :], s, None, ALU.mult)
                    else:
                        ins = v.scalar_tensor_tensor(to, t[:, kk, :], s, to, ALU.mult, ALU.add)
                    if kk == 0 and len(sums) == 2:
                        ins.then_inc(mac_even, 1)
                    elif kk == 0:
                        seq.step(ins)
                ins.then_inc(mac_done, 1)
                if len(sums) == 1:
                    v.wait_ge(mac_done, reg.m(i, k) + (1 + SLOTS))

            v.wait_ge(s_prt, 1)
            with v.Fori(0, ADA_FRONT // 2) as i:
                for b in range(2):
                    v.wait_ge(s_col, i * 2 + (b + 1))
                    for u in range(UPB):
                        mac(R_ADA, i, UPB * b + u, acc[b])
            v.wait_ge(s_prm, 1)
            v.wait_ge(s_colc, 2 + ADA_FRONT)
            v.tensor_tensor(mod[:, 0:2 * KT], mod[:, 0:2 * KT], b_ada[:, 0:2 * KT], ALU.add).then_inc(s_mod, 1)
            v.wait_ge(s_mod, 1)
            seq.step(v.scalar_tensor_tensor(hsc[:, :], mod[:, KT:2 * KT], 1.0, normw, ALU.add, ALU.mult))
            v.wait_ge(s_xTc, 16)

            def modulate(c):
                for k in range(4 * c, 4 * c + 4):
                    ins = v.tensor_scalar(full[:, k, :], full[:, k, :], hsc[:, k:k + 1], mod[:, k:k + 1],
                                          ALU.mult, ALU.add)
                ins.then_inc(s_h, 1)

            def low_a(base, c):
                def f():
                    v.wait_ge(s_ahi, base + c + 1)
                    v.tensor_tensor(a_lo[:, 4 * c:4 * c + 4, :], full[:, 4 * c:4 * c + 4, :],
                                    a_hi[:, 4 * c:4 * c + 4, :].bitcast(F32), ALU.subtract).then_inc(s_alo, 1)
                return f

            def split(reg, i, k, n=SLOT):
                r = reg.at_w[k] % SLOTS
                v.wait_ge(hi_ready, reg.w(i, k) + 1)
                v.tensor_tensor(w_lo[:, k % SLOTS, 0:n], raw[:, r, 0:n],
                                w_hi[:, k % SLOTS, 0:n].bitcast(F32), ALU.subtract).then_inc(lo_ready, 1)

            def main_block(reg, i, k, hooks=None):
                for u in range(k, k + UPB):
                    split(reg, i, u)
                    if reg.n_m and u % 3 == 2:
                        m = u // 3
                        if m % UPB == 0:
                            v.wait_ge(s_col, (reg.m(i, m) - R_KQ.m0) // UPB + (2 + ADA_FRONT)
                                      if isinstance(i, int) else i * 2 + (2 + ADA_FRONT + 1 + m // UPB))
                        mac(reg, i, m, (gacc[:, :],))
                    for f in (hooks or {}).get(u - k, ()):
                        f()

            modulate(0)
            for c in range(8):
                if c < 7:
                    modulate(c + 1)
                low_a(0, c)()
                if c % 2:
                    split(R_ODD, 0, c // 2, 8 * ODD)

            def dt_abs():
                multiplied(v, R_ODD, 0, 3)
                v.tensor_copy(odd[:, :, :], M[0][:, :, 0:ODD]).then_inc(main_free, 1)
                emptied(v, B_ODD)
                seq.step(v.tensor_tensor(odd[:, :, 0:H], odd[:, :, 0:H],
                                         dtb[:, 0, :].unsqueeze(1).to_broadcast([P, TT, H]), ALU.add))
                seq.step(v.tensor_scalar(tmp[:, 0, :, :], odd[:, :, 0:H], -1.0, None, ALU.mult))
                v.tensor_tensor(tmp[:, 0, :, :], tmp[:, 0, :, :], odd[:, :, 0:H], ALU.min).then_inc(s_du, 1)

            def dt_finish():
                v.wait_ge(s_de, 1)
                u_, z, z2 = tmp[:, 1, :, :], tmp[:, 0, :, :], tmp[:, 2, :, :]
                seq.step(v.tensor_scalar(z, u_, 2.0, None, ALU.add))
                seq.step(v.reciprocal(z, z))
                seq.step(v.tensor_tensor(z, z, u_, ALU.mult))
                seq.step(v.tensor_tensor(z2, z, z, ALU.mult))
                seq.step(v.tensor_scalar(dts[:, :, :], z2, 1.0 / 19, None, ALU.mult))
                for n in range(17, 1, -2):
                    seq.step(v.scalar_tensor_tensor(dts[:, :, :], dts[:, :, :], 1.0 / n, z2, ALU.add, ALU.mult))
                seq.step(v.scalar_tensor_tensor(dts[:, :, :], dts[:, :, :], 1.0, z, ALU.add, ALU.mult))
                seq.step(v.tensor_scalar(z2, odd[:, :, 0:H], 0.0, None, ALU.max))
                seq.step(v.scalar_tensor_tensor(dts[:, :, :], dts[:, :, :], 2.0, z2, ALU.mult, ALU.add))
                v.scalar_tensor_tensor(adt[:, :, :], dts[:, :, :], -1.0,
                                       dtb[:, 1, :].unsqueeze(1).to_broadcast([P, TT, H]), ALU.mult, ALU.mult)\
                 .then_inc(s_adt, 1)
                v.tensor_scalar(wgt[:, :, :], wgt[:, :, :], 1.0, 0.25, ALU.add, ALU.mult)
                v.tensor_scalar(prm[:, 1, :], prm[:, 1, :], 0.5, None, ALU.mult)
                seq.step(v.tensor_scalar(prm[:, 2, 0:32], prm[:, 2, 0:32], 0.5, None, ALU.mult))

            def blocks(w):
                def f():
                    v.wait_ge(s_ktc, 1)
                    if w:
                        v.wait_ge(s_blk, w)
                    c = ckT[:, 2 * w:2 * w + 2, :].rearrange("p g (i q) -> p q g i", q=16)
                    for half in range(2):
                        pe_ = prm[:, 2, 48 + 32 * w + 16 * half:64 + 32 * w + 16 * half]
                        for g in range(2):
                            ins = v.tensor_tensor(blk[:, 16 * half:16 * half + 16, g * NC:g * NC + NC],
                                                  c[:, :, g, half:half + NC],
                                                  pe_.unsqueeze(2).to_broadcast([P, 16, NC]), ALU.add)
                    ins.then_inc(s_blk0, 1)
                return f

            def blocks_lo(w):
                def f():
                    v.wait_ge(s_bhi, w + 1)
                    v.tensor_tensor(bhl[:, w, :, 30:60], blk[:, :, :], bhl[:, w, :, 0:30].bitcast(F32),
                                    ALU.subtract).then_inc(s_blk, 1)
                return f

            def z_silu(b):
                def f():
                    v.wait_ge(s_ztanh, b + 1)
                    for t in range(TT):
                        ins = v.scalar_tensor_tensor(za[:, t, b * BW:b * BW + BW], za[:, t, b * BW:b * BW + BW], 1.0,
                                                     M[b % 2][:, t, :], ALU.add, ALU.mult)
                    ins.then_inc(main_free, 1)
                return f

            def gelu_arg():
                multiplied(v, R_ZW, 0, 4 * UPB - 1)
                for w in range(2):
                    for half in range(2):
                        ins = v.tensor_copy(gel[:, 2 * w + half, :], X[2 + half][:, 64 * w:64 * w + 60])
                seq.step(ins)
                ga, gb_ = gel[:, :, 0:30], gel[:, :, 30:60]
                seq.step(v.tensor_tensor(gb_, ga, gb_, ALU.add))
                seq.step(v.tensor_tensor(gsq, gb_, gb_, ALU.mult))
                seq.step(v.tensor_scalar(gsq, gsq, 0.044715, 1.0, ALU.mult, ALU.add))
                v.tensor_tensor(ga, gsq, gb_, ALU.mult).then_inc(s_gl1, 1)

            def gelu_finish():
                ga, gb_ = gel[:, :, 0:30], gel[:, :, 30:60]
                v.wait_ge(s_gl2, 1)
                seq.step(v.scalar_tensor_tensor(gb_, ga, 1.0, gb_, ALU.add, ALU.mult))
                v.tensor_scalar(gb_, gb_, 0.5, None, ALU.mult).then_inc(s_gl3, 1)

            def cmp_keys():
                v.wait_ge(s_cmp, 1)
                v.tensor_copy(kcT[:, :, 0:NC], X[0][:, 0:30].rearrange("p (g k) -> p g k", g=2)).then_inc(s_cmpc, 1)

            main_block(R_KV0, 0, 0, {2: [dt_abs], 6: [dt_finish]})
            main_block(R_Z0, 0, 0, {6: [blocks(0)], 8: [blocks_lo(0)], 9: [blocks(1)], 11: [blocks_lo(1)]})
            for n in range(3 * UPB):
                split(R_ZW, 0, n + n // 3)
                if n % 3 == 2:
                    split(R_ZW, 0, 4 * (n // 3) + 3)
                if n % UPB == 3:
                    z_silu(n // UPB)()
            v.wait_ge(s_dec, 2)

            def wide(x, n):
                return x.unsqueeze(2).to_broadcast([P, R, n])

            def ssd(g):
                def conv(cs):
                    def f():
                        v.wait_ge(s_T, g + 1)
                        tiles = {0: g * 2, 1: g * 2 + 1, 2: g + 16, 3: g + 24}
                        for k in range(3, -1, -1):
                            for c in cs:
                                x = X[c // 2][:, (c % 2) * S:(c % 2) * S + S]
                                w = prm[:, 1, bass.ds(tiles[c] + 32 * k, 1)]
                                if k == 3:
                                    ins = v.tensor_scalar(cv[:, c, :], x, w, prm[:, 2, bass.ds(tiles[c], 1)],
                                                          ALU.mult, ALU.add)
                                else:
                                    s = 3 - k
                                    ins = v.scalar_tensor_tensor(cv[:, c, s:S], x[:, 0:S - s], w, cv[:, c, s:S],
                                                                 ALU.mult, ALU.add)
                            if k or cs[0] == 0:
                                seq.step(ins)
                            else:
                                ins.then_inc(s_conv, 1)
                    return f

                def conv_silu():
                    v.wait_ge(s_cth, g + 1)
                    flat = cv[:, :, :].rearrange("p a b -> p (a b)")
                    v.scalar_tensor_tensor(flat, th[:, :, :].rearrange("p a b -> p (a b)"), 1.0, flat,
                                           ALU.add, ALU.mult).then_inc(s_cs, 1)
                    v.wait_ge(s_cs, g + 1)
                    for c in range(2):
                        ins = v.tensor_tensor(ua[:, c, :, :], wide(adt[:, c, bass.ds(g * R, R)], P),
                                              after.unsqueeze(1).to_broadcast([P, R, P]), ALU.mult)
                    ins.then_inc(s_ua, 1)

                def operands():
                    v.wait_ge(s_A, g + 1)
                    for t in range(TT):
                        x = X[0][:, t * S:t * S + S].rearrange("p (r n) -> p r n", r=R)
                        v.tensor_tensor(xdt[:, t, :].rearrange("p (r n) -> p r n", r=R), x,
                                        wide(dts[:, t, bass.ds(g * R, R)], HP), ALU.mult)
                        v.tensor_tensor(y0[:, t, :].rearrange("p (r n) -> p r n", r=R), x,
                                        wide(dtb[:, 2, bass.ds(g * R, R)], HP), ALU.mult)
                    v.wait_ge(s_bt, g + 1)
                    seq.step(v.tensor_tensor(cbm.rearrange("p (c l) -> p c l", c=2),
                                             X[1][:, P:3 * P].rearrange("p (c l) -> p c l", c=2),
                                             tri.unsqueeze(1).to_broadcast([P, 2, P]), ALU.mult))
                    v.tensor_tensor(xdd.rearrange("p (r n) -> p r n", r=R),
                                    xdt[:, 0, :].rearrange("p (r n) -> p r n", r=R),
                                    wide(dec[:, 1, bass.ds(g * R, R)], HP), ALU.mult)
                    v.wait_ge(s_dm, g + 1)
                    for c in range(2):
                        ins = v.tensor_tensor(mm[:, c, :, :], mm[:, c, :, :],
                                              cbm[:, c * P:c * P + P].unsqueeze(1).to_broadcast([P, R, P]), ALU.mult)
                    ins.then_inc(s_m, 1)

                return {5: [conv((0, 1))], 7: [conv((2, 3))], 9: [conv_silu], 12: [operands]}

            def ssd_tail(g):
                def y_gate():
                    v.wait_ge(s_C, g + 1)
                    yf = y0[:, :, :].rearrange("p a b -> p (a b)")
                    seq.step(v.tensor_tensor(yf, yf, X[0][:, :], ALU.add))
                    seq.step(v.tensor_tensor(yof.rearrange("p (r n) -> p r n", r=R),
                                             X[1][:, GW:2 * GW].rearrange("p (r n) -> p r n", r=R),
                                             wide(dec[:, 0, bass.ds(g * R, R)], HP), ALU.mult))
                    seq.step(v.tensor_tensor(y0[:, 1, :], y0[:, 1, :], yof, ALU.add))
                    v.tensor_tensor(y0[:, :, :], y0[:, :, :], za[:, :, bass.ds(g * GW, GW)], ALU.mult).then_inc(s_y, 1)
                return {1: [y_gate]}

            PER_SSD = 4 + 3 + 1 + 3
            main_block(R_G01, 0, 0, {1: [gelu_arg], 3: [z_silu(3)], 4: [gelu_finish], 8: [cmp_keys]})
            main_block(R_G01, 0, UPB, ssd(0))
            seq.flat()
            with v.Fori(0, 3) as i:
                seq.enter(i, 2 * PER_SSD)
                for b in range(2):
                    main_block(R_G, i, UPB * b, both(ssd_tail(i * 2 + b), ssd(i * 2 + (1 + b))))
                seq.leave(2 * PER_SSD, 3)
            main_block(R_KQ, 0, 0, both(ssd_tail(6), ssd(7)))

            def rope(x, buf):
                def quad(n):
                    return buf[:, n, :].rearrange("p (t g r) -> p t g r", t=TT, g=2)
                h = ROT // 2
                cb = cosv[:, :, 0:h].unsqueeze(2).to_broadcast([P, TT, 2, h])
                sb_ = sinv[:, :, 0:h].unsqueeze(2).to_broadcast([P, TT, 2, h])
                x1, x2 = x[:, :, :, 0:h], x[:, :, :, h:ROT]
                v.tensor_tensor(quad(0), x1, cb, ALU.mult)
                v.tensor_tensor(quad(1), x2, sb_, ALU.mult)
                v.tensor_tensor(quad(2), x2, cb, ALU.mult)
                seq.step(v.tensor_tensor(quad(3), x1, sb_, ALU.mult))
                v.tensor_tensor(x1, quad(0), quad(1), ALU.subtract)
                return v.tensor_tensor(x2, quad(2), quad(3), ALU.add)

            def kv_rope(x):
                def f():
                    emptied(v, B_KV + x - 1)
                    if x == 2:
                        v.wait_ge(s_krot, 1)
                    rope(kst[:, :, 0:2 * DH].rearrange("p t (g d) -> p t g d", g=2), rp).then_inc(s_krot, 1)
                    v.tensor_copy(vv[:, (x - 1) * TT:x * TT, :, :].rearrange("p t g d -> p t (g d)"),
                                  kst[:, :, 2 * DH:BW]).then_inc(s_kvf, 1)
                return f

            main_block(R_KQ, 0, UPB, both(ssd_tail(7), {4: [kv_rope(1)]}))
            main_block(R_KQ, 0, 2 * UPB, {4: [kv_rope(2)]})
            seq.flat()

            def head(n, j, a_):
                def maxima():
                    v.wait_ge(s_sc, n + 1)
                    v.tensor_reduce(mx[:, 0, 1:3], X[1][:, 0:2 * P].rearrange("p (b k) -> p b k", b=2), AX.X, ALU.max)
                    v.tensor_reduce(mx[:, 1, 1:3], X[2][:, :].rearrange("p (b k) -> p b k", b=2), AX.X, ALU.max)
                    seq.step(v.tensor_reduce(mx[:, :, 0], X[1][:, 256:288].rearrange("p (t k) -> p t k", t=2)[:, :, 0:NC],
                                             AX.X, ALU.max))
                    v.tensor_scalar(mx[:, :, :], mx[:, :, :], NEG_CLAMP, -SCALE, ALU.max, ALU.mult).then_inc(s_mx, 1)

                def weights():
                    v.wait_ge(s_ex, n + 1)
                    seq.step(v.tensor_scalar(sm[:, :, :], sm[:, :, :], 1e-30, None, ALU.max))
                    seq.step(v.reciprocal(sm[:, :, :], sm[:, :, :]))
                    seq.step(v.tensor_tensor(sm[:, :, :], sm[:, :, :],
                                             wgt[:, :, bass.ds(j * 3 + 24 * a_, 3)], ALU.mult))
                    v.tensor_tensor(p0[:, :, :], p0[:, :, :], sm[:, 0, 1:3].unsqueeze(2).to_broadcast([P, 2, P]), ALU.mult)
                    v.tensor_tensor(p1[:, :, :], p1[:, :, :], sm[:, 1, 1:3].unsqueeze(2).to_broadcast([P, 2, S]), ALU.mult)
                    v.tensor_tensor(pc[:, :, 0:NC], pc[:, :, 0:NC],
                                    sm[:, :, 0].unsqueeze(2).to_broadcast([P, TT, NC]), ALU.mult).then_inc(s_pw, 1)

                def probs_c():
                    v.wait_ge(s_pt, n + 1)
                    v.tensor_copy(pt0, X[3][:, 0:2 * P])
                    v.tensor_copy(ptc[0:NC, :], X[3][0:NC, 2 * P:4 * P]).then_inc(s_ptv, 1)

                def gate_o():
                    v.wait_ge(s_o, n + 1)
                    v.tensor_tensor(og[:, :, :], X[1][:, 0:2 * P].rearrange("p (t d) -> p t d", t=TT),
                                    zt[:, :, a_ * DH:a_ * DH + DH], ALU.mult).then_inc(s_og, 1)

                return maxima, weights, probs_c, gate_o

            def two_heads(j, par):
                def q_prepare():
                    v.wait_ge(s_zth, j + 1)
                    for t in range(TT):
                        ins = v.scalar_tensor_tensor(zt[:, t, :], zt[:, t, :], 1.0, M[par][:, t, 2 * DH:BW],
                                                     ALU.add, ALU.mult)
                    ins.then_inc(main_free, 1)
                    seq.step(v.tensor_copy(qr[:, :, :], qs[:, :, :]))
                    rope(qr[:, :, :].rearrange("p t (g d) -> p t g d", g=2), rq).then_inc(s_qr, 1)

                m0, w0, c0, g0 = head(j * 2, j, 0)
                m1, w1_, c1, g1 = head(j * 2 + 1, j, 1)
                return by_block({4: [q_prepare], 9: [m0], 13: [w0], 15: [c0], 17: [g0], 22: [m1], 26: [w1_], 28: [c1],
                                 30: [g1]}, 3)

            PER_J = 2 * 4 + 2 + UPB
            with v.Fori(0, 3) as i:
                seq.enter(i, 2 * PER_J)
                for j2 in range(2):
                    steps = two_heads(i * 2 + j2, j2)
                    for n in range(3):
                        main_block(R_QG, i, UPB * (3 * j2 + n), steps[n])
                seq.leave(2 * PER_J, 3)
            steps = two_heads(6, 0)
            for n in range(3):
                main_block(R_Q6, 0, UPB * n, steps[n])
            steps = two_heads(7, 1)
            main_block(R_Q7, 0, 0, steps[0])
            main_block(R_Q7, 0, UPB, both(steps[1], {2 * c + 5: [low_a(8, c)] for c in range(6)}))

            def y_square():
                v.wait_ge(s_Dc, G + 1)
                seq.step(v.tensor_reduce(stat[:, 8:10], ssa[:, :, :], AX.X, ALU.add))
                v.tensor_scalar(stat[:, 8:10], stat[:, 8:10], 1.0 / (4 * INNER), EPS, ALU.mult, ALU.add)\
                 .then_inc(s_rms, 1)

            def y_rstd():
                v.wait_ge(s_rsq, 1)
                seq.step(v.reciprocal(stat[:, 10:12], stat[:, 8:10]))
                seq.step(v.tensor_scalar(stat[:, 10:12], stat[:, 10:12], 0.5, None, ALU.mult))

            def gate_bias():
                v.wait_ge(s_colc, 2 + ADA_FRONT + 8)
                v.tensor_tensor(mod[:, 2 * KT:3 * KT], mod[:, 2 * KT:3 * KT], b_ada[:, 2 * KT:3 * KT], ALU.add)\
                 .then_inc(s_gmod, 1)

            def merge(j, reg, i):
                def gates():
                    v.wait_ge(s_gl[0], j * 16 + 16)
                    v.wait_ge(s_gl[1], j * 16 + 16)
                    for t in range(TT):
                        v.tensor_scalar(gx[:, t, :], gx[:, t, :], 1.0, stat[:, 10 + t:11 + t], ALU.add, ALU.mult)
                    seq.step(v.tensor_scalar(gx[:, TT:2 * TT, :], gx[:, TT:2 * TT, :], 1.0, None, ALU.add))

                def part_a():
                    multiplied(v, reg, i, UPB // 2 - 1)
                    v.wait_ge(s_mT, j + 1)
                    v.tensor_tensor(mg[:, :, :], gx[:, 0:TT, :], M[0][:, :, :], ALU.mult).then_inc(main_free, 1)

                return {9: [gates], 12: [part_a]}

            def merge_tail(j, reg, i):
                def part_b():
                    multiplied(v, reg, i, -1)
                    v.tensor_tensor(mb[:, :, :], gx[:, TT:2 * TT, :], M[1][:, :, :], ALU.mult).then_inc(main_free, 1)
                    emptied(v, j * 2 + (B_PR + 1))
                    v.tensor_tensor(mg[:, :, :], mb[:, :, :], mg[:, :, :], ALU.add).then_inc(s_mgd, 1)
                return {3: [part_b]}

            main_block(R_PR0, 0, 0, both({1: [low_a(8, 6)]}, both(
                {2: [gate_bias], 4: [y_square], 5: [low_a(8, 7)], 6: [y_rstd]}, merge(0, R_PR0, 0))))
            seq.flat()
            with v.Fori(0, 6) as i:
                seq.enter(i, 1)
                main_block(R_PR, i, 0, both(merge_tail(i, R_PR, i), merge(i + 1, R_PR, i)))
                seq.leave(1, 6)
            main_block(R_PR7, 0, 0, both(merge_tail(6, R_PR7, 0), both(
                merge(7, R_PR7, 0), {2 * c + 5: [low_a(16, c)] for c in range(6)})))
            seq.flat()

            def out_block(n, reg, i, k, par):
                def f():
                    multiplied(v, reg, i, k - 1)
                    v.wait_ge(s_xr[par], (n - par) * 8 + 16)
                    v.wait_ge(s_gb, 32)
                    v.wait_ge(s_xo, n + 2)
                    cols = bass.ds(n * BW, BW)
                    for t in range(TT):
                        ins = v.scalar_tensor_tensor(mg[:, t, :], M[par][:, t, :], 0.5, gateb[:, cols],
                                                     ALU.mult, ALU.mult)
                    ins.then_inc(main_free, 1)
                    emptied(v, n + B_OUT)
                    v.tensor_tensor(xo[:, :, cols], mg[:, :, :], xr[:, TT * par:TT * par + TT, :], ALU.add)\
                     .then_inc(s_xo, 1)
                return f

            main_block(R_OUT0, 0, 0, both(merge_tail(7, R_OUT0, 0), {1: [low_a(16, 6)], 9: [low_a(16, 7)]}))
            v.wait_ge(s_mT, 9)
            with v.Fori(0, 3) as i:
                for b in range(2):
                    main_block(R_OUT, i, UPB * b, {2: [out_block(i * 2 + b, R_OUT, i, UPB * b, b)]})
            main_block(R_OUT7, 0, 0, {2: [out_block(6, R_OUT7, 0, 0, 0)]})
            out_block(7, R_OUT7, 0, UPB, 1)()
            v.wait_ge(s_osq, 9)
            seq.step(v.tensor_reduce(stat[:, 16:18], ssf[:, :, :], AX.X, ALU.add))
            v.tensor_scalar(stat[:, 16:18], stat[:, 16:18], 1.0 / D, EPS, ALU.mult, ALU.add).then_inc(s_fms, 1)
            v.wait_ge(s_fsq, 1)
            seq.step(v.reciprocal(stat[:, 18:20], stat[:, 16:18]))
            v.wait_ge(s_fn, 16)
            fn = raw[:, :, :].rearrange("p a b -> p (a b)")
            for q in range(4):
                for t in range(TT):
                    c = slice(q * 1024, q * 1024 + 1024)
                    v.scalar_tensor_tensor(xo[:, t, c], xo[:, t, c], stat[:, 18 + t:19 + t], fn[:, c],
                                           ALU.mult, ALU.mult).then_inc(s_fin, 1)

        @block.gpsimd
        def _(pool):
            pool.sem_inc(s_gfree[0], 1)
            pool.sem_inc(s_gfree[1], 1)
            pool.memset(stat[:, 20:22], -0.5).then_inc(s_ph, 1)
            pool.wait_ge(s_xms, 2)
            pool.tensor_scalar(stat[:, 2:4], stat[:, 0:2], 1.0 / D, EPS, ALU.mult, ALU.add).then_inc(s_ph, 1)
            pool.wait_ge(s_ph, 2)
            pool.tensor_tensor(stat[:, 4:6], stat[:, 2:4], stat[:, 20:22], ALU.pow).then_inc(s_xrs, 1)
            pool.wait_ge(s_xT, 16)
            for w, name in enumerate(("cmp_k_w2", "cmp_v_w2")):
                pool.dma_start(w2[:, 2 * w:2 * w + 2, :], a[name][0].rearrange("(h p) n -> p h n", p=P))\
                    .then_inc(s_w2, 16)

            def spill(j, m, col):
                emptied(pool, j * 3 + (B_QG + 1 + m))
                pool.dma_start(gsc[:, m, :, bass.ds(col, BW)], gst[:, 2 * m:2 * m + 2, :]).then_inc(s_gsp[m], 16)
                pool.wait_ge(s_gsp[m], j * 16 + 16)
                pool.sem_inc(s_gfree[m], 1)

            with pool.Fori(0, 8) as i:
                col = pool.snap(i * BW)
                for m in range(2):
                    spill(i, m, col)
            pool.wait_ge(s_oTc, NH + 1)
            for m in range(2):
                pool.dma_start(gx[:, TT * m:TT * m + TT, :], gsc[:, m, :, 0:BW]).then_inc(s_gl[m], 16)
            pool.wait_ge(s_gc, 1)
            pool.dma_start(a["gated"].rearrange("(t p) -> t p", p=P), gout[:, :]).then_inc(s_gd, 16)
            pool.wait_ge(s_gd, 16)
            for h in range(2):
                pool.dma_start(gateb[:, h * D // 2:(h + 1) * D // 2],
                               a["gated"][h * D // 2:(h + 1) * D // 2].partition_broadcast(P)).then_inc(s_gb, 16)
            with pool.Fori(0, 7) as i:
                col = pool.snap(i * BW + BW)
                emptied(pool, i * 2 + (B_PR + 1))
                for m in range(2):
                    pool.dma_start(gx[:, TT * m:TT * m + TT, :], gsc[:, m, :, bass.ds(col, BW)]).then_inc(s_gl[m], 16)
            pool.wait_ge(s_mgd, 8)
            with pool.Fori(0, 4) as i:
                for b in range(2):
                    col = pool.snap(i * (2 * BW) + b * BW)
                    pool.wait_ge(s_xo, i * 2 + (b + 1))
                    pool.dma_start(xr[:, TT * b:TT * b + TT, :], xd[:, :, bass.ds(col, BW)]).then_inc(s_xr[b], 16)


def kernel(x, c, w_ada, b_ada, norm_w, w_in, conv_w, conv_b, dt_bias, a_log, d_skip, ssm_norm_w, cmp_pe_k,
           cmp_pe_v, cmp_k_w1, cmp_k_w2, cmp_v_w1, cmp_v_w2, w_proj_a, w_proj_b, w_out, final_norm_w):
    import numpy as np
    import concourse.bacc as bacc
    from concourse.bass_utils import run_bass_kernel_spmd

    row, col = np.arange(P)[:, None], np.arange(P)[None, :]
    consts = np.zeros((P, K_N), np.float32)
    consts[:, K_ID:K_ID + P] = row == col
    consts[:, K_TRI:K_TRI + P] = row <= col
    consts[:, K_AFT:K_AFT + P] = row > col
    consts[:, K_NEG:K_NEG + P] = np.where(col > row, NEG, 0.0)
    pos = np.arange(S)
    cmp_end = np.arange(16) * 16 + 31
    mask = np.where(cmp_end[None, :] <= pos[:, None], 0.0, NEG)
    inv = np.float32(500000.0) ** (-np.arange(0, ROT, 2, dtype=np.float32) / np.float32(ROT))
    ang = pos.astype(np.float32)[:, None] * inv[None, :]
    for t in range(TT):
        tok = slice(t * P, t * P + P)
        consts[:, K_CM + 16 * t:K_CM + 16 * t + 16] = mask[tok]
        consts[:, K_COS + 16 * t:K_COS + 16 * t + 16] = np.cos(ang[tok])
        consts[:, K_SIN + 16 * t:K_SIN + 16 * t + 16] = np.sin(ang[tok])
    consts[:, K_ONE] = 1.0

    given = dict(x=x, c=c, w_ada=w_ada, b_ada=b_ada, norm_w=norm_w, w_in=w_in, conv_w=conv_w, conv_b=conv_b,
                 dt_bias=dt_bias, a_log=a_log, d_skip=d_skip, ssm_norm_w=ssm_norm_w, cmp_pe_k=cmp_pe_k,
                 cmp_pe_v=cmp_pe_v, cmp_k_w1=cmp_k_w1, cmp_k_w2=cmp_k_w2, cmp_v_w1=cmp_v_w1, cmp_v_w2=cmp_v_w2,
                 w_proj_a=w_proj_a, w_proj_b=w_proj_b, w_out=w_out, final_norm_w=final_norm_w, consts=consts)
    nc = bacc.Bacc("TRN2", target_bir_lowering=False, num_devices=1)
    arrays, aps = {}, {}
    for name, value in given.items():
        value = np.ascontiguousarray(value)
        arrays["in_" + name] = value
        aps[name] = nc.dram_tensor("in_" + name, value.shape, F32, kind="ExternalInput").ap()
    aps["out"] = nc.dram_tensor("out", (1, S, D), F32, kind="ExternalOutput").ap()
    aps["gscr"] = nc.dram_tensor("merge_gates", (2, S, D), F32, kind="Internal").ap()
    aps["gated"] = nc.dram_tensor("gate_row", (D,), F32, kind="Internal").ap()
    build(nc, aps)
    r = run_bass_kernel_spmd(nc, [arrays], core_ids=[0])
    return r.results[0]["out"]
```

```python
from contextlib import ExitStack

import concourse.bass as bass
from concourse import mybir

F32 = mybir.dt.float32
F32R = mybir.dt.float32r
BF16 = mybir.dt.bfloat16
ACT = mybir.ActivationFunctionType
ALU = mybir.AluOpType
AX = mybir.AxisListType

P = 128
D = 4096
S = 256
TT = S // P
KT = D // P
EPS = 1e-6
NEG = -1e30
NEG_CLAMP = -1e29

INNER = 2048
G = 8
R = 4
HP = 64
GW = R * HP
H = 32
NH = 16
DH = 128
NC = S // 16 - 1
ROT = DH // 4
SCALE = DH ** -0.5

C_Z = 0
C_X = C_Z + INNER
C_B = C_X + INNER
C_C = C_B + G * P
C_DT = C_C + G * P
C_Q = C_DT + H
C_KV = C_Q + INNER
C_NG = C_KV + 6 * 256
C_ZB = C_NG + NH * 3
C_GA = C_ZB + INNER
C_GB = C_GA + D
ODD = H + NH * 3

BW = 512
UK = 2
UPB = KT // UK
SLOTS = 4
SLOT = UK * BW

ADA_FRONT = 2 * D // BW

K_ID, K_TRI, K_AFT, K_NEG = 0, 128, 256, 384
K_CM = 512
K_COS = K_CM + 32
K_SIN = K_COS + 32
K_ONE = K_SIN + 32
K_N = K_ONE + 1


class Chain:

    def __init__(self, eng, sem):
        self.eng, self.sem, self.total, self.base, self.off = eng, sem, 0, 0, 0

    def enter(self, i=0, per=0):
        self.base, self.off = self.total + i * per, 0

    def leave(self, per, times=1):
        assert self.off == per, (self.off, per)
        self.total += per * times
        self.base, self.off = self.total, 0

    def inc(self, ins):
        self.off += 1
        ins.then_inc(self.sem, 1)

    def flat(self):
        self.total = self.base + self.off
        self.base, self.off = self.total, 0

    def wait(self):
        self.eng.wait_ge(self.sem, self.base + self.off)

    def step(self, ins):
        self.inc(ins)
        self.wait()


def both(x, y):
    return {u: list(x.get(u, ())) + list(y.get(u, ())) for u in {*x, *y}}




def by_block(steps, n):
    return [{u - UPB * b: fs for u, fs in steps.items() if u // UPB == b} for b in range(n)]


class Region:

    def __init__(self, after, kinds, iters=1, dmas=1):
        n_w, n_m = kinds.count("w"), kinds.count("m")
        dmas = dmas if isinstance(dmas, list) else [dmas] * n_w
        assert len(kinds) % SLOTS == 0 and n_w % SLOTS == 0 and len(dmas) == n_w
        self.w0 = after.w_end if after else 0
        self.m0 = after.m_end if after else 0
        self.slot0 = after.slot_end if after else [0] * SLOTS
        self.kinds, self.n_w, self.n_m = kinds, n_w, n_m
        self.at_w = [r for r, k in enumerate(kinds) if k == "w"]
        self.at_m = [r for r, k in enumerate(kinds) if k == "m"]
        self.count, self.per, w = [], [0] * SLOTS, 0
        for r, k in enumerate(kinds):
            self.per[r % SLOTS] += dmas[w] if k == "w" else 1
            w += k == "w"
            self.count.append(self.per[r % SLOTS])
        self.w_end, self.m_end = self.w0 + n_w * iters, self.m0 + n_m * iters
        self.slot_end = [x + y * iters for x, y in zip(self.slot0, self.per)]

    def w(self, i, k):
        return i * self.n_w + (self.w0 + k)

    def m(self, i, k):
        return i * self.n_m + (self.m0 + k)

    def landed(self, i, r):
        s = r % SLOTS
        return i * (16 * self.per[s]) + 16 * (self.slot0[s] + self.count[r])


MIX = "wwwm"
Q_DMAS = [4] * UPB
FRONT = "m" * 8 + ("w" + "m" * 6) * 4
R_A0 = Region(None, "m" * 2 * UPB)
R_A1 = Region(R_A0, FRONT)
R_A = Region(R_A1, FRONT, 6)
R_A8 = Region(R_A, "wwww")
R_ODD = Region(R_A8, "wwww", dmas=2)
R_Z1 = Region(R_ODD, "w" * UPB)
R_ZW = Region(R_Z1, "w" * 3 * UPB)
R_G01 = Region(R_ZW, "w" * 2 * UPB, dmas=3)
R_G = Region(R_G01, "w" * 2 * UPB, 3, dmas=3)
R_KQ = Region(R_G, MIX * UPB, dmas=[1] * 2 * UPB + Q_DMAS)
R_QG = Region(R_KQ, MIX * 2 * UPB, 3, dmas=([1] * 2 * UPB + Q_DMAS) * 2)
R_Q6 = Region(R_QG, MIX * UPB, dmas=[1] * 2 * UPB + Q_DMAS)
R_Q7 = Region(R_Q6, "w" * 2 * UPB)
R_PR0 = Region(R_Q7, "w" * UPB)
R_PR = Region(R_PR0, "w" * UPB, 6)
R_PR7 = Region(R_PR, "w" * UPB)
R_OUT0 = Region(R_PR7, "w" * UPB)
R_OUT = Region(R_OUT0, "w" * 2 * UPB, 3)
R_OUT7 = Region(R_OUT, "w" * UPB)

B_Z0, B_KV0, B_ODD, B_Z, B_G, B_KV = 0, 1, 2, 2, 6, 14
B_QG = 16
B_PR = B_QG + 24
B_OUT = B_PR + 16


def build(nc, a):
    ctx = ExitStack()
    with ctx:
        def sb(name, shape, dt=F32):
            return ctx.enter_context(nc.sbuf_tensor(name, shape, dt))

        def sem(name):
            return ctx.enter_context(nc.semaphore(name))

        a_hi = sb("a_hi", [P, KT, S], F32R)
        a_lo = sb("a_lo", [P, KT, S], F32R)
        full = sb("full", [P, KT, S])
        raw = sb("raw", [P, SLOTS, SLOT])
        w_hi = sb("w_hi", [P, SLOTS, SLOT], F32R)
        w_lo = sb("w_lo", [P, SLOTS, SLOT], F32R)
        cst = sb("cst", [P, K_N])
        msk = sb("msk", [P, 2 * P + 32], BF16)
        prm = sb("prm", [P, 3, P])
        mod = sb("mod", [P, 96])
        hsc = sb("hsc", [P, KT])
        cT = sb("cT", [P, 3, KT])
        dtb = sb("dtb", [P, 3, H])
        dt_work = sb("dt_work", [P, TT * (ODD + 6 * H + NH * 3)])
        stat = sb("stat", [P, 40])
        kcT = sb("kcT", [P, 2, 16])
        vcT = sb("vcT", [P, 2, DH])
        gacc = sb("gacc", [P, BW])
        ssa = sb("ssa", [P, TT, G])
        bhl = sb("bhl", [P, 2, 32, 60], F32R)
        ar = sb("ar", [P, 9216])

        def carve(at, *shape, of=None):
            n = 1
            for s in shape:
                n *= s
            v = (ar if of is None else of)[:, at:at + n]
            if len(shape) == 2:
                v = v.rearrange("p (a b) -> p a b", b=shape[1])
            if len(shape) == 3:
                v = v.rearrange("p (a b c) -> p a b c", b=shape[1], c=shape[2])
            return v, at + n

        odd, at = carve(0, TT, ODD, of=dt_work)
        dts, at = carve(at, TT, H, of=dt_work)
        adt, at = carve(at, TT, H, of=dt_work)
        tmp, at = carve(at, 3, TT, H, of=dt_work)
        dec, at = carve(at, 2, H, of=dt_work)
        wgt, at = carve(at, TT, NH * 3, of=dt_work)

        xin, at = carve(0, TT, D)
        acc1, at = carve(at, BW)
        stage, at = carve(at, 3, P)
        cst_in, at = carve(at, P)
        za, at = carve(0, TT, INNER)
        xst, at = carve(at, TT, BW)
        cv, at = carve(at, 4, S)
        th, at = carve(at, 4, S)
        ua = th.rearrange("p a b -> p (a b)").rearrange("p (c r s) -> p c r s", c=2, r=R)
        mm = xst.rearrange("p a b -> p (a b)").rearrange("p (c r s) -> p c r s", c=2, r=R)
        xdt, at = carve(at, TT, GW)
        y0, at = carve(at, TT, GW)
        cbm, at = carve(at, 2 * P)
        btok, at = carve(at, P)
        xdd, at = carve(at, GW)
        stt, at = carve(at, GW)
        yof = stt
        acc = [(gacc[:, :], dt_work[:, 0:BW]), (acc1, ar[:, TT * D + BW:TT * D + 2 * BW])]
        cst0, at = carve(TT * INNER, TT, BW)
        ckT, at = carve(at, 4, S)
        blk, at = carve(at, 32, 30)
        gel, at = carve(at, 4, 60)
        gsq, at = carve(at, 4, 30)
        w2, at = carve(at, 4, DH)
        oddT, at = carve(TT * D, S)
        hT, at = carve(at, 2, 2 * P)
        kT, at = carve(0, 2, 2, S)
        vv, at = carve(at, 2 * TT, 2, DH)
        at_kv = at
        kst, at = carve(at, TT, BW)
        rp, at = carve(at, 4, 64)
        at = at_kv
        qs, at = carve(at, TT, 2 * DH)
        qr, at = carve(at, TT, 2 * DH)
        zt, at = carve(at, TT, 2 * DH)
        qT, at = carve(at, 4 * P)
        p0, at = carve(at, 2, P)
        p1, at = carve(at, 2, S)
        pc, at = carve(at, TT, 16)
        mx, at = carve(at, TT, 3)
        sm, at = carve(at, TT, 3)
        pt0, at = carve(at, 2 * P)
        ptc, at = carve(at, 2 * P)
        pt1, at = carve(at, 4 * P)
        og, at = carve(at, TT, DH)
        rq, at = carve(at, 4, 64)
        gst, at = carve(at, 2 * TT, BW)
        gx, at = carve(0, 2 * TT, BW)
        mg, at = carve(at, TT, BW)
        mb, at = carve(at, TT, BW)
        xr, at = carve(0, 2 * TT, BW)
        gateb, at = carve(4096, D)
        xo = full[:, :, :].rearrange("p k s -> p (k s)").rearrange("p (t n) -> p t n", t=TT)
        ssf = sb("ssf", [P, TT, 8])
        gout = sb("gout", [KT, P])

        M = [ctx.enter_context(nc.psum_tensor(f"main{i}", [P, TT, BW], F32)) for i in range(2)]
        X = [ctx.enter_context(nc.psum_tensor(f"side{i}", [P, BW], F32)) for i in range(4)]

        ident = cst[:, K_ID:K_ID + P]
        tri = cst[:, K_TRI:K_TRI + P]
        after = cst[:, K_AFT:K_AFT + P]
        ident_b = msk[:, 0:P]
        negm = msk[:, P:2 * P]
        cmpm = msk[:, 2 * P:2 * P + 32].rearrange("p (t k) -> p t k", t=TT)
        cosv = cst[:, K_COS:K_COS + 32].rearrange("p (t k) -> p t k", t=TT)
        sinv = cst[:, K_SIN:K_SIN + 32].rearrange("p (t k) -> p t k", t=TT)
        one = cst[:, K_ONE:K_ONE + 1]
        b_ada, normw = prm[:, 0, 0:96], prm[:, 0, 96:128]

        s_in = sem("inputs_landed")
        s_x = [sem(f"x_landed{t}") for t in range(TT)]
        landed = [sem(f"raw_landed{s}") for s in range(SLOTS)]
        lo_ready = sem("w_lo_ready")
        mac_even = sem("ada_first_tile_summed")
        mac_done = sem("ada_last_tile_summed")
        hi_ready = sem("w_hi_ready")
        pe_used = sem("unit_multiplied")
        main_free = sem("main_free")
        v_seq, s_seq = sem("vector_self"), sem("scalar_self")
        s_cT = sem("c_transposed")
        s_cc = sem("c_copied")
        s_col = sem("ada_columns")
        s_colc = sem("ada_columns_copied")
        s_prt = sem("params_transposed")
        s_prm = sem("params_copied")
        s_xn = sem("x_normed")
        s_xms = sem("x_mean_square")
        s_xrs = sem("x_rstd")
        s_xT = sem("x_transposed")
        s_xTc = sem("x_transpose_copied")
        s_h = sem("modulation_ready")
        s_ahi = sem("a_hi_ready")
        s_alo = sem("a_lo_ready")
        s_ph = sem("pool_self")
        s_blk0 = sem("blocks_float")
        s_kvf = sem("kv_vector_done")
        s_gb = sem("gate_spread")
        s_gt = sem("gate_transposed")
        s_gc = sem("gate_copied")
        s_gd = sem("gate_in_dram")
        s_odd = sem("odd_copied")
        s_oddt = sem("odd_transposed")
        s_hc = sem("hidden_copied")
        s_ht = sem("hidden_transposed")
        s_du = sem("dt_abs")
        s_de = sem("dt_exp")
        s_adt = sem("adt_ready")
        s_dcp = sem("decay_sums")
        s_dec = sem("decays_ready")
        s_ztanh = sem("z_tanh")
        s_T = sem("xbc_transposed")
        s_conv = sem("conv_done")
        s_cth = sem("conv_tanh")
        s_cs = sem("conv_silu")
        s_ua = sem("segment_operand")
        s_seg = sem("segment_sums")
        s_dm = sem("segment_decays")
        s_A = sem("ssd_tok_major")
        s_bt = sem("b_tok_copied")
        s_m = sem("ssd_operands")
        s_Bq = sem("ssd_diag_done")
        s_st = sem("state_copied")
        s_C = sem("ssd_off_done")
        s_y = sem("y_gated")
        s_D = sem("y_transposed")
        s_Dc = sem("y_stored")
        s_krot = sem("k_rotated")
        s_kt = sem("kv_transposed")
        s_ktc = sem("kv_transpose_copied")
        s_blk = sem("blocks_ready")
        s_bhi = sem("blocks_hi")
        s_gl1 = sem("gelu_arg")
        s_gl2 = sem("gelu_tanh")
        s_gl3 = sem("gelu_done")
        s_cmp = sem("compressed")
        s_cmpc = sem("compressed_copied")
        s_w2 = sem("w2_landed")
        s_zth = sem("zb_tanh")
        s_qr = sem("q_rotated")
        s_qa = sem("q_transposed")
        s_qT = sem("q_transpose_copied")
        s_sc = sem("scores_done")
        s_mx = sem("score_max")
        s_ex = sem("exps_done")
        s_pw = sem("probs_weighted")
        s_pt = sem("probs_transposed")
        s_ptc = sem("probs_t_scalar")
        s_ptv = sem("probs_t_vector")
        s_o = sem("o_done")
        s_og = sem("o_gated")
        s_oT = sem("o_transposed")
        s_oTc = sem("o_stored")
        s_gsp = [sem("merge_spilled0"), sem("merge_spilled1")]
        s_gfree = [sem("spill_buffer_free0"), sem("spill_buffer_free1")]
        s_gmod = sem("gate_mod_ready")
        s_rms = sem("y_mean_square")
        s_rsq = sem("y_root")
        s_gl = [sem("merge_loaded0"), sem("merge_loaded1")]
        s_mgd = sem("merged_block")
        s_mT = sem("merged_transposed")
        s_mTc = sem("merged_copied")
        s_xr = [sem("x_again0"), sem("x_again1")]
        s_xo = sem("out_block")
        s_osq = sem("out_squares")
        s_fms = sem("out_mean_square")
        s_fsq = sem("out_root")
        s_fn = sem("final_norm_landed")
        s_fin = sem("final_ready")
        s_out = sem("out_written")

        win = a["w_in"][0].rearrange("(k p) n -> p k n", p=P)
        wada = a["w_ada"][0].rearrange("(k p) n -> p k n", p=P)
        wpa = a["w_proj_a"][0].rearrange("(k p) n -> p k n", p=P)
        wpb = a["w_proj_b"][0].rearrange("(k p) n -> p k n", p=P)
        wout = a["w_out"][0].rearrange("(k p) n -> p k n", p=P)
        w1 = [a["cmp_k_w1"][0].rearrange("(k p) n -> p k n", p=P),
              a["cmp_v_w1"][0].rearrange("(k p) n -> p k n", p=P)]
        xd = a["x"][0].rearrange("(t p) n -> p t n", p=P)
        od = a["out"][0].rearrange("(t p) n -> p t n", p=P)
        gsc = a["gscr"].rearrange("b (t p) n -> p b t n", p=P)

        heads = [win[:, :, c:c + INNER].rearrange("p k (b n) -> p k b n", b=2) for c in (C_Q, C_ZB)]

        def slot(t, u, n=BW, k=UK):
            return t[:, u % SLOTS, 0:k * n].rearrange("p (k n) -> p k n", k=k)

        block = ctx.enter_context(nc.Block())

        @block.sync
        def _(sp):
            def load_w(reg, i, k, parts):
                r = reg.at_w[k]
                mixed = reg.n_m or (reg is R_Q7 and k < SLOTS - 1)
                if reg is R_Q7 and k == SLOTS - 1:
                    sp.wait_ge(mac_done, R_Q7.m0 + SLOTS)
                sp.wait_ge(lo_ready, reg.w(i, k) + (2 if mixed else 1))
                for dst, src in parts(slot(raw, r)):
                    sp.dma_start(dst, src).then_inc(landed[r % SLOTS], 16)

            def load_m(reg, i, k, col):
                r = reg.at_m[k]
                if reg is R_KQ and k == 0:
                    sp.wait_ge(lo_ready, R_KQ.w0 + SLOTS)
                sp.wait_ge(mac_done, reg.m(i, k) + SLOTS)
                kt = UK * (k % UPB)
                sp.dma_start(slot(raw, r), wada[:, kt:kt + UK, bass.ds(col, BW)]).then_inc(landed[r % SLOTS], 16)

            def load_run(reg, i, blocks, cols=()):
                w = m = 0
                for kind in reg.kinds:
                    if kind == "w":
                        load_w(reg, i, w, blocks[w // UPB](w % UPB))
                        w += 1
                    else:
                        load_m(reg, i, m, cols[m // UPB])
                        m += 1

            def plain(w, col):
                return lambda u: lambda t: [(t, w[:, UK * u:UK * u + UK, bass.ds(col, BW)])]

            def group(g):
                cx, cb, cc = g * GW + C_X, g * P + C_B, g * P + C_C
                if not isinstance(g, int):
                    cx, cb, cc = sp.snap(cx), sp.snap(cb), sp.snap(cc)

                def unit(u):
                    k = slice(UK * u, UK * u + UK)
                    return lambda t: [(t[:, :, 0:GW], win[:, k, bass.ds(cx, GW)]),
                                      (t[:, :, GW:GW + P], win[:, k, bass.ds(cb, P)]),
                                      (t[:, :, GW + P:BW], win[:, k, bass.ds(cc, P)])]
                return unit

            def queries(j):
                col = j * P if isinstance(j, int) else sp.snap(j * P)

                def unit(u):
                    return lambda t: [(t[:, k, 2 * n * P:2 * n * P + 2 * P].rearrange("p (b n) -> p b n", b=2),
                                       heads[n][:, UK * u + k, :, bass.ds(col, P)])
                                      for k in range(UK) for n in range(2)]
                return unit

            def merge_gate(base, j):
                return plain(win, j * BW + base if isinstance(j, int) else sp.snap(j * BW + base))

            def front_free(reg, i, r):
                if r >= SLOTS and reg.kinds[r - SLOTS] == "w":
                    sp.wait_ge(lo_ready, reg.w(i, reg.at_w.index(r - SLOTS)) + (1 + SLOTS))
                else:
                    back = reg.at_m.index(r - SLOTS) if r >= SLOTS else r - SLOTS
                    value = sp.snap(reg.m(i, back) + (1 + SLOTS))
                    sp.wait_ge(mac_even, value)
                    sp.wait_ge(mac_done, value)

            def load_front(reg, i, c):
                cols = [sp.snap(c * BW + n * D) for n in range(2)]
                rows = [sp.snap(c * 4 + (UK * n - 4)) for n in range(2)] if reg.n_w else ()
                w = m = 0
                for r, kind in enumerate(reg.kinds):
                    if kind == "w":
                        src = win[:, bass.ds(rows[w % 2], UK), (C_Z, C_KV)[w // 2]:(C_Z, C_KV)[w // 2] + BW]
                        w += 1
                    else:
                        kt = UK * (m % UPB)
                        src = wada[:, kt:kt + UK, bass.ds(cols[m // UPB], BW)]
                        m += 1
                    front_free(reg, i, r)
                    sp.dma_start(slot(raw, r), src).then_inc(landed[r % SLOTS], 16)

            load_front(R_A0, 0, 0)
            load_front(R_A1, 0, 1)
            with sp.Fori(0, 6) as i:
                load_front(R_A, i, i + 2)
            for e in range(4):
                front_free(R_A8, 0, e)
                sp.dma_start(slot(raw, e), win[:, KT - 4 + UK * (e % 2):KT - 4 + UK * (e % 2) + UK,
                                               (C_Z, C_KV)[e // 2]:(C_Z, C_KV)[e // 2] + BW]).then_inc(landed[e], 16)
            for u in range(4):
                t = slot(raw, u, ODD, 8)
                k = slice(8 * u, 8 * u + 8)
                load_w(R_ODD, 0, u, lambda _, t=t, k=k: [(t[:, :, 0:H], win[:, k, C_DT:C_DT + H]),
                                                         (t[:, :, H:ODD], win[:, k, C_NG:C_NG + ODD - H])])
            load_run(R_Z1, 0, [plain(win, C_Z + BW)])
            for n in range(2 * UPB):
                b, u, v = 2 + n // UPB, n % UPB, n // 2
                load_w(R_ZW, 0, n + v, plain(win, C_Z + b * BW)(u))
                if n % 2:
                    k = 4 * (v % 8)
                    load_w(R_ZW, 0, 3 * v + 2, lambda _, v=v, k=k: [(slot(raw, 3 * v + 2, 256, 4),
                                                                     w1[v // 8][:, k:k + 4, :])])
            load_run(R_G01, 0, [group(0), group(1)])
            with sp.Fori(0, 3) as i:
                load_run(R_G, i, [group(i * 2 + 2), group(i * 2 + 3)])
            load_run(R_KQ, 0, [plain(win, C_KV + BW), plain(win, C_KV + 2 * BW), queries(0)], [2 * D])
            with sp.Fori(0, 3) as i:
                blocks, cols = [], []
                for j2 in range(2):
                    j = i * 2 + j2
                    blocks += [merge_gate(C_GA, j), merge_gate(C_GB, j), queries(i * 2 + (j2 + 1))]
                    cols.append(sp.snap(i * (2 * BW) + (2 * D + BW + j2 * BW)))
                load_run(R_QG, i, blocks, cols)
            load_run(R_Q6, 0, [merge_gate(C_GA, 6), merge_gate(C_GB, 6), queries(7)], [3 * D - BW])
            load_run(R_Q7, 0, [merge_gate(C_GA, 7), merge_gate(C_GB, 7)])

            def project(col):
                return lambda u: plain(wpa, col)(u) if u < UPB // 2 else plain(wpb, col)(u - UPB // 2)

            load_run(R_PR0, 0, [project(0)])
            with sp.Fori(0, 6) as i:
                load_run(R_PR, i, [project(sp.snap(i * BW + BW))])
            load_run(R_PR7, 0, [project(7 * BW)])
            load_run(R_OUT0, 0, [plain(wout, 0)])
            with sp.Fori(0, 3) as i:
                load_run(R_OUT, i, [plain(wout, sp.snap(i * (2 * BW) + BW)), plain(wout, sp.snap(i * (2 * BW) + 2 * BW))])
            load_run(R_OUT7, 0, [plain(wout, 7 * BW)])
            sp.wait_ge(lo_ready, R_OUT7.w_end + SLOTS)
            sp.dma_start(raw[:, :, :].rearrange("p a b -> p (a b)"), a["final_norm_w"].partition_broadcast(P))\
              .then_inc(s_fn, 16)
            for q in range(4):
                for t in range(TT):
                    sp.wait_ge(s_fin, q * TT + t + 1)
                    c = slice(q * 1024, q * 1024 + 1024)
                    sp.dma_start(od[:, t, c], xo[:, t, c]).then_inc(s_out, 16)
            sp.wait_ge(s_out, 16 * 8)

        def multiplied(eng, reg, i, k):
            eng.wait_ge(pe_used, reg.w(i, k) + (1 + SLOTS))

        def emptied(eng, blk_):
            eng.wait_ge(main_free, blk_ + 3)

        @block.tensor
        def _(pe):
            pe.sem_inc(pe_used, SLOTS)
            pe.sem_inc(s_col, 2)
            pe.sem_inc(s_mT, 1)

            def tr(out, in_, k=P):
                return pe.transpose(out, in_, ident[0:k, 0:k])

            def unit(reg, i, k, out, k0, last, n=BW, per=UK, first=0):
                pe.wait_ge(lo_ready, reg.w(i, k) + (1 + SLOTS))
                hi, lo = slot(w_hi, k, n, per), slot(w_lo, k, n, per)
                for kk in range(per):
                    kt = k0 + kk
                    for t in range(TT):
                        tok = slice(t * P, t * P + P)
                        o = out[:, t, 0:n]
                        pe.matmul(o, a_hi[:, kt, tok], hi[:, kk, :], start=kt == first, stop=False)
                        pe.matmul(o, a_lo[:, kt, tok], hi[:, kk, :], start=False, stop=False)
                        ins = pe.matmul(o, a_hi[:, kt, tok], lo[:, kk, :], start=False, stop=kt == last)
                ins.then_inc(pe_used, 1)

            def pair_free(blk_):
                pe.wait_ge(main_free, blk_ + 1)

            def main_block(reg, i, k, blk_, par, hooks=None, alo=None):
                pair_free(blk_)
                for u in range(UPB):
                    if alo is not None:
                        pe.wait_ge(s_alo, alo + u // 2 + 1)
                    unit(reg, i, k + u, M[par], UK * u, KT - 1)
                    for f in (hooks or {}).get(u, ()):
                        f()

            pe.wait_ge(s_in, 16 * 12)
            tr(X[3][:, 0:KT], cst_in[0:KT, :], KT).then_inc(s_cT, 1)
            tr(X[2][:, 0:P], stage[:, 0, :])
            tr(X[2][:, P:2 * P], stage[:, 1, :])
            tr(X[2][:, 2 * P:2 * P + 112], stage[0:112, 2, :], 112).then_inc(s_prt, 1)
            for t in range(TT):
                pe.wait_ge(s_xn, t + 1)
                for q in range(8):
                    n = 8 * t + q
                    if n < 2:
                        pe.wait_ge(s_prm, 1)
                        pe.wait_ge(s_cc, 1)
                    else:
                        pe.wait_ge(s_xTc, n - 1)
                    for k in range(4):
                        ins = tr(X[2 + n % 2][:, k * P:k * P + P], xin[:, t, (4 * q + k) * P:(4 * q + k + 1) * P])
                    ins.then_inc(s_xT, 1)

            def columns(reg, i, k, bank, sums):
                pe.wait_ge(mac_done, reg.m(i, k) + (1 + SLOTS))
                if len(sums) == 2:
                    pe.wait_ge(mac_even, reg.m(i, k) + (1 + SLOTS))
                for c in range(4):
                    for n, s in enumerate(sums):
                        ins = pe.matmul(bank[:, c:c + 1], s[:, c * P:c * P + P], one, start=n == 0,
                                        stop=n == len(sums) - 1)
                ins.then_inc(s_col, 1)

            def early_units(reg, i, e0, c):
                pe.wait_ge(s_alo, c + 1)
                for e in (e0, e0 + 1):
                    pe.wait_ge(lo_ready, reg.w(i, e) + (1 + SLOTS))
                    hi, lo = slot(w_hi, e), slot(w_lo, e)
                    for kk in range(UK):
                        kt = c * 4 + (UK * (e % 2) + kk)
                        for t in range(TT):
                            o = M[e0 // 2][:, t, :]
                            tok = slice(t * P, t * P + P)
                            pe.matmul(o, a_hi[:, kt, tok], hi[:, kk, :], start=kt == 0, stop=False)
                            pe.matmul(o, a_lo[:, kt, tok], hi[:, kk, :], start=False, stop=False)
                            ins = pe.matmul(o, a_hi[:, kt, tok], lo[:, kk, :], start=False, stop=kt == KT - 1)
                    ins.then_inc(pe_used, 1)

            def front(reg, i, c):
                for b in range(2):
                    if reg.n_w:
                        early_units(reg, i, 2 * b, c - 1)
                    pe.wait_ge(s_colc, c * 2 + (b + 1))
                    columns(reg, i, UPB * b + UPB - 1, X[b], acc[b])

            pair_free(B_Z0)
            pair_free(B_KV0)
            front(R_A0, 0, 0)
            front(R_A1, 0, 1)
            for i in range(6):
                front(R_A, i, i + 2)
            for b in range(2):
                early_units(R_A8, 0, 2 * b, 7)

            pair_free(B_ODD)
            for u in range(4):
                pe.wait_ge(lo_ready, R_ODD.w(0, u) + (1 + SLOTS))
                hi, lo = slot(w_hi, u, ODD, 8), slot(w_lo, u, ODD, 8)
                for kk in range(8):
                    kt, o = 8 * u + kk, M[0][0:ODD, 0, 0:S]
                    pe.matmul(o, hi[:, kk, :], a_hi[:, kt, :], start=kt == 0, stop=False)
                    pe.matmul(o, hi[:, kk, :], a_lo[:, kt, :], start=False, stop=False)
                    ins = pe.matmul(o, lo[:, kk, :], a_hi[:, kt, :], start=False, stop=kt == KT - 1)
                ins.then_inc(pe_used, 1)

            def odd_tokens():
                pe.wait_ge(s_odd, 1)
                for t in range(TT):
                    ins = tr(X[3][:, t * ODD:t * ODD + ODD], oddT[0:ODD, t * P:t * P + P], ODD)
                ins.then_inc(s_oddt, 1)

            def decay_sums():
                pe.wait_ge(s_adt, 1)
                pe.matmul(X[3][:, 0:H], tri, adt[:, 1, :], start=True, stop=True)
                pe.matmul(X[3][:, H:2 * H], after, adt[:, 0, :], start=True, stop=True).then_inc(s_dcp, 1)

            def to_channels(src, n):
                for c in range(n):
                    for t in range(TT):
                        ins = tr(X[c // 2][:, (c % 2) * S + t * P:(c % 2) * S + t * P + P], src[:, t, c * P:c * P + P])
                return ins

            def cmp_channels():
                emptied(pe, B_KV0)
                to_channels(cst0, 4).then_inc(s_kt, 1)

            main_block(R_Z1, 0, 0, B_Z + 1, 1, {1: [cmp_channels], 2: [odd_tokens], 14: [decay_sums]})

            def hidden(v):
                w = v // 8
                if v == 8:
                    pe.wait_ge(s_dec, 2)
                if v % 8 == 0:
                    pe.wait_ge(s_blk, w + 1)
                pe.wait_ge(lo_ready, R_ZW.w(0, 3 * v + 2) + (1 + SLOTS))
                hi, lo = slot(w_hi, 3 * v + 2, 256, 4), slot(w_lo, 3 * v + 2, 256, 4)
                for k in range(4):
                    pos = 4 * (v % 8) + k
                    pe.matmul(X[2 + w][0:60, 0:256], bhl[:, w, pos, :], hi[:, k, :], start=pos == 0, stop=False,
                              skip_group_check=True)
                    ins = pe.matmul(X[2 + w][0:30, 0:256], bhl[:, w, pos, 0:30], lo[:, k, :], start=False,
                                    stop=pos == 31, skip_group_check=True)
                ins.then_inc(pe_used, 1)

            for n in range(2 * UPB):
                b, u, v = 2 + n // UPB, n % UPB, n // 2
                if u == 0:
                    pair_free(B_Z + b)
                unit(R_ZW, 0, n + v, M[b % 2], UK * u, KT - 1)
                if n % 2:
                    hidden(v)

            def hidden_channels():
                pe.wait_ge(s_hc, 1)
                for w in range(2):
                    for half in range(2):
                        o = X[0][:, 64 * (2 * w + half):64 * (2 * w + half) + 30]
                        pe.matmul(o, hT[0:60, w, half * P:half * P + P], ident[0:60, 0:30], start=True, stop=False)
                        ins = pe.matmul(o, hT[0:60, w, half * P:half * P + P], ident[0:60, 30:60],
                                        start=False, stop=True)
                ins.then_inc(s_ht, 1)

            def compress():
                pe.wait_ge(s_gl3, 1)
                pe.wait_ge(s_w2, 32)
                for half in range(2):
                    pe.matmul(X[0][:, 0:30], w2[:, half, :], gel[:, half, 30:60], start=half == 0, stop=half == 1)
                for g in range(2):
                    for half in range(2):
                        ins = pe.matmul(X[1][0:NC, g * DH:g * DH + DH],
                                        gel[:, 2 + half, 30 + g * NC:30 + g * NC + NC],
                                        w2[:, 2 + half, :], start=half == 0, stop=half == 1)
                ins.then_inc(s_cmp, 1)

            def ssd(g):
                def channels():
                    emptied(pe, g + B_G)
                    pe.wait_ge(s_cmpc, 2)
                    to_channels(xst, 4).then_inc(s_T, 1)

                def tokens():
                    pe.wait_ge(s_cs, g + 1)
                    pe.wait_ge(s_Dc, g + 1)
                    for t in range(TT):
                        for c in range(2):
                            tr(X[0][:, t * S + c * P:t * S + c * P + P], cv[:, c, t * P:t * P + P])
                    tr(X[1][:, 0:P], cv[:, 2, 0:P])
                    for t in range(TT):
                        ins = pe.matmul(X[1][:, (1 + t) * P:(2 + t) * P], cv[:, 2, t * P:t * P + P],
                                        cv[:, 3, t * P:t * P + P], start=True, stop=True)
                    ins.then_inc(s_A, 1)
                    pe.wait_ge(s_ua, g + 1)
                    for c in range(2):
                        for r in range(R):
                            ins = pe.matmul(X[2 + c][:, r * P:r * P + P], ua[:, c, r, :], tri, start=True, stop=True)
                    ins.then_inc(s_seg, 1)

                def diag():
                    pe.wait_ge(s_m, g + 1)
                    for c in range(2):
                        for r in range(R):
                            pe.matmul(X[0][:, c * GW + r * HP:c * GW + r * HP + HP], mm[:, c, r, :],
                                      xdt[:, c, r * HP:r * HP + HP], start=True, stop=True)
                    pe.wait_ge(s_bt, g + 1)
                    pe.matmul(X[1][:, 0:GW], btok, xdd, start=True, stop=True).then_inc(s_Bq, 1)

                def off():
                    pe.wait_ge(s_st, g + 1)
                    pe.matmul(X[1][:, GW:2 * GW], cv[:, 3, P:2 * P], stt, start=True, stop=True).then_inc(s_C, 1)

                def y_channels():
                    pe.wait_ge(s_y, g + 1)
                    for c in range(2):
                        for t in range(TT):
                            ins = tr(X[2][:, c * S + t * P:c * S + t * P + P], y0[:, t, c * P:c * P + P])
                    ins.then_inc(s_D, 1)

                return {1: [channels], 7: [tokens], 11: [diag], 13: [off], 15: [y_channels]}

            main_block(R_G01, 0, 0, B_G, 0, {1: [hidden_channels], 9: [compress]})
            main_block(R_G01, 0, UPB, B_G + 1, 1, ssd(0))
            with pe.Fori(0, 3) as i:
                for b in range(2):
                    main_block(R_G, i, UPB * b, i * 2 + (B_G + 2 + b), b,
                               ssd(i * 2 + (1 + b)))
            main_block(R_KQ, 0, 0, B_KV, 0, ssd(7))

            def keys_channels(x):
                def f():
                    pe.wait_ge(s_krot, x)
                    pe.wait_ge(s_ktc, x)
                    to_channels(kst, 2).then_inc(s_kt, 1)
                return f

            main_block(R_KQ, 0, UPB, B_KV + 1, 1, {8: [keys_channels(1)]})
            main_block(R_KQ, 0, 2 * UPB, B_QG, 0, {5: [keys_channels(2)]})
            pe.wait_ge(s_ktc, 3)

            def head(n, j, a_):
                def q_channels():
                    if a_ == 0:
                        pe.wait_ge(s_qr, j + 1)
                    c = slice(a_ * DH, a_ * DH + DH)
                    for t in range(TT):
                        tr(X[0][:, t * P:t * P + P], qs[:, t, c])
                    for t in range(TT):
                        ins = tr(X[0][:, (2 + t) * P:(3 + t) * P], qr[:, t, c])
                    ins.then_inc(s_qa, 1)

                def scores():
                    pe.wait_ge(s_qT, n + 1)
                    pe.wait_ge(s_oTc, n + 1)
                    for br in range(2):
                        o = X[1][:, br * P:br * P + P]
                        pe.matmul(o, qT[:, 2 * P:3 * P], kT[:, br, a_, 0:P], start=True, stop=False)
                        pe.matmul(o, ident_b, negm, start=False, stop=True)
                    for t in range(TT):
                        o = X[1][:, 256 + 16 * t:256 + 16 * t + NC]
                        pe.matmul(o, qT[:, t * P:t * P + P], kcT[:, a_, 0:NC], start=True, stop=False)
                        pe.matmul(o, ident_b, cmpm[:, t, 0:NC], start=False, stop=True)
                    for br in range(2):
                        o = X[2][:, br * S:br * S + S]
                        pe.matmul(o, qT[:, 3 * P:4 * P], kT[:, br, a_, :], start=True, stop=False)
                        ins = pe.matmul(o[:, P:S], ident_b, negm, start=False, stop=True)
                    ins.then_inc(s_sc, 1)

                def probs_t():
                    pe.wait_ge(s_pw, n + 1)
                    if a_ == 0:
                        pe.wait_ge(s_colc, j + (3 + ADA_FRONT))
                    for br in range(2):
                        for t in range(TT):
                            tr(X[0][:, (2 * br + t) * P:(2 * br + t + 1) * P], p1[:, br, t * P:t * P + P])
                    for br in range(2):
                        tr(X[3][:, br * P:br * P + P], p0[:, br, :])
                    for t in range(TT):
                        ins = tr(X[3][0:NC, (2 + t) * P:(3 + t) * P], pc[:, t, 0:NC])
                    ins.then_inc(s_pt, 1)

                def values():
                    pe.wait_ge(s_ptc, n + 1)
                    pe.wait_ge(s_ptv, n + 1)
                    o = X[1][:, 0:P]
                    pe.matmul(o, pt0[:, 0:P], vv[:, 0, a_, :], start=True, stop=False)
                    pe.matmul(o, pt0[:, P:2 * P], vv[:, 2, a_, :], start=False, stop=False)
                    pe.matmul(o, ptc[0:NC, 0:P], vcT[0:NC, a_, :], start=False, stop=True)
                    o = X[1][:, P:2 * P]
                    for q in range(4):
                        pe.matmul(o, pt1[:, q * P:q * P + P], vv[:, q, a_, :], start=q == 0, stop=False)
                    pe.matmul(o, ptc[0:NC, P:2 * P], vcT[0:NC, a_, :], start=False, stop=True).then_inc(s_o, 1)

                def o_channels():
                    pe.wait_ge(s_og, n + 1)
                    for t in range(TT):
                        ins = tr(X[2][:, t * P:t * P + P], og[:, t, :])
                    ins.then_inc(s_oT, 1)

                return q_channels, scores, probs_t, values, o_channels

            def two_heads(j):
                q0, s0, t0, v0, o0 = head(j * 2, j, 0)
                q1, s1, t1, v1, o1 = head(j * 2 + 1, j, 1)

                def gate_columns():
                    columns(R_KQ, 0, j * UPB + (UPB - 1), X[3], (gacc,))

                return by_block({0: [gate_columns], 3: [q0], 5: [s0], 11: [t0], 13: [v0], 15: [o0],
                                 16: [q1], 18: [s1], 24: [t1], 26: [v1], 28: [o1]}, 2)

            with pe.Fori(0, 3) as i:
                for j2 in range(2):
                    steps = two_heads(i * 2 + j2)
                    for n in range(3):
                        q = 3 * j2 + n
                        main_block(R_QG, i, UPB * q, i * 6 + (B_QG + 1 + q), (1 + q) % 2, steps[n] if n < 2 else {})
            steps = two_heads(6)
            for n in range(3):
                main_block(R_Q6, 0, UPB * n, B_QG + 19 + n, (19 + n) % 2, steps[n] if n < 2 else {})
            steps = two_heads(7)
            for n in range(2):
                main_block(R_Q7, 0, UPB * n, B_QG + 22 + n, (22 + n) % 2, steps[n])

            def project(reg, i, j, hooks, fresh=False):
                for u in range(UPB):
                    half = u // (UPB // 2)
                    if u % (UPB // 2) == 0:
                        pair_free(j * 2 + (B_PR + half))
                    if fresh:
                        pe.wait_ge(s_alo, 8 + u // 2 + 1)
                    unit(reg, i, u, M[half], UK * u, (half + 1) * KT // 2 - 1, first=half * KT // 2)
                    for f in hooks.get(u, ()):
                        f()

            def merged_channels(j):
                def f():
                    pe.wait_ge(s_mgd, j + 1)
                    to_channels(mg, 4).then_inc(s_mT, 1)
                return f

            def gate_row():
                pe.wait_ge(s_gmod, 1)
                tr(X[3][0:KT, 0:P], mod[:, 2 * KT:3 * KT]).then_inc(s_gt, 1)

            project(R_PR0, 0, 0, {4: [gate_row]}, fresh=True)
            with pe.Fori(0, 6) as i:
                project(R_PR, i, i + 1, {5: [merged_channels(i)]})
            project(R_PR7, 0, 7, {5: [merged_channels(6)]})
            main_block(R_OUT0, 0, 0, B_OUT, 0, {5: [merged_channels(7)]}, alo=16)
            with pe.Fori(0, 3) as i:
                for b in range(2):
                    main_block(R_OUT, i, UPB * b, i * 2 + (B_OUT + 1 + b), (1 + b) % 2)
            main_block(R_OUT7, 0, 0, B_OUT + 7, 1)

        @block.scalar
        def _(act):
            seq = Chain(act, s_seq)
            act.sem_inc(s_colc, 2)
            act.sem_inc(s_Dc, 1)
            act.sem_inc(s_oTc, 1)
            act.sem_inc(s_mTc, 1)
            act.sem_inc(s_osq, 1)
            for dst, src in (
                    (cst_in[0:KT, :], a["c"].rearrange("a (t p) -> (a t) p", p=P)),
                    (cst[:, :], a["consts"]),
                    (stage[0:96, 0, :], a["b_ada"].rearrange("a (t p) -> (a t) p", p=P)),
                    (stage[96:128, 0, :], a["norm_w"].rearrange("a (t p) -> (a t) p", p=P)),
                    (stage[:, 1, :], a["conv_w"][0].rearrange("a (t p) -> (a t) p", p=P)),
                    (stage[0:32, 2, :], a["conv_b"].rearrange("a (t p) -> (a t) p", p=P)),
                    (stage[32:48, 2, :], a["ssm_norm_w"].rearrange("a (t p) -> (a t) p", p=P)),
                    (stage[48:80, 2, :], a["cmp_pe_k"][0]),
                    (stage[80:112, 2, :], a["cmp_pe_v"][0]),
                    (dtb[:, 0, :], a["dt_bias"][0].partition_broadcast(P)),
                    (dtb[:, 1, :], a["a_log"][0].partition_broadcast(P)),
                    (dtb[:, 2, :], a["d_skip"][0].partition_broadcast(P))):
                act.dma_start(dst, src).then_inc(s_in, 16)
            for t in range(TT):
                act.dma_start(xin[:, t, :], xd[:, t, :]).then_inc(s_x[t], 16)
            act.wait_ge(s_cT, 1)
            act.activation(cT[:, 0, :], X[3][:, 0:KT], ACT.Copy).then_inc(s_cc, 1)
            seq.step(act.activation(cT[:, 1, :], X[3][:, 0:KT], ACT.Tanh, scale=0.5))
            act.wait_ge(s_prt, 1)
            act.activation(prm[:, 0:2, :].rearrange("p a b -> p (a b)"), X[2][:, 0:2 * P], ACT.Copy)
            act.activation(prm[:, 2, 0:112], X[2][:, 2 * P:2 * P + 112], ACT.Copy).then_inc(s_prm, 1)
            for t in range(TT):
                act.wait_ge(s_x[t], 16)
                act.activation(full[:, 16 * t:16 * t + 16, :].rearrange("p a b -> p (a b)"), xin[:, t, :],
                               ACT.Square, accum_out=stat[:, t:t + 1]).then_inc(s_xms, 1)
            act.wait_ge(s_xrs, 1)
            for t in range(TT):
                act.activation(xin[:, t, :], xin[:, t, :], ACT.Copy, scale=stat[:, 4 + t:5 + t]).then_inc(s_xn, 1)
            for n in range(16):
                t, q = n // 8, n % 8
                act.wait_ge(s_xT, n + 1)
                act.activation(full[:, 4 * q:4 * q + 4, t * P:t * P + P],
                               X[2 + n % 2][:, :].rearrange("p (k s) -> p k s", k=4), ACT.Copy).then_inc(s_xTc, 1)
            def round_a(c):
                act.activation(a_hi[:, 4 * c:4 * c + 4, :], full[:, 4 * c:4 * c + 4, :], ACT.Copy).then_inc(s_ahi, 1)

            def round_behind(reg, k, c):
                def f():
                    multiplied(act, reg, 0, k + 2 * c + 1)
                    round_a(c)
                return f

            def split(reg, i, k, n=SLOT):
                r = reg.at_w[k] % SLOTS
                act.wait_ge(landed[r], reg.landed(i, reg.at_w[k]))
                act.wait_ge(pe_used, reg.w(i, k) + 1)
                act.activation(w_hi[:, k % SLOTS, 0:n], raw[:, r, 0:n], ACT.Copy).then_inc(hi_ready, 1)

            def main_block(reg, i, k, hooks=None):
                for u in range(UPB):
                    split(reg, i, k + u)
                    for f in (hooks or {}).get(u, ()):
                        f()

            def modulate(c):
                act.wait_ge(s_h, c + 1)
                for k in range(4):
                    kt = bass.ds(c * 4 + k, 1)
                    ins = act.activation(full[:, kt, :], full[:, kt, :], ACT.Identity, scale=hsc[:, kt],
                                         bias=mod[:, kt])
                seq.step(ins)

            act.wait_ge(s_xTc, 16)

            def front(reg, i, c):
                if reg.n_w:
                    modulate(c - 1)
                    rows = bass.ds(c * 4 - 4, 4)
                    act.activation(a_hi[:, rows, :], full[:, rows, :], ACT.Copy).then_inc(s_ahi, 1)
                for b in range(2):
                    if reg.n_w:
                        split(reg, i, 2 * b)
                        split(reg, i, 2 * b + 1)
                    act.wait_ge(s_col, c * 2 + (b + 3))
                    act.activation(mod[:, bass.ds(c * 4 + b * KT, 4)], X[b][:, 0:4], ACT.Copy).then_inc(s_colc, 1)

            front(R_A0, 0, 0)
            front(R_A1, 0, 1)
            seq.flat()
            with act.Fori(0, 6) as i:
                seq.enter(i, 1)
                front(R_A, i, i + 2)
                seq.leave(1, 6)
            split(R_A8, 0, 0)
            modulate(7)
            round_a(7)
            for e in range(1, 4):
                split(R_A8, 0, e)

            def dt_exp():
                act.wait_ge(s_du, 1)
                act.activation(tmp[:, 1, :, :], tmp[:, 0, :, :], ACT.Exp)
                act.activation(dtb[:, 1, :], dtb[:, 1, :], ACT.Exp)
                act.activation(wgt[:, :, :], odd[:, :, H:ODD], ACT.Tanh, scale=0.5).then_inc(s_de, 1)

            def decays():
                act.wait_ge(s_dcp, 1)
                act.activation(dec[:, :, :], X[3][:, 0:2 * H].rearrange("p (a h) -> p a h", a=2), ACT.Exp)\
                   .then_inc(s_dec, 2)

            def copy_out(reg, i, k, par, dst):
                def f():
                    multiplied(act, reg, i, k - 1)
                    act.activation(dst, M[par][:, :, :], ACT.Copy).then_inc(main_free, 1)
                return f

            def cmp_store():
                act.wait_ge(s_kt, 1)
                for c in range(2):
                    ins = act.activation(ckT[:, 2 * c:2 * c + 2, :],
                                         X[c][:, :].rearrange("p (c s) -> p c s", c=2), ACT.Copy)
                ins.then_inc(s_ktc, 1)

            def blk_hi(w):
                def f():
                    act.wait_ge(s_blk0, w + 1)
                    act.activation(bhl[:, w, :, 0:30], blk[:, :, :], ACT.Copy).then_inc(s_bhi, 1)
                return f

            def z_tanh(reg, k, b):
                def f():
                    multiplied(act, reg, 0, k - 1)
                    act.activation(za[:, :, b * BW:b * BW + BW], M[b % 2][:, :, :], ACT.Tanh, scale=0.5)\
                       .then_inc(s_ztanh, 1)
                return f

            split(R_ODD, 0, 0, 8 * ODD)
            z_tanh(R_A8, 2, 0)()
            split(R_ODD, 0, 1, 8 * ODD)
            split(R_ODD, 0, 2, 8 * ODD)
            emptied(act, B_Z0)
            copy_out(R_ODD, 0, 0, 1, cst0[:, :, :])()
            split(R_ODD, 0, 3, 8 * ODD)
            main_block(R_Z1, 0, 0, {5: [cmp_store], 8: [dt_exp, blk_hi(0)], 11: [blk_hi(1)]})
            for n in range(2 * UPB):
                split(R_ZW, 0, n + n // 2)
                if n % 2:
                    split(R_ZW, 0, n + n // 2 + 1)
                if n == 1:
                    decays()
                if n == 3:
                    z_tanh(R_ZW, 0, 1)()
                if n == UPB + 3:
                    z_tanh(R_ZW, 3 * UPB // 2, 2)()

            def gelu_tanh():
                act.wait_ge(s_gl1, 1)
                act.activation(gel[:, :, 0:30], gel[:, :, 0:30], ACT.Tanh, scale=0.7978845608028654).then_inc(s_gl2, 1)

            def cmp_values():
                act.wait_ge(s_cmp, 1)
                act.activation(vcT[0:NC, :, :], X[1][0:NC, 0:2 * DH].rearrange("p (g d) -> p g d", g=2), ACT.Copy)\
                   .then_inc(s_cmpc, 1)

            def ssd(g, reg, i, k, par):
                def conv_tanh():
                    act.wait_ge(s_conv, g + 1)
                    act.wait_ge(s_Dc, g + 1)
                    act.activation(th[:, :, :], cv[:, :, :], ACT.Tanh).then_inc(s_cth, 1)

                def decay_exp():
                    act.wait_ge(s_A, g + 1)
                    act.activation(btok, X[1][:, 0:P], ACT.Copy).then_inc(s_bt, 1)
                    act.wait_ge(s_seg, g + 1)
                    for c in range(2):
                        ins = act.activation(mm[:, c, :, :], X[2 + c][:, :].rearrange("p (r s) -> p r s", r=R), ACT.Exp)
                    ins.then_inc(s_dm, 1)

                def state():
                    act.wait_ge(s_Bq, g + 1)
                    act.activation(stt, X[1][:, 0:GW], ACT.Copy).then_inc(s_st, 1)

                return {3: [copy_out(reg, i, k, par, xst[:, :, :])], 8: [conv_tanh], 11: [decay_exp], 15: [state]}

            def ssd_tail(g):
                def y_out():
                    act.wait_ge(s_D, g + 1)
                    for t in range(TT):
                        act.activation(th[:, t, :], y0[:, t, :], ACT.Square, accum_out=ssa[:, t, bass.ds(g, 1)])
                    for c in range(2):
                        ins = act.activation(full[:, bass.ds(g * 2 + c, 1), :], X[2][:, c * S:c * S + S].unsqueeze(1),
                                             ACT.Copy, scale=prm[:, 2, bass.ds(g * 2 + (32 + c), 1)])
                    ins.then_inc(s_Dc, 1)
                return {3: [y_out]}

            main_block(R_G01, 0, 0, {3: [z_tanh(R_G01, 0, 3)], 6: [gelu_tanh], 13: [cmp_values]})
            main_block(R_G01, 0, UPB, ssd(0, R_G01, 0, UPB, 0))
            with act.Fori(0, 3) as i:
                for b in range(2):
                    main_block(R_G, i, UPB * b, both(ssd_tail(i * 2 + b),
                                                     ssd(i * 2 + (1 + b), R_G, i, UPB * b, (1 + b) % 2)))
            main_block(R_KQ, 0, 0, both(ssd_tail(6), ssd(7, R_KQ, 0, 0, 1)))

            def kv_copy(x):
                def f():
                    if x == 2:
                        act.wait_ge(s_kt, 2)
                        act.wait_ge(s_kvf, 1)
                    copy_out(R_KQ, 0, UPB * x, (x - 1) % 2, kst[:, :, :])()
                return f

            def kv_store(x):
                def f():
                    act.wait_ge(s_kt, x + 1)
                    act.activation(kT[:, x - 1, :, :], X[0][:, :].rearrange("p (c s) -> p c s", c=2), ACT.Copy)\
                       .then_inc(s_ktc, 1)
                return f

            main_block(R_KQ, 0, UPB, both(ssd_tail(7), {3: [kv_copy(1)], 12: [kv_store(1)]}))
            main_block(R_KQ, 0, 2 * UPB, {3: [kv_copy(2)], 9: [kv_store(2)]})

            def head(n, a_, j):
                def q_t():
                    act.wait_ge(s_qa, n + 1)
                    act.activation(qT, X[0][:, :], ACT.Copy).then_inc(s_qT, 1)

                def exps():
                    act.wait_ge(s_mx, n + 1)
                    for t in range(TT):
                        act.activation(pc[:, t, 0:NC], X[1][:, 256 + 16 * t:256 + 16 * t + NC], ACT.Exp, scale=SCALE,
                                       bias=mx[:, t, 0:1], accum_out=sm[:, t, 0:1])
                    for br in range(2):
                        act.activation(p0[:, br, :], X[1][:, br * P:br * P + P], ACT.Exp, scale=SCALE,
                                       bias=mx[:, 0, 1 + br:2 + br], accum_out=sm[:, 0, 1 + br:2 + br])
                        ins = act.activation(p1[:, br, :], X[2][:, br * S:br * S + S], ACT.Exp, scale=SCALE,
                                             bias=mx[:, 1, 1 + br:2 + br], accum_out=sm[:, 1, 1 + br:2 + br])
                    ins.then_inc(s_ex, 1)

                def probs_t():
                    act.wait_ge(s_pt, n + 1)
                    act.activation(pt1, X[0][:, :], ACT.Copy).then_inc(s_ptc, 1)

                def o_store():
                    act.wait_ge(s_oT, n + 1)
                    act.activation(full[:, bass.ds(j + (16 + 8 * a_), 1), :], X[2][:, 0:S].unsqueeze(1),
                                   ACT.Copy).then_inc(s_oTc, 1)

                return q_t, exps, probs_t, o_store

            def two_heads(j, regs, i, k, pars):
                q0, e0, t0, o0 = head(j * 2, 0, j)
                q1, e1, t1, o1 = head(j * 2 + 1, 1, j)

                def q_copy():
                    multiplied(act, regs[0], i, k[0] - 1)
                    act.activation(qs[:, :, :], M[pars[0]][:, :, 0:2 * DH], ACT.Copy)
                    act.activation(zt[:, :, :], M[pars[0]][:, :, 2 * DH:BW], ACT.Tanh, scale=0.5).then_inc(s_zth, 1)

                def gate_columns():
                    act.wait_ge(s_col, j + (3 + ADA_FRONT))
                    act.activation(mod[:, bass.ds(j * 4 + 2 * KT, 4)], X[3][:, 0:4], ACT.Copy).then_inc(s_colc, 1)

                def merge_tanh(m):
                    def f():
                        multiplied(act, regs[m + 1], i, k[m + 1] - 1)
                        act.wait_ge(s_gfree[m], j + 1)
                        act.activation(gst[:, 2 * m:2 * m + 2, :], M[pars[m + 1]][:, :, :], ACT.Tanh, scale=0.5)\
                           .then_inc(main_free, 1)
                    return f

                return by_block({3: [q_copy], 4: [gate_columns], 7: [q0], 11: [e0], 15: [t0], 19: [merge_tanh(0), o0],
                                 20: [q1], 24: [e1], 28: [t1], 32: [o1], 35: [merge_tanh(1)]}, 3)

            with act.Fori(0, 3) as i:
                for j2 in range(2):
                    ks = [UPB * (3 * j2 + n) for n in range(3)]
                    steps = two_heads(i * 2 + j2, [R_QG] * 3, i, ks, [(3 * j2 + n) % 2 for n in range(3)])
                    for n in range(3):
                        main_block(R_QG, i, ks[n], steps[n])
            steps = two_heads(6, [R_Q6] * 3, 0, [0, UPB, 2 * UPB], [(18 + n) % 2 for n in range(3)])
            for n in range(3):
                main_block(R_Q6, 0, UPB * n, steps[n])
            steps = two_heads(7, [R_Q7, R_Q7, R_PR0], 0, [0, UPB, 0], [(21 + n) % 2 for n in range(3)])
            main_block(R_Q7, 0, 0, steps[0])
            main_block(R_Q7, 0, UPB, both(steps[1], {2 * c + 5: [round_behind(R_Q7, UPB, c)] for c in range(6)}))

            def y_root():
                act.wait_ge(s_rms, 1)
                act.activation(stat[:, 8:10], stat[:, 8:10], ACT.Sqrt).then_inc(s_rsq, 1)

            def gate_row():
                act.wait_ge(s_gt, 1)
                act.activation(gout[:, :], X[3][0:KT, 0:P], ACT.Copy).then_inc(s_gc, 1)

            def merged_store(j):
                def f():
                    act.wait_ge(s_mT, j + 2)
                    for c in range(2):
                        ins = act.activation(full[:, bass.ds(j * 4 + 2 * c, 2), :],
                                             X[c][:, :].rearrange("p (c s) -> p c s", c=2), ACT.Copy)
                    ins.then_inc(s_mTc, 1)
                return f

            def again(reg, k, sem_, value, c):
                def f():
                    act.wait_ge(sem_, value)
                    multiplied(act, reg, 0, k - 1)
                    round_a(c)
                return f

            main_block(R_PR0, 0, 0, both({1: [round_behind(R_Q7, UPB, 6)]},
                                         both(steps[2], {4: [again(R_PR0, 0, s_oTc, NH + 1, 7)], 5: [y_root],
                                                         8: [gate_row]})))
            with act.Fori(0, 6) as i:
                main_block(R_PR, i, 0, {9: [merged_store(i)]})
            main_block(R_PR7, 0, 0, both({9: [merged_store(6)]},
                                         {2 * c + 5: [round_behind(R_PR7, 0, c)] for c in range(6)}))
            def squares(n):
                def f():
                    act.wait_ge(s_xo, n + 3)
                    act.wait_ge(s_osq, n + 1)
                    for t in range(TT):
                        ins = act.activation(mb[:, t, :], xo[:, t, bass.ds(n * BW, BW)], ACT.Square,
                                             accum_out=ssf[:, t, bass.ds(n, 1)])
                    ins.then_inc(s_osq, 1)
                return f

            main_block(R_OUT0, 0, 0, {1: [round_behind(R_PR7, 0, 6)], 8: [merged_store(7)], 9: [again(R_OUT0, 0, s_mTc, 9, 7)]})
            with act.Fori(0, 3) as i:
                for b in range(2):
                    main_block(R_OUT, i, UPB * b, {5: [squares(i * 2 + b)]})
            main_block(R_OUT7, 0, 0, {5: [squares(6)]})
            squares(7)()
            act.wait_ge(s_fms, 1)
            act.activation(stat[:, 16:18], stat[:, 16:18], ACT.Sqrt).then_inc(s_fsq, 1)

        @block.vector
        def _(v):
            seq = Chain(v, v_seq)
            v.sem_inc(lo_ready, SLOTS)
            v.sem_inc(mac_even, SLOTS)
            v.sem_inc(mac_done, SLOTS)
            v.sem_inc(main_free, 2)
            v.sem_inc(s_xo, 2)

            v.wait_ge(s_cc, 1)
            v.wait_ge(s_seq, 1)
            seq.step(v.scalar_tensor_tensor(cT[:, 2, :], cT[:, 1, :], 1.0, cT[:, 0, :], ALU.add, ALU.mult))
            seq.step(v.tensor_scalar(cT[:, 2, :], cT[:, 2, :], 0.5, None, ALU.mult))
            seq.flat()

            def mac(reg, i, k, sums):
                r = reg.at_m[k]
                v.wait_ge(landed[r % SLOTS], reg.landed(i, r))
                t = slot(raw, r)
                for kk in range(UK):
                    kt = UK * (k % UPB) + kk
                    s, to = cT[:, 2, kt:kt + 1], sums[kk % len(sums)]
                    if len(sums) == 2:
                        v.wait_ge((mac_even, mac_done)[kk], reg.m(i, k) + SLOTS)
                    if kt < len(sums):
                        ins = v.tensor_scalar(to, t[:, kk, :], s, None, ALU.mult)
                    else:
                        ins = v.scalar_tensor_tensor(to, t[:, kk, :], s, to, ALU.mult, ALU.add)
                    if kk == 0 and len(sums) == 2:
                        ins.then_inc(mac_even, 1)
                    elif kk == 0:
                        seq.step(ins)
                ins.then_inc(mac_done, 1)
                if len(sums) == 1:
                    v.wait_ge(mac_done, reg.m(i, k) + (1 + SLOTS))

            v.wait_ge(s_prt, 1)
            v.tensor_copy(msk[:, 0:P], ident)
            v.tensor_copy(msk[:, P:2 * P + 32], cst[:, K_NEG:K_CM + 32])
            def modulation(c):
                v.wait_ge(s_colc, c * 2 + 4)
                lo4, hi4 = bass.ds(c * 4, 4), bass.ds(c * 4 + KT, 4)
                v.tensor_tensor(mod[:, lo4], mod[:, lo4], b_ada[:, lo4], ALU.add)
                seq.step(v.tensor_tensor(mod[:, hi4], mod[:, hi4], b_ada[:, hi4], ALU.add))
                v.scalar_tensor_tensor(hsc[:, lo4], mod[:, hi4], 1.0, normw[:, lo4], ALU.add, ALU.mult)\
                 .then_inc(s_h, 1)

            def low_a(base, c):
                def f():
                    v.wait_ge(s_ahi, base + c + 1)
                    v.tensor_tensor(a_lo[:, 4 * c:4 * c + 4, :], full[:, 4 * c:4 * c + 4, :],
                                    a_hi[:, 4 * c:4 * c + 4, :].bitcast(F32), ALU.subtract).then_inc(s_alo, 1)
                return f

            def split(reg, i, k, n=SLOT):
                r = reg.at_w[k] % SLOTS
                v.wait_ge(hi_ready, reg.w(i, k) + 1)
                v.tensor_tensor(w_lo[:, k % SLOTS, 0:n], raw[:, r, 0:n],
                                w_hi[:, k % SLOTS, 0:n].bitcast(F32), ALU.subtract).then_inc(lo_ready, 1)

            def main_block(reg, i, k, hooks=None):
                for u in range(k, k + UPB):
                    split(reg, i, u)
                    if reg.n_m and u % 3 == 2:
                        m = u // 3
                        if m % UPB == 0:
                            v.wait_ge(s_col, (reg.m(i, m) - R_KQ.m0) // UPB + (2 + ADA_FRONT)
                                      if isinstance(i, int) else i * 2 + (2 + ADA_FRONT + 1 + m // UPB))
                        mac(reg, i, m, (gacc[:, :],))
                    for f in (hooks or {}).get(u - k, ()):
                        f()

            def low_front(c):
                v.wait_ge(s_ahi, c + 1)
                rows = bass.ds(c * 4, 4)
                v.tensor_tensor(a_lo[:, rows, :], full[:, rows, :], a_hi[:, rows, :].bitcast(F32), ALU.subtract)\
                 .then_inc(s_alo, 1)

            def front(reg, i, c):
                w = m = 0
                for kind in reg.kinds:
                    if kind == "w":
                        split(reg, i, w)
                        w += 1
                        continue
                    if m % UPB == 0:
                        v.wait_ge(s_col, c * 2 + (m // UPB + 1))
                    mac(reg, i, m, acc[m // UPB])
                    m += 1
                    if reg.n_w and m == 3:
                        modulation(c - 1)
                    if reg.n_w and m == 7:
                        low_front(c - 1)

            front(R_A0, 0, 0)
            v.wait_ge(s_prm, 1)
            front(R_A1, 0, 1)
            seq.flat()
            with v.Fori(0, 6) as i:
                seq.enter(i, 1)
                front(R_A, i, i + 2)
                seq.leave(1, 6)
            modulation(7)
            split(R_A8, 0, 0)
            low_front(7)
            for e in range(1, 4):
                split(R_A8, 0, e)

            def odd_copy():
                multiplied(v, R_ODD, 0, 3)
                emptied(v, B_KV0)
                v.tensor_copy(oddT[0:ODD, :], M[0][0:ODD, 0, 0:S]).then_inc(main_free, 1)
                emptied(v, B_ODD)
                v.sem_inc(s_odd, 1)

            def dt_abs():
                v.wait_ge(s_oddt, 1)
                seq.step(v.tensor_copy(odd[:, :, :], X[3][:, 0:TT * ODD].rearrange("p (t n) -> p t n", t=TT)))
                seq.step(v.tensor_tensor(odd[:, :, 0:H], odd[:, :, 0:H],
                                         dtb[:, 0, :].unsqueeze(1).to_broadcast([P, TT, H]), ALU.add))
                seq.step(v.tensor_scalar(tmp[:, 0, :, :], odd[:, :, 0:H], -1.0, None, ALU.mult))
                v.tensor_tensor(tmp[:, 0, :, :], tmp[:, 0, :, :], odd[:, :, 0:H], ALU.min).then_inc(s_du, 1)

            def dt_finish():
                v.wait_ge(s_de, 1)
                u_, z, z2 = tmp[:, 1, :, :], tmp[:, 0, :, :], tmp[:, 2, :, :]
                seq.step(v.tensor_scalar(z, u_, 2.0, None, ALU.add))
                seq.step(v.reciprocal(z, z))
                seq.step(v.tensor_tensor(z, z, u_, ALU.mult))
                seq.step(v.tensor_tensor(z2, z, z, ALU.mult))
                seq.step(v.tensor_scalar(dts[:, :, :], z2, 1.0 / 19, None, ALU.mult))
                for n in range(17, 1, -2):
                    seq.step(v.scalar_tensor_tensor(dts[:, :, :], dts[:, :, :], 1.0 / n, z2, ALU.add, ALU.mult))
                seq.step(v.scalar_tensor_tensor(dts[:, :, :], dts[:, :, :], 1.0, z, ALU.add, ALU.mult))
                seq.step(v.tensor_scalar(z2, odd[:, :, 0:H], 0.0, None, ALU.max))
                seq.step(v.scalar_tensor_tensor(dts[:, :, :], dts[:, :, :], 2.0, z2, ALU.mult, ALU.add))
                v.scalar_tensor_tensor(adt[:, :, :], dts[:, :, :], -1.0,
                                       dtb[:, 1, :].unsqueeze(1).to_broadcast([P, TT, H]), ALU.mult, ALU.mult)\
                 .then_inc(s_adt, 1)
                v.tensor_scalar(wgt[:, :, :], wgt[:, :, :], 1.0, 0.25, ALU.add, ALU.mult)
                v.tensor_scalar(prm[:, 1, :], prm[:, 1, :], 0.5, None, ALU.mult)
                seq.step(v.tensor_scalar(prm[:, 2, 0:32], prm[:, 2, 0:32], 0.5, None, ALU.mult))

            def blocks(w):
                def f():
                    v.wait_ge(s_ktc, 1)
                    if w:
                        v.wait_ge(s_blk, w)
                    c = ckT[:, 2 * w:2 * w + 2, :].rearrange("p g (i q) -> p q g i", q=16)
                    for half in range(2):
                        pe_ = prm[:, 2, 48 + 32 * w + 16 * half:64 + 32 * w + 16 * half]
                        for g in range(2):
                            ins = v.tensor_tensor(blk[:, 16 * half:16 * half + 16, g * NC:g * NC + NC],
                                                  c[:, :, g, half:half + NC],
                                                  pe_.unsqueeze(2).to_broadcast([P, 16, NC]), ALU.add)
                    ins.then_inc(s_blk0, 1)
                return f

            def blocks_lo(w):
                def f():
                    v.wait_ge(s_bhi, w + 1)
                    v.tensor_tensor(bhl[:, w, :, 30:60], blk[:, :, :], bhl[:, w, :, 0:30].bitcast(F32),
                                    ALU.subtract).then_inc(s_blk, 1)
                return f

            def z_silu(b):
                def f():
                    v.wait_ge(s_ztanh, b + 1)
                    for t in range(TT):
                        ins = v.scalar_tensor_tensor(za[:, t, b * BW:b * BW + BW], za[:, t, b * BW:b * BW + BW], 1.0,
                                                     M[b % 2][:, t, :], ALU.add, ALU.mult)
                    ins.then_inc(main_free, 1)
                return f

            def hidden_copy():
                multiplied(v, R_ZW, 0, 3 * UPB - 1)
                for w in range(2):
                    ins = v.tensor_copy(hT[0:60, w, :], X[2 + w][0:60, 0:256])
                ins.then_inc(s_hc, 1)

            def gelu_arg():
                v.wait_ge(s_ht, 1)
                ga, gb_ = gel[:, :, 0:30], gel[:, :, 30:60]
                seq.step(v.tensor_copy(gb_, X[0][:, 0:256].rearrange("p (a b) -> p a b", a=4)[:, :, 0:30]))
                seq.step(v.tensor_tensor(gsq, gb_, gb_, ALU.mult))
                seq.step(v.tensor_scalar(gsq, gsq, 0.044715, 1.0, ALU.mult, ALU.add))
                v.tensor_tensor(ga, gsq, gb_, ALU.mult).then_inc(s_gl1, 1)

            def gelu_finish():
                ga, gb_ = gel[:, :, 0:30], gel[:, :, 30:60]
                v.wait_ge(s_gl2, 1)
                seq.step(v.scalar_tensor_tensor(gb_, ga, 1.0, gb_, ALU.add, ALU.mult))
                v.tensor_scalar(gb_, gb_, 0.5, None, ALU.mult).then_inc(s_gl3, 1)

            def cmp_keys():
                v.wait_ge(s_cmp, 1)
                v.tensor_copy(kcT[:, :, 0:NC], X[0][:, 0:30].rearrange("p (g k) -> p g k", g=2)).then_inc(s_cmpc, 1)

            z_silu(0)()
            for u in range(4):
                split(R_ODD, 0, u, 8 * ODD)
            main_block(R_Z1, 0, 0, {3: [odd_copy], 6: [dt_abs, blocks(0)], 9: [blocks_lo(0)], 10: [blocks(1)],
                                    12: [blocks_lo(1), dt_finish]})
            for n in range(2 * UPB):
                split(R_ZW, 0, n + n // 2)
                if n % 2:
                    split(R_ZW, 0, n + n // 2 + 1)
                if n % UPB == 4:
                    z_silu(1 + n // UPB)()
            v.wait_ge(s_dec, 2)

            def wide(x, n):
                return x.unsqueeze(2).to_broadcast([P, R, n])

            def ssd(g):
                def conv(cs):
                    def f():
                        v.wait_ge(s_T, g + 1)
                        tiles = {0: g * 2, 1: g * 2 + 1, 2: g + 16, 3: g + 24}
                        for k in range(3, -1, -1):
                            for c in cs:
                                x = X[c // 2][:, (c % 2) * S:(c % 2) * S + S]
                                w = prm[:, 1, bass.ds(tiles[c] + 32 * k, 1)]
                                if k == 3:
                                    ins = v.tensor_scalar(cv[:, c, :], x, w, prm[:, 2, bass.ds(tiles[c], 1)],
                                                          ALU.mult, ALU.add)
                                else:
                                    s = 3 - k
                                    ins = v.scalar_tensor_tensor(cv[:, c, s:S], x[:, 0:S - s], w, cv[:, c, s:S],
                                                                 ALU.mult, ALU.add)
                            if k or cs[0] == 0:
                                seq.step(ins)
                            else:
                                ins.then_inc(s_conv, 1)
                    return f

                def conv_silu():
                    v.wait_ge(s_cth, g + 1)
                    flat = cv[:, :, :].rearrange("p a b -> p (a b)")
                    v.scalar_tensor_tensor(flat, th[:, :, :].rearrange("p a b -> p (a b)"), 1.0, flat,
                                           ALU.add, ALU.mult).then_inc(s_cs, 1)
                    v.wait_ge(s_cs, g + 1)
                    for c in range(2):
                        ins = v.tensor_tensor(ua[:, c, :, :], wide(adt[:, c, bass.ds(g * R, R)], P),
                                              after.unsqueeze(1).to_broadcast([P, R, P]), ALU.mult)
                    ins.then_inc(s_ua, 1)

                def operands():
                    v.wait_ge(s_A, g + 1)
                    for t in range(TT):
                        x = X[0][:, t * S:t * S + S].rearrange("p (r n) -> p r n", r=R)
                        v.tensor_tensor(xdt[:, t, :].rearrange("p (r n) -> p r n", r=R), x,
                                        wide(dts[:, t, bass.ds(g * R, R)], HP), ALU.mult)
                        v.tensor_tensor(y0[:, t, :].rearrange("p (r n) -> p r n", r=R), x,
                                        wide(dtb[:, 2, bass.ds(g * R, R)], HP), ALU.mult)
                    v.wait_ge(s_bt, g + 1)
                    seq.step(v.tensor_tensor(cbm.rearrange("p (c l) -> p c l", c=2),
                                             X[1][:, P:3 * P].rearrange("p (c l) -> p c l", c=2),
                                             tri.unsqueeze(1).to_broadcast([P, 2, P]), ALU.mult))
                    v.tensor_tensor(xdd.rearrange("p (r n) -> p r n", r=R),
                                    xdt[:, 0, :].rearrange("p (r n) -> p r n", r=R),
                                    wide(dec[:, 1, bass.ds(g * R, R)], HP), ALU.mult)
                    v.wait_ge(s_dm, g + 1)
                    for c in range(2):
                        ins = v.tensor_tensor(mm[:, c, :, :], mm[:, c, :, :],
                                              cbm[:, c * P:c * P + P].unsqueeze(1).to_broadcast([P, R, P]), ALU.mult)
                    ins.then_inc(s_m, 1)

                return {5: [conv((0, 1))], 7: [conv((2, 3))], 9: [conv_silu], 12: [operands]}

            def ssd_tail(g):
                def y_gate():
                    v.wait_ge(s_C, g + 1)
                    yf = y0[:, :, :].rearrange("p a b -> p (a b)")
                    seq.step(v.tensor_tensor(yf, yf, X[0][:, :], ALU.add))
                    seq.step(v.tensor_tensor(yof.rearrange("p (r n) -> p r n", r=R),
                                             X[1][:, GW:2 * GW].rearrange("p (r n) -> p r n", r=R),
                                             wide(dec[:, 0, bass.ds(g * R, R)], HP), ALU.mult))
                    seq.step(v.tensor_tensor(y0[:, 1, :], y0[:, 1, :], yof, ALU.add))
                    v.tensor_tensor(y0[:, :, :], y0[:, :, :], za[:, :, bass.ds(g * GW, GW)], ALU.mult).then_inc(s_y, 1)
                return {1: [y_gate]}

            PER_SSD = 4 + 3 + 1 + 3
            main_block(R_G01, 0, 0, {3: [hidden_copy, z_silu(3)], 5: [gelu_arg], 7: [gelu_finish], 13: [cmp_keys]})
            main_block(R_G01, 0, UPB, ssd(0))
            seq.flat()
            with v.Fori(0, 3) as i:
                seq.enter(i, 2 * PER_SSD)
                for b in range(2):
                    main_block(R_G, i, UPB * b, both(ssd_tail(i * 2 + b), ssd(i * 2 + (1 + b))))
                seq.leave(2 * PER_SSD, 3)
            main_block(R_KQ, 0, 0, both(ssd_tail(6), ssd(7)))

            def rope(x, buf):
                def quad(n):
                    return buf[:, n, :].rearrange("p (t g r) -> p t g r", t=TT, g=2)
                h = ROT // 2
                cb = cosv[:, :, 0:h].unsqueeze(2).to_broadcast([P, TT, 2, h])
                sb_ = sinv[:, :, 0:h].unsqueeze(2).to_broadcast([P, TT, 2, h])
                x1, x2 = x[:, :, :, 0:h], x[:, :, :, h:ROT]
                v.tensor_tensor(quad(0), x1, cb, ALU.mult)
                v.tensor_tensor(quad(1), x2, sb_, ALU.mult)
                v.tensor_tensor(quad(2), x2, cb, ALU.mult)
                seq.step(v.tensor_tensor(quad(3), x1, sb_, ALU.mult))
                v.tensor_tensor(x1, quad(0), quad(1), ALU.subtract)
                return v.tensor_tensor(x2, quad(2), quad(3), ALU.add)

            def kv_rope(x):
                def f():
                    emptied(v, B_KV + x - 1)
                    if x == 2:
                        v.wait_ge(s_krot, 1)
                    rope(kst[:, :, 0:2 * DH].rearrange("p t (g d) -> p t g d", g=2), rp).then_inc(s_krot, 1)
                    v.tensor_copy(vv[:, (x - 1) * TT:x * TT, :, :].rearrange("p t g d -> p t (g d)"),
                                  kst[:, :, 2 * DH:BW]).then_inc(s_kvf, 1)
                return f

            main_block(R_KQ, 0, UPB, both(ssd_tail(7), {4: [kv_rope(1)]}))
            main_block(R_KQ, 0, 2 * UPB, {4: [kv_rope(2)]})
            seq.flat()

            def head(n, j, a_):
                def maxima():
                    v.wait_ge(s_sc, n + 1)
                    v.tensor_reduce(mx[:, 0, 1:3], X[1][:, 0:2 * P].rearrange("p (b k) -> p b k", b=2), AX.X, ALU.max)
                    v.tensor_reduce(mx[:, 1, 1:3], X[2][:, :].rearrange("p (b k) -> p b k", b=2), AX.X, ALU.max)
                    seq.step(v.tensor_reduce(mx[:, :, 0], X[1][:, 256:288].rearrange("p (t k) -> p t k", t=2)[:, :, 0:NC],
                                             AX.X, ALU.max))
                    v.tensor_scalar(mx[:, :, :], mx[:, :, :], NEG_CLAMP, -SCALE, ALU.max, ALU.mult).then_inc(s_mx, 1)

                def weights():
                    v.wait_ge(s_ex, n + 1)
                    seq.step(v.tensor_scalar(sm[:, :, :], sm[:, :, :], 1e-30, None, ALU.max))
                    seq.step(v.reciprocal(sm[:, :, :], sm[:, :, :]))
                    seq.step(v.tensor_tensor(sm[:, :, :], sm[:, :, :],
                                             wgt[:, :, bass.ds(j * 3 + 24 * a_, 3)], ALU.mult))
                    v.tensor_tensor(p0[:, :, :], p0[:, :, :], sm[:, 0, 1:3].unsqueeze(2).to_broadcast([P, 2, P]), ALU.mult)
                    v.tensor_tensor(p1[:, :, :], p1[:, :, :], sm[:, 1, 1:3].unsqueeze(2).to_broadcast([P, 2, S]), ALU.mult)
                    v.tensor_tensor(pc[:, :, 0:NC], pc[:, :, 0:NC],
                                    sm[:, :, 0].unsqueeze(2).to_broadcast([P, TT, NC]), ALU.mult).then_inc(s_pw, 1)

                def probs_c():
                    v.wait_ge(s_pt, n + 1)
                    v.tensor_copy(pt0, X[3][:, 0:2 * P])
                    v.tensor_copy(ptc[0:NC, :], X[3][0:NC, 2 * P:4 * P]).then_inc(s_ptv, 1)

                def gate_o():
                    v.wait_ge(s_o, n + 1)
                    v.tensor_tensor(og[:, :, :], X[1][:, 0:2 * P].rearrange("p (t d) -> p t d", t=TT),
                                    zt[:, :, a_ * DH:a_ * DH + DH], ALU.mult).then_inc(s_og, 1)

                return maxima, weights, probs_c, gate_o

            def two_heads(j, par):
                def q_prepare():
                    v.wait_ge(s_zth, j + 1)
                    for t in range(TT):
                        ins = v.scalar_tensor_tensor(zt[:, t, :], zt[:, t, :], 1.0, M[par][:, t, 2 * DH:BW],
                                                     ALU.add, ALU.mult)
                    ins.then_inc(main_free, 1)
                    seq.step(v.tensor_copy(qr[:, :, :], qs[:, :, :]))
                    rope(qr[:, :, :].rearrange("p t (g d) -> p t g d", g=2), rq).then_inc(s_qr, 1)

                m0, w0, c0, g0 = head(j * 2, j, 0)
                m1, w1_, c1, g1 = head(j * 2 + 1, j, 1)
                return by_block({4: [q_prepare], 9: [m0], 13: [w0], 15: [c0], 17: [g0], 22: [m1], 26: [w1_], 28: [c1],
                                 30: [g1]}, 3)

            PER_J = 2 * 4 + 2 + UPB
            with v.Fori(0, 3) as i:
                seq.enter(i, 2 * PER_J)
                for j2 in range(2):
                    steps = two_heads(i * 2 + j2, j2)
                    for n in range(3):
                        main_block(R_QG, i, UPB * (3 * j2 + n), steps[n])
                seq.leave(2 * PER_J, 3)
            steps = two_heads(6, 0)
            for n in range(3):
                main_block(R_Q6, 0, UPB * n, steps[n])
            steps = two_heads(7, 1)
            main_block(R_Q7, 0, 0, steps[0])
            main_block(R_Q7, 0, UPB, both(steps[1], {2 * c + 5: [low_a(8, c)] for c in range(6)}))

            def y_square():
                v.wait_ge(s_Dc, G + 1)
                seq.step(v.tensor_reduce(stat[:, 8:10], ssa[:, :, :], AX.X, ALU.add))
                v.tensor_scalar(stat[:, 8:10], stat[:, 8:10], 1.0 / (4 * INNER), EPS, ALU.mult, ALU.add)\
                 .then_inc(s_rms, 1)

            def y_rstd():
                v.wait_ge(s_rsq, 1)
                seq.step(v.reciprocal(stat[:, 10:12], stat[:, 8:10]))
                seq.step(v.tensor_scalar(stat[:, 10:12], stat[:, 10:12], 0.5, None, ALU.mult))

            def gate_bias():
                v.wait_ge(s_colc, 2 + ADA_FRONT + 8)
                v.tensor_tensor(mod[:, 2 * KT:3 * KT], mod[:, 2 * KT:3 * KT], b_ada[:, 2 * KT:3 * KT], ALU.add)\
                 .then_inc(s_gmod, 1)

            def merge(j, reg, i):
                def gates():
                    v.wait_ge(s_gl[0], j * 16 + 16)
                    v.wait_ge(s_gl[1], j * 16 + 16)
                    for t in range(TT):
                        v.tensor_scalar(gx[:, t, :], gx[:, t, :], 1.0, stat[:, 10 + t:11 + t], ALU.add, ALU.mult)
                    seq.step(v.tensor_scalar(gx[:, TT:2 * TT, :], gx[:, TT:2 * TT, :], 1.0, None, ALU.add))

                def part_a():
                    multiplied(v, reg, i, UPB // 2 - 1)
                    v.wait_ge(s_mT, j + 1)
                    v.tensor_tensor(mg[:, :, :], gx[:, 0:TT, :], M[0][:, :, :], ALU.mult).then_inc(main_free, 1)

                return {9: [gates], 12: [part_a]}

            def merge_tail(j, reg, i):
                def part_b():
                    multiplied(v, reg, i, -1)
                    v.tensor_tensor(mb[:, :, :], gx[:, TT:2 * TT, :], M[1][:, :, :], ALU.mult).then_inc(main_free, 1)
                    emptied(v, j * 2 + (B_PR + 1))
                    v.tensor_tensor(mg[:, :, :], mb[:, :, :], mg[:, :, :], ALU.add).then_inc(s_mgd, 1)
                return {3: [part_b]}

            main_block(R_PR0, 0, 0, both({1: [low_a(8, 6)]}, both(
                {2: [gate_bias], 4: [y_square], 5: [low_a(8, 7)], 6: [y_rstd]}, merge(0, R_PR0, 0))))
            seq.flat()
            with v.Fori(0, 6) as i:
                seq.enter(i, 1)
                main_block(R_PR, i, 0, both(merge_tail(i, R_PR, i), merge(i + 1, R_PR, i)))
                seq.leave(1, 6)
            main_block(R_PR7, 0, 0, both(merge_tail(6, R_PR7, 0), both(
                merge(7, R_PR7, 0), {2 * c + 5: [low_a(16, c)] for c in range(6)})))
            seq.flat()

            def out_block(n, reg, i, k, par):
                def f():
                    multiplied(v, reg, i, k - 1)
                    v.wait_ge(s_xr[par], (n - par) * 8 + 16)
                    v.wait_ge(s_gb, 32)
                    v.wait_ge(s_xo, n + 2)
                    cols = bass.ds(n * BW, BW)
                    for t in range(TT):
                        ins = v.scalar_tensor_tensor(mg[:, t, :], M[par][:, t, :], 0.5, gateb[:, cols],
                                                     ALU.mult, ALU.mult)
                    ins.then_inc(main_free, 1)
                    emptied(v, n + B_OUT)
                    v.tensor_tensor(xo[:, :, cols], mg[:, :, :], xr[:, TT * par:TT * par + TT, :], ALU.add)\
                     .then_inc(s_xo, 1)
                return f

            main_block(R_OUT0, 0, 0, both(merge_tail(7, R_OUT0, 0), {1: [low_a(16, 6)], 9: [low_a(16, 7)]}))
            v.wait_ge(s_mT, 9)
            with v.Fori(0, 3) as i:
                for b in range(2):
                    main_block(R_OUT, i, UPB * b, {2: [out_block(i * 2 + b, R_OUT, i, UPB * b, b)]})
            main_block(R_OUT7, 0, 0, {2: [out_block(6, R_OUT7, 0, 0, 0)]})
            out_block(7, R_OUT7, 0, UPB, 1)()
            v.wait_ge(s_osq, 9)
            seq.step(v.tensor_reduce(stat[:, 16:18], ssf[:, :, :], AX.X, ALU.add))
            v.tensor_scalar(stat[:, 16:18], stat[:, 16:18], 1.0 / D, EPS, ALU.mult, ALU.add).then_inc(s_fms, 1)
            v.wait_ge(s_fsq, 1)
            seq.step(v.reciprocal(stat[:, 18:20], stat[:, 16:18]))
            v.wait_ge(s_fn, 16)
            fn = raw[:, :, :].rearrange("p a b -> p (a b)")
            for q in range(4):
                for t in range(TT):
                    c = slice(q * 1024, q * 1024 + 1024)
                    v.scalar_tensor_tensor(xo[:, t, c], xo[:, t, c], stat[:, 18 + t:19 + t], fn[:, c],
                                           ALU.mult, ALU.mult).then_inc(s_fin, 1)

        @block.gpsimd
        def _(pool):
            pool.sem_inc(s_gfree[0], 1)
            pool.sem_inc(s_gfree[1], 1)
            pool.memset(stat[:, 20:22], -0.5).then_inc(s_ph, 1)
            pool.wait_ge(s_xms, 2)
            pool.tensor_scalar(stat[:, 2:4], stat[:, 0:2], 1.0 / D, EPS, ALU.mult, ALU.add).then_inc(s_ph, 1)
            pool.wait_ge(s_ph, 2)
            pool.tensor_tensor(stat[:, 4:6], stat[:, 2:4], stat[:, 20:22], ALU.pow).then_inc(s_xrs, 1)
            pool.wait_ge(s_xT, 16)
            for w, name in enumerate(("cmp_k_w2", "cmp_v_w2")):
                pool.dma_start(w2[:, 2 * w:2 * w + 2, :], a[name][0].rearrange("(h p) n -> p h n", p=P))\
                    .then_inc(s_w2, 16)

            def spill(j, m, col):
                emptied(pool, j * 3 + (B_QG + 1 + m))
                pool.dma_start(gsc[:, m, :, bass.ds(col, BW)], gst[:, 2 * m:2 * m + 2, :]).then_inc(s_gsp[m], 16)
                pool.wait_ge(s_gsp[m], j * 16 + 16)
                pool.sem_inc(s_gfree[m], 1)

            with pool.Fori(0, 8) as i:
                col = pool.snap(i * BW)
                for m in range(2):
                    spill(i, m, col)
            pool.wait_ge(s_oTc, NH + 1)
            for m in range(2):
                pool.dma_start(gx[:, TT * m:TT * m + TT, :], gsc[:, m, :, 0:BW]).then_inc(s_gl[m], 16)
            pool.wait_ge(s_gc, 1)
            pool.dma_start(a["gated"].rearrange("(t p) -> t p", p=P), gout[:, :]).then_inc(s_gd, 16)
            pool.wait_ge(s_gd, 16)
            for h in range(2):
                pool.dma_start(gateb[:, h * D // 2:(h + 1) * D // 2],
                               a["gated"][h * D // 2:(h + 1) * D // 2].partition_broadcast(P)).then_inc(s_gb, 16)
            with pool.Fori(0, 7) as i:
                col = pool.snap(i * BW + BW)
                emptied(pool, i * 2 + (B_PR + 1))
                for m in range(2):
                    pool.dma_start(gx[:, TT * m:TT * m + TT, :], gsc[:, m, :, bass.ds(col, BW)]).then_inc(s_gl[m], 16)
            pool.wait_ge(s_mgd, 8)
            with pool.Fori(0, 4) as i:
                for b in range(2):
                    col = pool.snap(i * (2 * BW) + b * BW)
                    pool.wait_ge(s_xo, i * 2 + (b + 1))
                    pool.dma_start(xr[:, TT * b:TT * b + TT, :], xd[:, :, bass.ds(col, BW)]).then_inc(s_xr[b], 16)


def kernel(x, c, w_ada, b_ada, norm_w, w_in, conv_w, conv_b, dt_bias, a_log, d_skip, ssm_norm_w, cmp_pe_k,
           cmp_pe_v, cmp_k_w1, cmp_k_w2, cmp_v_w1, cmp_v_w2, w_proj_a, w_proj_b, w_out, final_norm_w):
    import numpy as np
    import concourse.bacc as bacc
    from concourse.bass_utils import run_bass_kernel_spmd

    row, col = np.arange(P)[:, None], np.arange(P)[None, :]
    consts = np.zeros((P, K_N), np.float32)
    consts[:, K_ID:K_ID + P] = row == col
    consts[:, K_TRI:K_TRI + P] = row <= col
    consts[:, K_AFT:K_AFT + P] = row > col
    consts[:, K_NEG:K_NEG + P] = np.where(col > row, NEG, 0.0)
    pos = np.arange(S)
    cmp_end = np.arange(16) * 16 + 31
    mask = np.where(cmp_end[None, :] <= pos[:, None], 0.0, NEG)
    inv = np.float32(500000.0) ** (-np.arange(0, ROT, 2, dtype=np.float32) / np.float32(ROT))
    ang = pos.astype(np.float32)[:, None] * inv[None, :]
    for t in range(TT):
        tok = slice(t * P, t * P + P)
        consts[:, K_CM + 16 * t:K_CM + 16 * t + 16] = mask[tok]
        consts[:, K_COS + 16 * t:K_COS + 16 * t + 16] = np.cos(ang[tok])
        consts[:, K_SIN + 16 * t:K_SIN + 16 * t + 16] = np.sin(ang[tok])
    consts[:, K_ONE] = 1.0

    given = dict(x=x, c=c, w_ada=w_ada, b_ada=b_ada, norm_w=norm_w, w_in=w_in, conv_w=conv_w, conv_b=conv_b,
                 dt_bias=dt_bias, a_log=a_log, d_skip=d_skip, ssm_norm_w=ssm_norm_w, cmp_pe_k=cmp_pe_k,
                 cmp_pe_v=cmp_pe_v, cmp_k_w1=cmp_k_w1, cmp_k_w2=cmp_k_w2, cmp_v_w1=cmp_v_w1, cmp_v_w2=cmp_v_w2,
                 w_proj_a=w_proj_a, w_proj_b=w_proj_b, w_out=w_out, final_norm_w=final_norm_w, consts=consts)
    nc = bacc.Bacc("TRN2", target_bir_lowering=False, num_devices=1)
    arrays, aps = {}, {}
    for name, value in given.items():
        value = np.ascontiguousarray(value)
        arrays["in_" + name] = value
        aps[name] = nc.dram_tensor("in_" + name, value.shape, F32, kind="ExternalInput").ap()
    aps["out"] = nc.dram_tensor("out", (1, S, D), F32, kind="ExternalOutput").ap()
    aps["gscr"] = nc.dram_tensor("merge_gates", (2, S, D), F32, kind="Internal").ap()
    aps["gated"] = nc.dram_tensor("gate_row", (D,), F32, kind="Internal").ap()
    build(nc, aps)
    r = run_bass_kernel_spmd(nc, [arrays], core_ids=[0])
    return r.results[0]["out"]
```
